# Optimizing a Trainium2 kernel written in Bass

```python
import math
import jax, jax.numpy as jnp
from jax import lax
import numpy as np

D_MODEL = 1024
BATCH = 1
SEQ = 1024
DEPTH = 1
DEC_BATCH = 8
DEC_SEQ = 8
PAST_LEN = 8192
PAGE_SIZE = 128

W_LRU = D_MODEL
LRU_BLOCKS = 8
LRU_BW = W_LRU // LRU_BLOCKS
CONV_W = 4
RG_C = 8.0
GLA_HEADS = 4
GLA_DK = (D_MODEL // 2) // GLA_HEADS
GLA_DV = D_MODEL // GLA_HEADS
GATE_RANK = 16
GATE_NORM = 16.0
CHUNK = 64
IN_SIZES = [W_LRU, W_LRU, GLA_HEADS * GLA_DK, GLA_HEADS * GLA_DK,
            GLA_HEADS * GLA_DV, GLA_HEADS * GLA_DV, GATE_RANK, 2 * D_MODEL]
N_IN = sum(IN_SIZES)
IN_SPLITS = [int(s) for s in np.cumsum(IN_SIZES)[:-1]]
EPS = 1e-6

kernel_name = "hawk_gla_parallel_gated_step"

def rms_norm(x, g):
    xf = x.astype(jnp.float32)
    y = xf * lax.rsqrt(jnp.mean(xf * xf, axis=-1, keepdims=True) + EPS)
    return (y * g.astype(jnp.float32)).astype(x.dtype)

def causal_conv(x, buf, w, b):
    T = x.shape[1]
    xp = jnp.concatenate([buf.astype(x.dtype), x], axis=1)
    y = b + xp[:, 0:T] * w[0]
    for k in range(1, CONV_W):
        y = y + xp[:, k:k + T] * w[k]
    return y, xp[:, -(CONV_W - 1):]

def rg_lru(x, h0, w_r, b_r, w_i, b_i, lam):
    B, T, W = x.shape
    xf = x.astype(jnp.float32)
    xb = xf.reshape(B, T, LRU_BLOCKS, LRU_BW)
    r = jax.nn.sigmoid(jnp.einsum('btnc,ncd->btnd', xb, w_r.astype(jnp.float32))
                       + b_r.astype(jnp.float32).reshape(LRU_BLOCKS, LRU_BW)).reshape(B, T, W)
    i = jax.nn.sigmoid(jnp.einsum('btnc,ncd->btnd', xb, w_i.astype(jnp.float32))
                       + b_i.astype(jnp.float32).reshape(LRU_BLOCKS, LRU_BW)).reshape(B, T, W)
    log_a = -RG_C * r * jax.nn.softplus(-lam.astype(jnp.float32))
    a = jnp.exp(log_a)
    u = jnp.sqrt(-jnp.expm1(2.0 * log_a)) * (i * xf)
    u = u.at[:, 0].add(a[:, 0] * h0.astype(jnp.float32))

    def comb(left, right):
        al, bl = left
        ar, br = right
        return al * ar, ar * bl + br

    _, h = lax.associative_scan(comb, (a, u), axis=1)
    return h, h[:, -1]

def gla_chunked(q, k, v, g, S0):
    B, T, H, _ = q.shape
    C = CHUNK if T >= CHUNK else T
    pad = (-T) % C
    if pad:
        padf = lambda z: jnp.pad(z, ((0, 0), (0, pad), (0, 0), (0, 0)))
        q, k, v, g = padf(q), padf(k), padf(v), padf(g)
    n = (T + pad) // C
    to_chunks = lambda z: z.reshape(B, n, C, H, z.shape[-1]).transpose(1, 0, 3, 2, 4)
    causal = jnp.tril(jnp.ones((C, C), dtype=bool))

    def step(S, inp):
        qc, kc, vc, gc = inp
        b = jnp.cumsum(gc, axis=2)
        diff = b[:, :, :, None, :] - b[:, :, None, :, :]
        decay = jnp.exp(jnp.where(causal[:, :, None], diff, -jnp.inf))
        att = jnp.einsum('bhtd,bhsd,bhtsd->bhts', qc, kc, decay)
        o = (jnp.einsum('bhts,bhsv->bhtv', att, vc)
             + jnp.einsum('bhtd,bhdv->bhtv', qc * jnp.exp(b), S))
        b_last = b[:, :, -1:, :]
        S_new = (jnp.exp(b_last[:, :, 0, :])[..., None] * S
                 + jnp.einsum('bhsd,bhsv->bhdv', kc * jnp.exp(b_last - b), vc))
        return S_new, o

    S_fin, o = lax.scan(step, S0.astype(jnp.float32),
                        (to_chunks(q), to_chunks(k), to_chunks(v), to_chunks(g)))
    o = o.transpose(1, 0, 3, 2, 4).reshape(B, n * C, H, v.shape[-1])[:, :T]
    return o, S_fin

def mixer_layer(x, h0, conv0, S0, norm_g, w_in, conv_w, conv_b, w_r, b_r, w_i, b_i, lam,
                w_a2, b_a, gla_norm_g, w_lru_o, w_gla_o, b_merge, w_out):
    B, T, _ = x.shape
    dt = x.dtype
    xn = rms_norm(x, norm_g)
    proj = jnp.einsum('btd,dn->btn', xn, w_in)
    x_lru, z_lru, q, k, v, z_gla, a_lo, gate_logits = jnp.split(proj, IN_SPLITS, axis=-1)

    xc, conv_new = causal_conv(x_lru, conv0, conv_w, conv_b)
    h, h_last = rg_lru(xc, h0, w_r, b_r, w_i, b_i, lam)
    y_a = jnp.einsum('btw,wd->btd', h.astype(dt) * jax.nn.silu(z_lru), w_lru_o)

    qf = q.astype(jnp.float32).reshape(B, T, GLA_HEADS, GLA_DK) * (GLA_DK ** -0.5)
    kf = k.astype(jnp.float32).reshape(B, T, GLA_HEADS, GLA_DK)
    vf = v.astype(jnp.float32).reshape(B, T, GLA_HEADS, GLA_DV)
    g = jax.nn.log_sigmoid((jnp.einsum('btr,rk->btk', a_lo, w_a2) + b_a).astype(jnp.float32)) / GATE_NORM
    g = g.reshape(B, T, GLA_HEADS, GLA_DK)
    o, S_new = gla_chunked(qf, kf, vf, g, S0)
    o = o * lax.rsqrt(jnp.mean(o * o, axis=-1, keepdims=True) + EPS)
    o = (o * gla_norm_g.astype(jnp.float32).reshape(GLA_HEADS, GLA_DV)).reshape(B, T, GLA_HEADS * GLA_DV)
    y_b = jnp.einsum('btv,vd->btd', o.astype(dt) * jax.nn.silu(z_gla), w_gla_o)

    gates = jax.nn.sigmoid(gate_logits + b_merge)
    g_a, g_b = jnp.split(gates, 2, axis=-1)
    merged = g_a * y_a + g_b * y_b
    out = x + jnp.einsum('btd,de->bte', merged, w_out)
    return out, h_last, conv_new, S_new

def setup_inputs(seed: int = 0) -> dict:
    key = jax.random.key(seed)
    ks = jax.random.split(key, 24)
    nrm = lambda k_, shape, s: jax.random.normal(k_, shape, jnp.float32) * s
    u = jax.random.uniform(ks[9], (DEPTH, W_LRU), jnp.float32, 0.9, 0.999)
    s = u ** (1.0 / RG_C)
    lam = jnp.log(s) - jnp.log1p(-s)
    return {
        "x_prompt": nrm(ks[0], (BATCH, SEQ, D_MODEL), 1.0),
        "x_sample": nrm(ks[1], (DEC_BATCH, DEC_SEQ, D_MODEL), 1.0),
        "state_lru_h": nrm(ks[2], (DEPTH, DEC_BATCH, W_LRU), 0.5),
        "state_lru_conv": nrm(ks[3], (DEPTH, DEC_BATCH, CONV_W - 1, W_LRU), 1.0),
        "state_gla": nrm(ks[4], (DEPTH, DEC_BATCH, GLA_HEADS, GLA_DK, GLA_DV), 0.5),
        "norm_g": 1.0 + nrm(ks[5], (DEPTH, D_MODEL), 0.01),
        "w_in": nrm(ks[6], (DEPTH, D_MODEL, N_IN), D_MODEL ** -0.5),
        "conv_w": nrm(ks[7], (DEPTH, CONV_W, W_LRU), CONV_W ** -0.5),
        "conv_b": nrm(ks[8], (DEPTH, W_LRU), 0.01),
        "w_r": nrm(ks[10], (DEPTH, LRU_BLOCKS, LRU_BW, LRU_BW), LRU_BW ** -0.5),
        "b_r": nrm(ks[11], (DEPTH, W_LRU), 0.01),
        "w_i": nrm(ks[12], (DEPTH, LRU_BLOCKS, LRU_BW, LRU_BW), LRU_BW ** -0.5),
        "b_i": nrm(ks[13], (DEPTH, W_LRU), 0.01),
        "lam": lam,
        "w_a2": nrm(ks[14], (DEPTH, GATE_RANK, GLA_HEADS * GLA_DK), GATE_RANK ** -0.5),
        "b_a": nrm(ks[15], (DEPTH, GLA_HEADS * GLA_DK), 0.01),
        "gla_norm_g": 1.0 + nrm(ks[16], (DEPTH, GLA_HEADS * GLA_DV), 0.01),
        "w_lru_o": nrm(ks[17], (DEPTH, W_LRU, D_MODEL), W_LRU ** -0.5),
        "w_gla_o": nrm(ks[18], (DEPTH, GLA_HEADS * GLA_DV, D_MODEL), (GLA_HEADS * GLA_DV) ** -0.5),
        "b_merge": nrm(ks[19], (DEPTH, 2 * D_MODEL), 0.01),
        "w_out": nrm(ks[20], (DEPTH, D_MODEL, D_MODEL), D_MODEL ** -0.5),
        "final_norm_g": 1.0 + nrm(ks[21], (D_MODEL,), 0.01),
    }

def reference(x_prompt, x_sample, state_lru_h, state_lru_conv, state_gla, norm_g, w_in, conv_w, conv_b,
              w_r, b_r, w_i, b_i, lam, w_a2, b_a, gla_norm_g, w_lru_o, w_gla_o, b_merge, w_out, final_norm_g):
    Bp = x_prompt.shape[0]
    hp, cp, sp, hs, cs, ss = [], [], [], [], [], []
    xp, xs = x_prompt, x_sample
    for l in range(DEPTH):
        w = (norm_g[l], w_in[l], conv_w[l], conv_b[l], w_r[l], b_r[l], w_i[l], b_i[l], lam[l],
             w_a2[l], b_a[l], gla_norm_g[l], w_lru_o[l], w_gla_o[l], b_merge[l], w_out[l])
        h0 = jnp.zeros((Bp, W_LRU), jnp.float32)
        c0 = jnp.zeros((Bp, CONV_W - 1, W_LRU), xp.dtype)
        S0 = jnp.zeros((Bp, GLA_HEADS, GLA_DK, GLA_DV), jnp.float32)
        xp, h_p, c_p, s_p = mixer_layer(xp, h0, c0, S0, *w)
        xs, h_s, c_s, s_s = mixer_layer(xs, state_lru_h[l], state_lru_conv[l], state_gla[l], *w)
        hp.append(h_p); cp.append(c_p); sp.append(s_p)
        hs.append(h_s); cs.append(c_s); ss.append(s_s)
    y_prompt = rms_norm(xp, final_norm_g)
    y_sample = rms_norm(xs, final_norm_g)
    return (y_prompt, y_sample, jnp.stack(hp), jnp.stack(cp), jnp.stack(sp),
            jnp.stack(hs), jnp.stack(cs), jnp.stack(ss))


_drawn_inputs = setup_inputs


def setup_inputs(seed=0):
    import zlib

    import numpy as np

    out = dict(_drawn_inputs(seed))
    spreads = {}
    factors = {'norm_g': 3.746,
     'b_r': 38.698,
     'b_i': 26.418,
     'b_a': 24.294,
     'gla_norm_g': 46.607,
     'b_merge': 28.717,
     'final_norm_g': 30.141,
     'conv_b': 3.263}
    for name, (base, spread) in spreads.items():
        noise = np.random.default_rng([zlib.crc32(name.encode()), seed]).standard_normal(out[name].shape)
        drawn = base * np.exp(spread * noise) if base else spread * noise
        out[name] = __import__('jax').numpy.asarray(drawn.astype(out[name].dtype))
    for name, factor in factors.items():
        out[name] = (out[name] * factor).astype(out[name].dtype)
    return out
```

```python
import concourse.bass as bass
from concourse import mybir
from contextlib import ExitStack

F32 = mybir.dt.float32
F32R = mybir.dt.float32r
BF16 = mybir.dt.bfloat16
U32 = mybir.dt.uint32
ALU = mybir.AluOpType
ACT = mybir.ActivationFunctionType

P = 128
D = 1024
KT = D // P
SEQ = 1024
NSEQ, SLEN = 8, 8
STOK = NSEQ * SLEN
NTOK = SEQ + STOK
PIECE = 364
PIECES = 3
TOK = PIECE * PIECES
CONV = 4
HIST = CONV - 1
HEADS = 4
DK = 128
DV = 256
VH = DV // P
RANK = 16
CHUNK = 128
NCHUNK = SEQ // CHUNK
TTILES = NCHUNK + 1
LEVELS = (64, 32, 16, 8, 4, 2, 1)
SLEVELS = (4, 2, 1)
GATE_NORM = 16.0
EPS = 1e-6
RG_C = 8.0
COL_X, COL_Z, COL_Q, COL_K, COL_V, COL_ZG = 0, D, 2 * D, 2 * D + 512, 3 * D, 4 * D
COL_A = 5 * D
COL_GA = COL_A + RANK
COL_GB = COL_GA + D
N_IN = COL_GB + D
R_CONVW, R_CONVB, R_BR, R_BI, R_LAM, R_GN, R_BM, R_BA = 0, 4, 5, 6, 7, 8, 9, 11
R_H0, R_CS = 12, 20
NROW = R_CS + NSEQ * HIST
V_BR, V_BI, V_BMA, V_BMB, V_C, V_NC = range(6)
N_LRU, N_MIXA, N_GLA = 0, 2 * KT, 4 * KT
N_GB = N_GLA + 6 * HEADS
N_YB = N_GB + 8
NTAIL = 1 + NSEQ + HIST + NSEQ * HIST
T_H, T_C = 0, 1 + NSEQ
XS = HIST + SEQ
XW = XS + NSEQ * (HIST + SLEN)


def head_steps():
    steps = [("g0", "act"), ("g1", "act"), ("g2", "act"), ("dg0", "dve"), ("dg1", "dve")]
    steps += [("L0", "dve"), ("L1", "dve"), ("L2", "dve"), ("vt0a", "act"), ("vt0b", "act"), ("vt0c", "act")]
    steps += [("L3", "dve"), ("L4", "dve"), ("L5", "dve"), ("L6", "dve")]
    steps += [("vt1a", "act"), ("vt1b", "act"), ("vt1c", "act"), ("smp", "dve")]
    steps += [("kTa", "act"), ("kTb", "act"), ("kTc", "act")]
    steps += [(f"KV{n}", "dve") for n in range(NCHUNK // 2)]
    steps += [(f"O{g}{d}", "act") for g in range(2) for d in range(VH)] + [("Os", "act")]
    steps += [(f"sKV{n}", "dve") for n in range(NSEQ // 2)]
    steps += [(f"nrm{j}", "act") for j in range(PIECES)]
    return steps


def build(nc, t, out):
    ctx = ExitStack()
    with ctx:
        base = -(-nc.sbuf_base // 32) * 32

        def at(name, shape, dt, offset):
            return nc.alloc_sbuf_tensor_at(name, shape, dt, offset=base + offset)

        TILE = TOK * 4
        SLOT = -(-TILE // 32) * 32
        o_xn = 0
        o_raw = o_xn + 2 * KT * TILE
        o_hi = o_raw + 2 * KT * P * 4
        o_lo = o_hi + 2 * KT * P * 4
        o_keep = o_lo + 2 * KT * P * 4
        o_const = o_keep + KT * TILE
        xn = at("xn", [P, 2, KT, TOK], F32R, o_xn)
        raw = at("raw", [P, 2, KT, P], F32, o_raw)
        whi = at("whi", [P, 2, KT, P], F32R, o_hi)
        wlo = at("wlo", [P, 2, KT, P], F32R, o_lo)
        keep = at("keep", [P, KT, TOK], F32, o_keep)
        a = [o_const]

        def take(name, shape, dt, size):
            h = at(name, shape, dt, a[0])
            a[0] += -(-size // 32) * 32
            return h

        ident = take("ident", [P, P], F32, P * 4)
        vec = take("vec", [P, KT, NROW], F32, KT * NROW * 4)
        dvec = take("dvec", [P, KT, 6], F32, KT * 6 * 4)
        tiny = take("tiny", [P, 5, KT], F32, 5 * KT * 4)
        ssum = take("ssum", [P, 32], F32, 128)
        rstd = take("rstd", [P, 32], F32, 128)
        o_glaconst = a[0]
        ones = take("ones", [P, P], F32, P * 4)
        notfirst = take("notfirst", [P, TOK], BF16, TOK * 2)
        lmask = take("lmask", [P, len(LEVELS), 64], F32, len(LEVELS) * 64 * 4)
        smask = take("smask", [STOK, NSEQ], F32, NSEQ * 4)
        wa2 = take("wa2", [2 * RANK, P], F32, P * 4)
        o_alo = a[0]
        alo = take("alo", [2 * RANK, TOK], F32, TILE)
        tails = at("tails", [P, KT, NTAIL], F32, o_alo)
        o_work = a[0]

        w = [o_work]

        def work(name, shape, dt, size):
            h = at(name, shape, dt, w[0])
            w[0] += -(-size // 32) * 32
            return h

        xbuf = work("xbuf", [P, XW], F32, XW * 4)
        xc = work("xc", [P, TOK], F32, TILE)
        xcs = work("xcs", [P, 2, TOK], F32R, 2 * TILE)
        tr = work("tr", [P, TOK], F32, TILE)
        ti = work("ti", [P, TOK], F32, TILE)
        dec = work("dec", [P, TOK], F32, TILE)
        wt = work("wt", [P, TOK], F32, TILE)
        tz = work("tz", [P, TOK], F32, TILE)
        sz = work("sz", [P, TOK], F32, TILE)
        hh = work("hh", [P, TOK], F32, TILE)
        fix = work("fix", [P, NSEQ], F32, NSEQ * 4)
        graw = work("graw", [P, 2, P], F32, 2 * P * 4)
        ghi = work("ghi", [P, 2, P], F32R, 2 * P * 4)
        glo = work("glo", [P, 2, P], F32R, 2 * P * 4)
        rows = at("rows", [NROW, D], F32, o_work + 60000)
        xt = at("xt", [P, 4, D], F32, o_work)
        ngb = at("ngb", [P, D], F32, o_work + 4 * D * 4)
        junk0 = at("junk0", [P, D], F32, o_work + 5 * D * 4)
        act_s = at("act_s", [P, 2, KT, TOK], F32R, o_work)
        ta = at("ta", [P, TOK], F32, o_keep)
        ma = at("ma", [P, TOK], F32, o_keep + SLOT)
        trow = at("trow", [NTAIL, D], F32, o_keep + 2 * SLOT)
        araw = at("araw", [P, KT, RANK], F32, o_keep + 3 * SLOT)
        aw = at("aw", [P, KT, P], F32R, o_keep + 4 * SLOT)
        w[0] = o_work
        qb = work("qb", [P, TOK], F32, TILE)
        kb = work("kb", [P, TOK], F32, TILE)
        gb = work("gb", [P, TOK], F32, TILE)
        dd = work("dd", [P, TOK], F32, TILE)
        qk = work("qk", [P, 2, TOK], F32, 2 * TILE)
        qks = work("qks", [P, len(SLEVELS), STOK], F32, len(SLEVELS) * STOK * 4)
        vT = work("vT", [P, TOK], F32, TILE)
        vv = work("vv", [P, TTILES, DV], F32, TTILES * DV * 4)
        att = work("att", [P, TTILES, P], F32, TTILES * P * 4)
        kt = work("kt", [P, TOK], F32, TILE)
        kT = work("kT", [P, TTILES, P], F32, TTILES * P * 4)
        st = work("st", [P, NCHUNK, DV], F32, NCHUNK * DV * 4)
        st0 = work("st0", [P, NSEQ, DV], F32, NSEQ * DV * 4)
        dlast = work("dlast", [P, NCHUNK + NSEQ], F32, 64)
        assert w[0] <= nc.sbuf_usable_end - base and o_work + 2 * KT * TILE <= nc.sbuf_usable_end - base
        assert NTAIL * KT * 4 <= TILE
        oo = [gb, kb]
        ring = [dd, kt]
        wos = at("wos", [P, 2, KT, D], F32R, o_xn)
        woraw = at("woraw", [P, D], F32, o_xn + 2 * KT * D * 4)
        mal = at("mal", [P, 2, NTOK], F32, o_glaconst)
        assert o_glaconst + 2 * NTOK * 4 <= o_work
        w[0] = o_work
        ms = work("ms", [P, 2, 2, KT, P], F32R, 4 * KT * P * 4)
        xr = work("xr", [P, 2, D], F32, 2 * D * 4)
        yy = work("yy", [P, 2, D], F32, 2 * D * 4)
        fng = work("fng", [P, D], F32, D * 4)
        junk1 = work("junk1", [P, D], F32, D * 4)

        ps = ctx.enter_context(nc.psum_tensor("ps", [P, 8, 512], F32))
        bankA, bankB = 0, 3

        def slot3(b):
            return ps[:, b:b + PIECES, 0:PIECE]

        def p3(ap):
            return ap.rearrange("p (a b) -> p a b", a=PIECES)

        scratch = nc.dram_tensor("branch_a", (KT, P, TOK), F32, kind="Internal").ap()

        def sem(name):
            return ctx.enter_context(nc.semaphore(name))

        s = {n: sem(n) for n in (
            "rows_in", "ng_in", "ident_ok", "rows_T", "vec_ok", "dvec_ok", "tiny_ok", "masks_ok", "pool_step",
            "x_sq", "x_rms", "x_rstd", "x_scaled", "x_T", "x_hi", "x_lo", "pad_ok",
            "hi_ok", "lo_ok", "job_done",
            "g_in", "g_hi", "g_lo", "x_evac", "hist_ok", "conv_step", "x_tail", "xc_hi", "xc_lo", "z_tanh", "z_silu",
            "r_done", "i_done", "r_tanh", "i_tanh", "a_ok", "t_ok", "i_x", "a_sq", "w_ok", "m_ok", "u_ok",
            "fix_step", "h_ok", "hz_ok", "h_tail", "tails_T", "tails_ok", "tails_out",
            "act_hi", "act_lo", "dve_passed", "pe_passed", "sp_passed", "act_passed", "ga_tanh", "ma_ok", "ma_out",
            "alo_in", "alo_zero", "alo_hi", "alo_lo", "alo_mm", "alo_ok", "wa2_in", "att_zero", "c_full", "c_act", "c_dve",
            "g_abs", "g_exp", "g_ln", "g_ok", "b_ok", "q_ok", "k_ok", "lev_d", "lev_e", "lev_qk", "vT_ok",
            "kt_d", "kt_e", "kt_ok", "qb_e", "qb_ok", "dlast_ok", "st_ok", "ktm_ok", "att_step", "st0_in", "st_out", "st0_out",
            "o_sq", "n_ln", "n_rstd", "zg_tanh", "zg_silu", "o_norm", "og_ok",
            "gb_tanh0", "gb_tanh1", "wo_in", "wo_hi", "wo_lo", "mal_in0", "mal_in1", "yb_part", "merged0", "merged1",
            "fng_in", "m_hi", "m_lo", "y_mm", "y_res", "y_sq", "y_rms", "y_rstd", "y_ok", "y_out0", "y_out1",
        )}
        s_x = [sem(f"x_in{n}") for n in range(4)]
        s_raw = [sem(f"raw_in{n}") for n in range(2)]
        s_xr = [sem(f"xr_in{n}") for n in range(2)]
        gb_tanh = [s["gb_tanh0"], s["gb_tanh1"]]
        mal_in = [s["mal_in0"], s["mal_in1"]]
        merged = [s["merged0"], s["merged1"]]
        y_out = [s["y_out0"], s["y_out1"]]

        STEPS = head_steps()
        NSTEP = len(STEPS)
        INDEX = {name: n for n, (name, _) in enumerate(STEPS)}
        assert NSTEP % 2 == 0
        PER = {e: sum(x == e for _, x in STEPS) for e in ("act", "dve")}

        def bank(name):
            return 6 + INDEX[name] % 2

        def full_at(h, name):
            return h * NSTEP + (INDEX[name] + 1)

        def drained_at(h, n):
            if n < 0:
                assert STEPS[-1][1] == STEPS[n][1]
                return s["c_" + STEPS[-1][1]], h * PER[STEPS[-1][1]]
            engine = STEPS[n][1]
            count = sum(x == engine for _, x in STEPS[:n + 1])
            return s["c_" + engine], h * PER[engine] + count

        def emptied(h, name):
            return drained_at(h, INDEX[name])

        w_in = t["w_in"][0].rearrange("(k p) n -> p k n", p=P)
        w_lo_v = t["w_lru_o"][0].rearrange("(k p) n -> p k n", p=P)
        w_go_v = t["w_gla_o"][0].rearrange("(k p) n -> p k n", p=P)
        x_rows = [(t["x_prompt"][0], n * P, P) for n in range(NCHUNK)] + [(t["x_sample"].rearrange("a b d -> (a b) d"), 0, STOK)]

        def half(ap, m, which):
            return ap.rearrange("p (n h m) -> p n h m", h=2, m=m)[:, :, which, :]

        y_rows = [(out[0][0], n * P, P) for n in range(NCHUNK)] + [(out[1].rearrange("a b d -> (a b) d"), 0, STOK)]

        def store_y(sp, n):
            dst, r0, nr = y_rows[n]
            sp.wait_ge(s["y_ok"], n + 1)
            sp.dma_start(dst[r0:r0 + nr, :], yy[0:nr, n % 2, :]).then_inc(y_out[n % 2], 16)

        block = ctx.enter_context(nc.Block())

        @block.sync
        def _(sp):
            def row(r, ap):
                sp.dma_start(rows[r:r + ap.shape[0], 0:ap.shape[1]], ap).then_inc(s["rows_in"], 16)

            sp.wait_ge(s["pad_ok"], 1)
            row(R_CONVW, t["conv_w"][0])
            for r, name in ((R_CONVB, "conv_b"), (R_BR, "b_r"), (R_BI, "b_i"), (R_LAM, "lam"), (R_GN, "gla_norm_g"), (R_BA, "b_a")):
                row(r, t[name])
            row(R_BM, t["b_merge"].rearrange("o (r d) -> (o r) d", r=2))
            row(R_H0, t["state_lru_h"][0])
            row(R_CS, t["state_lru_conv"][0].rearrange("b k w -> (b k) w"))
            for n in range(TTILES):
                if n >= 4:
                    sp.wait_ge(s["x_T"], n - 3)
                src, r0, nr = x_rows[n]
                sp.dma_start(xt[0:nr, n % 4, :], src[r0:r0 + nr, :]).then_inc(s_x[n % 4], 16)
                if n == 2:
                    sp.dma_start(raw[:, 0], w_in[:, :, COL_X:COL_X + P]).then_inc(s_raw[0], 16)
                if n == 3:
                    sp.dma_start(raw[:, 1], w_in[:, :, COL_Z:COL_Z + P]).then_inc(s_raw[1], 16)

            def load(n, slot, src):
                sp.wait_ge(s["lo_ok"], n - 1)
                sp.sem_inc(s["sp_passed"], 1)
                sp.dma_start(raw[:, slot], src).then_inc(s_raw[slot], 16)

            def load_gates(i):
                sp.dma_start(graw[:, 0], t["w_r"][0][i]).then_inc(s["g_in"], 16)
                sp.dma_start(graw[:, 1], t["w_i"][0][i]).then_inc(s["g_in"], 16)

            sp.wait_ge(s["x_T"], TTILES)
            load_gates(0)
            with sp.Fori(1, KT) as i:
                load(2 * i, 0, w_in[:, :, bass.ds(i * P + COL_X, P)])
                load(2 * i + 1, 1, w_in[:, :, bass.ds(i * P + COL_Z, P)])
                sp.wait_ge(s["g_lo"], i)
                load_gates(i)
            with sp.Fori(0, KT) as i:
                load(2 * i + N_MIXA, 0, w_in[:, :, bass.ds(i * P + COL_GA, P)])
                load(2 * i + N_MIXA + 1, 1, w_lo_v[:, :, bass.ds(i * P, P)])
            sp.wait_ge(s["act_lo"], KT)
            sp.dma_start(araw[:, :, :], w_in[:, :, COL_A:COL_A + RANK]).then_inc(s["alo_in"], 16)
            with sp.Fori(0, HEADS) as h:
                for j, (col, step) in enumerate(((COL_Q, P), (COL_K, P), (COL_V, DV), (COL_V + P, DV), (COL_ZG, DV), (COL_ZG + P, DV))):
                    load(6 * h + (N_GLA + j), (N_GLA + j) % 2, w_in[:, :, bass.ds(h * step + col, P)])
            with sp.Fori(0, KT // 2) as i:
                for j in range(2):
                    load(2 * i + (N_GB + j), (N_GB + j) % 2, w_in[:, :, bass.ds(i * 2 * P + (COL_GB + j * P), P)])
            sp.wait_ge(s["ma_out"], 16 * KT)
            with sp.Fori(0, KT // 2) as i:
                for j in range(2):
                    load(2 * i + (N_YB + j), (N_YB + j) % 2, w_go_v[:, :, bass.ds(i * 2 * P + j * P, P)])
                    sp.wait_ge(s["job_done"], N_YB)
                    sp.wait_ge(s["wo_lo"], 2 * i + j)
                    sp.dma_start(woraw[:, :], t["w_out"][0][bass.ds(i * 2 * P + j * P, P), :]).then_inc(s["wo_in"], 16)
                    sp.wait_ge(merged[j], i)
                    sp.dma_start(mal[:, j, :], scratch[2 * i + j][:, 0:NTOK]).then_inc(mal_in[j], 16)
            sp.wait_ge(s["job_done"], N_YB + KT)
            sp.dma_start(fng[:, :], t["final_norm_g"].rearrange("(o d) -> o d", o=1).to_broadcast([P, D])).then_inc(s["fng_in"], 16)
            for n in range(TTILES):
                if n >= 2:
                    sp.wait_ge(s["y_res"], n - 1)
                src, r0, nr = x_rows[n]
                sp.dma_start(xr[0:nr, n % 2, :], src[r0:r0 + nr, :]).then_inc(s_xr[n % 2], 16)
                if n >= 1:
                    store_y(sp, n - 1)
            store_y(sp, TTILES - 1)
            for sm, v in ((y_out[0], 16 * 5), (y_out[1], 16 * 4), (s["tails_out"], 64), (s["st_out"], 16 * HEADS),
                          (s["st0_out"], 16 * HEADS), (s["ma_out"], 16 * KT)):
                sp.wait_ge(sm, v)


        @block.gpsimd
        def _(pool):
            n = [0]

            def step(ins):
                n[0] += 1
                ins.then_inc(s["pool_step"], 1)
                pool.wait_ge(s["pool_step"], n[0])

            step(pool.memset(ident[:, :], 0.0))
            pool.affine_select(out=ident[:, :], in_=ident[:, :], compare_op=ALU.not_equal, fill=1.0, base=0,
                               pattern=[[-1, P]], channel_multiplier=1).then_inc(s["ident_ok"], 1)
            for l, m in enumerate(LEVELS):
                mask = lmask[:, l, :]
                step(pool.memset(mask, 1.0))
                step(pool.affine_select(out=mask, in_=mask, compare_op=ALU.is_ge, fill=0.0, base=0,
                                        pattern=[[-2 * m, 64 // m], [0, m]], channel_multiplier=1))
                step(pool.affine_select(out=mask, in_=mask, compare_op=ALU.is_ge, fill=0.0, base=m - 1,
                                        pattern=[[2 * m, 64 // m], [0, m]], channel_multiplier=-1))
            step(pool.memset(smask[:, :], 1.0))
            step(pool.affine_select(out=smask[:, :], in_=smask[:, :], compare_op=ALU.is_ge, fill=0.0, base=0,
                                    pattern=[[-SLEN, NSEQ]], channel_multiplier=1))
            step(pool.affine_select(out=smask[:, :], in_=smask[:, :], compare_op=ALU.is_ge, fill=0.0, base=SLEN - 1,
                                    pattern=[[SLEN, NSEQ]], channel_multiplier=-1))
            step(pool.memset(ones[:, :], 1.0 / DV))
            step(pool.memset(notfirst[:, :], 1.0))
            step(pool.memset(notfirst[:, 0:SEQ].rearrange("p (n c) -> p n c", c=CHUNK)[:, :, 0:1], 0.0))
            step(pool.memset(notfirst[:, SEQ:NTOK].rearrange("p (n c) -> p n c", c=SLEN)[:, :, 0:1], 0.0))
            pool.memset(notfirst[:, NTOK:TOK], 0.0).then_inc(s["masks_ok"], 1)

            def lo(i, c):
                pool.wait_ge(s["hi_ok"], 2 * i + (c + 1))
                pool.tensor_tensor(wlo[:, c % 2], raw[:, c % 2], whi[:, c % 2].bitcast(F32), ALU.subtract).then_inc(s["lo_ok"], 1)

            with pool.Fori(0, (N_YB + KT) // 2) as i:
                lo(i, 0)
                lo(i, 1)

        @block.tensor
        def _(pe):
            def split_product(dst, wh, wl, mh, ml, first, last):
                pe.matmul(dst, wh, mh, start=first, stop=False)
                pe.matmul(dst, wh, ml, start=False, stop=False)
                return pe.matmul(dst, wl, mh, start=False, stop=last)

            def piece(c, b, mov, j):
                for k in range(KT):
                    cols = slice(j * PIECE, (j + 1) * PIECE)
                    ins = split_product(ps[:, b + j, 0:PIECE], whi[:, c % 2, k, :], wlo[:, c % 2, k, :],
                                        mov[:, 0, k, cols], mov[:, 1, k, cols], k == 0, k == KT - 1)
                return ins

            def job(i, c, b, mov):
                pe.wait_ge(s["lo_ok"], 2 * i + (c + 1))
                for j in range(PIECES):
                    ins = piece(c, b, mov, j)
                ins.then_inc(s["job_done"], 1)

            pe.wait_ge(s["ident_ok"], 1)
            pe.wait_ge(s["rows_in"], 16 * 10)
            for k in range(KT):
                ins = pe.transpose(ps[:, 6, k * NROW:(k + 1) * NROW], rows[:, k * P:(k + 1) * P], ident[0:NROW, 0:NROW])
            ins.then_inc(s["rows_T"], 1)
            for n in range(TTILES):
                nr = x_rows[n][2]
                b = bankA if n % 2 == 0 else bankB
                pe.wait_ge(s["x_scaled"], n + 1)
                if n >= 2:
                    pe.wait_ge(s["x_lo"], n - 1)
                for k in range(KT):
                    ins = pe.transpose(ps[:, b + k // 4, (k % 4) * P:(k % 4) * P + nr], xt[0:nr, n % 4, k * P:(k + 1) * P],
                                       ident[0:nr, 0:nr])
                ins.then_inc(s["x_T"], 1)
            pe.wait_ge(s["x_lo"], TTILES)
            pe.wait_ge(s["pad_ok"], 2)

            with pe.Fori(0, KT) as i:
                pe.wait_ge(s["r_tanh"], i)
                job(i, N_LRU, bankA, xn)
                pe.wait_ge(s["i_tanh"], i)
                job(i, N_LRU + 1, bankB, xn)
                pe.wait_ge(s["xc_lo"], i + 1)
                pe.wait_ge(s["g_lo"], i + 1)
                for g, b in ((0, bankA), (1, bankB)):
                    if g == 1:
                        pe.wait_ge(s["z_silu"], i + 1)
                    for j in range(PIECES):
                        cols = slice(j * PIECE, (j + 1) * PIECE)
                        ins = split_product(ps[:, b + j, 0:PIECE], ghi[:, g, :], glo[:, g, :], xcs[:, 0, cols], xcs[:, 1, cols],
                                            True, True)
                    ins.then_inc(s["r_done"] if g == 0 else s["i_done"], 1)

            with pe.Fori(0, KT) as i:
                pe.wait_ge(s["r_tanh"], KT)
                pe.wait_ge(s["ga_tanh"], i)
                job(i, N_MIXA, bankA, xn)
                pe.wait_ge(s["act_lo"], KT)
                pe.wait_ge(s["i_tanh"], KT)
                pe.wait_ge(s["ma_ok"], i)
                job(i, N_MIXA + 1, bankB, act_s)
            pe.wait_ge(s["h_tail"], KT)
            pe.wait_ge(s["vec_ok"], 1)
            for k in range(KT):
                ins = pe.transpose(ps[0:NTAIL, 6 + k // 4, (k % 4) * P:(k % 4 + 1) * P], tails[:, k, :], ident[:, :])
            ins.then_inc(s["tails_T"], 1)

            pe.wait_ge(s["alo_lo"], 1)
            pe.wait_ge(s["ga_tanh"], KT)
            for j in range(PIECES):
                for k in range(KT):
                    for r in range(2):
                        ins = pe.matmul(ps[:, bankA + j, 0:PIECE], aw[:, k, :], xn[:, r, k, j * PIECE:(j + 1) * PIECE],
                                        start=(k == 0 and r == 0), stop=(k == KT - 1 and r == 1))
            ins.then_inc(s["alo_mm"], 1)
            pe.wait_ge(s["masks_ok"], 1)
            pe.wait_ge(s["alo_ok"], 1)
            pe.wait_ge(s["tails_ok"], 2)
            pe.wait_ge(s["ma_ok"], KT)
            with pe.Fori(0, HEADS) as h:
                def c_step(name, emit):
                    pe.wait_ge(*drained_at(h, INDEX[name] - 2))
                    emit(bank(name)).then_inc(s["c_full"], 1)

                def gate(j):
                    def emit(b):
                        return pe.matmul(ps[:, b, 0:PIECE], wa2[:, :], alo[:, j * PIECE:(j + 1) * PIECE], start=True, stop=True)
                    c_step(f"g{j}", emit)

                def diagonal(n):
                    def emit(b):
                        for c in range(4):
                            cols = slice((4 * n + c) * P, (4 * n + c + 1) * P)
                            ins = pe.matmul(ps[:, b, c * P:(c + 1) * P], kb[:, cols], qb[:, cols], start=True, stop=True)
                        return ins
                    c_step(f"dg{n}", emit)

                def level(l):
                    pe.wait_ge(s["lev_qk"], h * len(LEVELS) + (l + 1))

                    def emit(b):
                        for c in range(NCHUNK):
                            tile = qk[:, l % 2, c * P:(c + 1) * P]
                            ins = pe.matmul(ps[:, b, c * 64:(c + 1) * 64], tile, half(tile, LEVELS[l], 1), start=True, stop=True)
                        return ins
                    c_step(f"L{l}", emit)

                def sample_levels(b):
                    for l, m in enumerate(SLEVELS):
                        pe.matmul(ps[0:STOK, b, 32 * l:32 * l + 32], qks[:, l, :], half(qks[:, l, :], m, 1), start=True, stop=True)
                    return pe.matmul(ps[0:STOK, b, 128:128 + STOK], kb[:, SEQ:NTOK], qb[:, SEQ:NTOK], start=True, stop=True)

                def transposes(prefix, src):
                    for g, name in enumerate("abc"):
                        def emit(b):
                            if g == 2:
                                pe.sem_inc(s["pe_passed"], 1)
                            for n in range(4 * g, min(4 * g + 4, TTILES)):
                                nr = P if n < NCHUNK else STOK
                                ins = pe.transpose(ps[0:nr, b, (n % 4) * P:(n % 4 + 1) * P], src[:, n * P:n * P + nr], ident[:, :])
                            return ins
                        c_step(prefix + name, emit)

                def outer(n):
                    def emit(b):
                        for c in range(2):
                            ins = pe.matmul(ps[:, b, c * DV:(c + 1) * DV], kT[:, 2 * n + c, :], vv[:, 2 * n + c, :], start=True, stop=True)
                        return ins
                    c_step(f"KV{n}", emit)

                def output(g, d):
                    def emit(b):
                        for c in range(4 * g, 4 * g + 4):
                            dst = ps[:, b, (c % 4) * P:(c % 4 + 1) * P]
                            ins = pe.matmul(dst, vv[:, c, d * P:(d + 1) * P], att[:, c, :], start=True, stop=(c == 0))
                            if c > 0:
                                ins = pe.matmul(dst, st[:, c - 1, d * P:(d + 1) * P], qb[:, c * P:(c + 1) * P], start=False, stop=True)
                        return ins
                    c_step(f"O{g}{d}", emit)

                def sample_output(b):
                    for d in range(VH):
                        lo = d * STOK
                        pe.matmul(ps[:, b, lo:lo + STOK], vv[0:STOK, NCHUNK, d * P:(d + 1) * P], att[0:STOK, NCHUNK, 0:STOK],
                                  start=True, stop=False, skip_group_check=True)
                        for q in range(NSEQ):
                            ins = pe.matmul(ps[:, b, lo + q * SLEN:lo + (q + 1) * SLEN], st0[:, q, d * P:(d + 1) * P],
                                            qb[:, SEQ + q * SLEN:SEQ + (q + 1) * SLEN], start=False, stop=(q == NSEQ - 1),
                                            skip_group_check=True)
                    return ins

                def sample_outer(n):
                    def emit(b):
                        for c in range(2):
                            ins = pe.matmul(ps[:, b, c * DV:(c + 1) * DV], kt[0:STOK, (2 * n + c) * P:(2 * n + c + 1) * P],
                                            vv[0:STOK, NCHUNK, :], start=True, stop=True)
                        return ins
                    c_step(f"sKV{n}", emit)

                def mean_square(j):
                    def emit(b):
                        for d in range(VH):
                            ins = pe.matmul(ps[:, b, 0:PIECE], ones[:, :], qk[:, d, j * PIECE:(j + 1) * PIECE], start=(d == 0), stop=(d == 1))
                        return ins
                    c_step(f"nrm{j}", emit)

                def start_job(c):
                    pe.wait_ge(s["lo_ok"], 6 * h + (N_GLA + c + 1))

                def part(c, b, j):
                    ins = piece(N_GLA + c, b, xn, j)
                    if j == PIECES - 1:
                        ins.then_inc(s["job_done"], 1)

                start_job(0)
                pe.wait_ge(s["zg_silu"], 2 * h)
                for j in range(PIECES):
                    part(0, bankA, j)
                pe.wait_ge(s["wa2_in"], 32 * (h + 1))
                gate(0)
                gate(1)
                start_job(1)
                part(1, bankB, 0)
                gate(2)
                part(1, bankB, 1)
                part(1, bankB, 2)
                start_job(2)
                pe.wait_ge(s["q_ok"], h + 1)
                part(2, bankA, 0)
                pe.wait_ge(s["k_ok"], h + 1)
                diagonal(0)
                diagonal(1)
                part(2, bankA, 1)
                level(0)
                part(2, bankA, 2)
                level(1)
                start_job(3)
                part(3, bankB, 0)
                level(2)
                pe.wait_ge(s["vT_ok"], 2 * h + 1)
                transposes("vt0", vT)
                part(3, bankB, 1)
                level(3)
                part(3, bankB, 2)
                level(4)
                start_job(4)
                part(4, bankA, 0)
                level(5)
                part(4, bankA, 1)
                level(6)
                pe.wait_ge(s["vT_ok"], 2 * h + 2)
                transposes("vt1", vT)
                part(4, bankA, 2)
                c_step("smp", sample_levels)
                pe.wait_ge(s["kt_ok"], h + 1)
                transposes("kT", kt)
                start_job(5)
                part(5, bankB, 0)
                pe.wait_ge(*emptied(h, "kTc"))
                for n in range(NCHUNK // 2):
                    outer(n)
                part(5, bankB, 1)
                pe.wait_ge(s["qb_ok"], h + 1)
                pe.wait_ge(*emptied(h, "KV3"))
                for g in range(2):
                    for d in range(VH):
                        output(g, d)
                pe.wait_ge(s["st0_in"], 16 * (h + 1))
                c_step("Os", sample_output)
                part(5, bankB, 2)
                pe.wait_ge(s["ktm_ok"], h + 1)
                for n in range(NSEQ // 2):
                    sample_outer(n)
                pe.wait_ge(s["o_sq"], 2 * (h + 1))
                for j in range(PIECES):
                    mean_square(j)

            pe.wait_ge(s["zg_silu"], 2 * HEADS)
            with pe.Fori(0, KT // 2) as i:
                for j, b in ((0, bankA), (1, bankB)):
                    pe.wait_ge(gb_tanh[j], i)
                    job(i, N_GB + j, b, xn)
            pe.wait_ge(s["act_lo"], 2 * KT)
            pe.wait_ge(gb_tanh[0], KT // 2)
            pe.wait_ge(gb_tanh[1], KT // 2)
            with pe.Fori(0, KT // 2) as i:
                for j, b in ((0, bankA), (1, bankB)):
                    pe.wait_ge(merged[j], i)
                    job(i, N_YB + j, b, act_s)
            pe.wait_ge(s["wo_lo"], KT)
            pe.wait_ge(merged[0], KT // 2)
            pe.wait_ge(merged[1], KT // 2)

            def out_tile(n, slot):
                pe.wait_ge(s["m_lo"], n + 1)
                b = (bankA, bankB)[slot]
                for e in range(2):
                    for k in range(KT):
                        ins = split_product(ps[:, b + e, :], ms[:, slot, 0, k, :], ms[:, slot, 1, k, :],
                                            wos[:, 0, k, e * 512:(e + 1) * 512], wos[:, 1, k, e * 512:(e + 1) * 512],
                                            k == 0, k == KT - 1)
                ins.then_inc(s["y_mm"], 1)

            out_tile(0, 0)
            out_tile(1, 1)
            with pe.Fori(1, NCHUNK // 2) as i:
                for slot in range(2):
                    pe.wait_ge(s["y_res"], 2 * i + (slot - 1))
                    out_tile(2 * i + slot, slot)
            pe.wait_ge(s["y_res"], NCHUNK - 1)
            out_tile(NCHUNK, 0)

        @block.scalar
        def _(act):
            def hi(i, c):
                act.wait_ge(s_raw[c % 2], 16 * i + 16 * (c // 2 + 1))
                if not (isinstance(i, int) and 2 * i + c < 2):
                    act.wait_ge(s["job_done"], 2 * i + (c - 1))
                act.activation(whi[:, c % 2], raw[:, c % 2], ACT.Copy).then_inc(s["hi_ok"], 1)

            act.dma_start(ngb[:, :], t["norm_g"][0:1, :].to_broadcast([P, D])).then_inc(s["ng_in"], 16)

            def x_hi(n):
                nr = x_rows[n][2]
                b = bankA if n % 2 == 0 else bankB
                act.wait_ge(s["x_T"], n + 1)
                act.activation(xn[:, 0, :, n * P:n * P + nr], ps[:, b:b + 2, :].rearrange("p a (c n) -> p (a c) n", n=P)[:, :, 0:nr],
                               ACT.Copy).then_inc(s["x_hi"], 1)

            for n in range(TTILES):
                nr = x_rows[n][2]
                act.wait_ge(s_x[n % 4], 16 * (n // 4 + 1))
                act.activation(junk0[0:nr, :], xt[0:nr, n % 4, :], ACT.Square, accum_out=ssum[0:nr, n:n + 1]).then_inc(s["x_sq"], 1)
                act.wait_ge(s["x_sq"], n + 1)
                act.wait_ge(s["pad_ok"], 3)
                act.activation(rstd[0:nr, n:n + 1], ssum[0:nr, n:n + 1], ACT.Sqrt, scale=1.0 / D, bias=ssum[0:nr, 31:32]).then_inc(s["x_rms"], 1)
                if n >= 1:
                    x_hi(n - 1)
            x_hi(TTILES - 1)
            hi(0, 0)
            hi(0, 1)
            act.wait_ge(s["vec_ok"], 1)
            act.activation(tiny[:, 0, :], vec[:, :, R_LAM], ACT.Abs).then_inc(s["tiny_ok"], 1)
            act.wait_ge(s["tiny_ok"], 1)
            act.activation(tiny[:, 0, :], tiny[:, 0, :], ACT.Exp, scale=-1.0).then_inc(s["tiny_ok"], 1)
            act.wait_ge(s["x_T"], TTILES)
            act.wait_ge(s["x_lo"], TTILES)

            act.wait_ge(s["dvec_ok"], 1)
            with act.Fori(0, KT) as i:
                act.wait_ge(s["job_done"], 2 * i + 1)
                act.wait_ge(s["x_tail"], i)
                act.activation(xbuf[:, HIST:HIST + 2 * PIECE].rearrange("p (a b) -> p a b", a=2), ps[:, bankA:bankA + 2, 0:PIECE], ACT.Copy)
                act.activation(xbuf[:, HIST + 2 * PIECE:XS], ps[:, bankA + 2, 0:SEQ - 2 * PIECE], ACT.Copy)
                act.activation(xbuf[:, XS:XW].rearrange("p (q n) -> p q n", q=NSEQ)[:, :, HIST:HIST + SLEN],
                               ps[:, bankA + 2, SEQ - 2 * PIECE:NTOK - 2 * PIECE].rearrange("p (q n) -> p q n", q=NSEQ),
                               ACT.Copy).then_inc(s["x_evac"], 1)
                hi(i, 2)
                act.wait_ge(s["g_in"], 32 * (i + 1))
                act.wait_ge(s["i_done"], i)
                act.activation(ghi[:, :, :], graw[:, :, :], ACT.Copy).then_inc(s["g_hi"], 1)
                act.wait_ge(s["conv_step"], 8 * (i + 1))
                act.activation(xcs[:, 0, :], xc[:, :], ACT.Copy).then_inc(s["xc_hi"], 1)
                act.wait_ge(s["job_done"], 2 * i + 2)
                act.wait_ge(s["z_silu"], i)
                act.activation(p3(tz[:, :]), slot3(bankB), ACT.Tanh, scale=0.5).then_inc(s["z_tanh"], 1)
                hi(i, 3)
                act.wait_ge(s["r_done"], i + 1)
                act.activation(p3(tr[:, :]), slot3(bankA), ACT.Tanh, scale=0.5, bias=dvec[:, i, V_BR:V_BR + 1]).then_inc(s["r_tanh"], 1)
                act.wait_ge(s["i_done"], i + 1)
                act.wait_ge(s["hz_ok"], i)
                act.activation(p3(ti[:, :]), slot3(bankB), ACT.Tanh, scale=0.5, bias=dvec[:, i, V_BI:V_BI + 1]).then_inc(s["i_tanh"], 1)
                act.wait_ge(s["r_tanh"], i + 1)
                act.activation(dec[:, :], tr[:, :], ACT.Exp, scale=dvec[:, i, V_NC:V_NC + 1], bias=dvec[:, i, V_NC:V_NC + 1]).then_inc(s["a_ok"], 1)
                act.activation(wt[:, :], tr[:, :], ACT.Tanh, scale=dvec[:, i, V_C:V_C + 1], bias=dvec[:, i, V_C:V_C + 1]).then_inc(s["t_ok"], 1)
                act.wait_ge(s["w_ok"], i + 1)
                act.activation(wt[:, :], wt[:, :], ACT.Sqrt, scale=0.25).then_inc(s["m_ok"], 1)

            act.wait_ge(s["hz_ok"], KT)
            act.wait_ge(s["x_tail"], KT)
            with act.Fori(0, KT) as i:
                act.activation(act_s[:, 0, i, :], keep[:, i, :], ACT.Copy).then_inc(s["act_hi"], 1)
            act.wait_ge(s["act_lo"], KT)
            with act.Fori(0, KT) as i:
                act.wait_ge(s["job_done"], 2 * i + (N_MIXA + 1))
                act.wait_ge(s["ma_ok"], i)
                act.activation(p3(ta[:, :]), slot3(bankA), ACT.Tanh, scale=0.5, bias=dvec[:, i, V_BMA:V_BMA + 1]).then_inc(s["ga_tanh"], 1)
                hi(i, N_MIXA + 2)
                act.wait_ge(s["job_done"], 2 * i + (N_MIXA + 2))
                hi(i, N_MIXA + 3)
                act.wait_ge(s["ma_ok"], i + 1)
                act.dma_start(scratch[i], ma[:, :]).then_inc(s["ma_out"], 16)
            act.wait_ge(s["alo_in"], 16)
            act.wait_ge(s["alo_zero"], 1)
            act.activation(aw[:, :, 0:RANK], araw[:, :, :], ACT.Copy).then_inc(s["alo_hi"], 1)
            act.wait_ge(s["tails_T"], 1)
            for n in range(2):
                act.activation(trow[:, n * 512:(n + 1) * 512], ps[0:NTAIL, 6 + n, :], ACT.Copy).then_inc(s["tails_ok"], 1)
            act.wait_ge(s["tails_ok"], 2)
            for dst, r0, nr in ((out[2][0], 0, 1), (out[5][0], 1, NSEQ), (out[3][0, 0], T_C, HIST),
                                (out[6][0].rearrange("b k w -> (b k) w"), T_C + HIST, NSEQ * HIST)):
                act.dma_start(dst, trow[r0:r0 + nr, :]).then_inc(s["tails_out"], 16)
            act.wait_ge(s["alo_mm"], 1)
            act.activation(alo[:, :].rearrange("p (a b) -> p a b", a=PIECES), ps[0:2 * RANK, bankA:bankA + PIECES, 0:PIECE],
                           ACT.Copy).then_inc(s["alo_ok"], 1)

            with act.Fori(0, HEADS) as h:
                def job_at(c):
                    act.wait_ge(s["job_done"], 6 * h + (N_GLA + c + 1))

                def full(name):
                    act.wait_ge(s["c_full"], full_at(h, name))

                def token_tiles(prefix, dst):
                    for g, name in enumerate("abc"):
                        full(prefix + name)
                        if g < 2:
                            act.activation(dst(4 * g, 4, P), ps[:, bank(prefix + name), :].rearrange("p (c n) -> p c n", n=P),
                                           ACT.Copy).then_inc(s["c_act"], 1)
                        else:
                            act.activation(dst(8, 1, STOK), ps[0:STOK, bank(prefix + name), 0:P].rearrange("p (c n) -> p c n", n=P),
                                           ACT.Copy).then_inc(s["c_act"], 1)

                def level_exp(l):
                    m = LEVELS[l]
                    n = SEQ if m > SLEVELS[0] else NTOK
                    act.wait_ge(s["lev_d"], h * len(LEVELS) + (l + 1))
                    for which, sign in ((0, -1.0), (1, 1.0)):
                        v = half(ring[l % 2][:, 0:n], m, which)
                        ins = act.activation(v, v, ACT.Exp, scale=sign / GATE_NORM)
                    ins.then_inc(s["lev_e"], 1)

                for r in range(2):
                    act.dma_start(wa2[r * RANK:(r + 1) * RANK, :], t["w_a2"][0][:, bass.ds(h * P, P)]).then_inc(s["wa2_in"], 16)
                job_at(0)
                act.activation(p3(qb[:, :]), slot3(bankA), ACT.Copy, scale=float(DK) ** -0.5).then_inc(s["q_ok"], 1)
                hi(3 * h, N_GLA + 2)
                act.wait_ge(s["st0_out"], 16 * h)
                act.dma_start(st0[:, :, :], t["state_gla"][0].rearrange("b h p v -> h p b v")[h]).then_inc(s["st0_in"], 16)
                act.wait_ge(s["og_ok"], 2 * h)
                for j in range(PIECES):
                    full(f"g{j}")
                    act.sem_inc(s["act_passed"], 1)
                    act.activation(gb[:, j * PIECE:(j + 1) * PIECE], ps[:, bank(f"g{j}"), 0:PIECE], ACT.Identity,
                                   bias=vec[:, h, R_BA:R_BA + 1]).then_inc(s["c_act"], 1)
                act.wait_ge(*emptied(h, "g2"))
                act.activation(dd[:, :], gb[:, :], ACT.Abs).then_inc(s["g_abs"], 1)
                act.wait_ge(s["g_abs"], h + 1)
                act.activation(dd[:, :], dd[:, :], ACT.Exp, scale=-1.0).then_inc(s["g_exp"], 1)
                act.wait_ge(s["g_exp"], h + 1)
                act.activation(dd[:, :], dd[:, :], ACT.Ln, bias=1.0).then_inc(s["g_ln"], 1)
                job_at(1)
                act.activation(p3(kb[:, :]), slot3(bankB), ACT.Copy).then_inc(s["k_ok"], 1)
                hi(3 * h, N_GLA + 3)
                level_exp(0)
                level_exp(1)
                level_exp(2)
                job_at(2)
                act.activation(p3(vT[:, :]), slot3(bankA), ACT.Copy).then_inc(s["vT_ok"], 1)
                hi(3 * h, N_GLA + 4)
                level_exp(3)
                token_tiles("vt0", lambda c, n, nr: vv[0:nr, c:c + n, 0:P])
                level_exp(4)
                job_at(3)
                act.activation(p3(vT[:, :]), slot3(bankB), ACT.Copy).then_inc(s["vT_ok"], 1)
                hi(3 * h, N_GLA + 5)
                level_exp(5)
                level_exp(6)
                token_tiles("vt1", lambda c, n, nr: vv[0:nr, c:c + n, P:DV])
                act.activation(dlast[:, 0:NCHUNK], gb[:, CHUNK - 1:SEQ:CHUNK], ACT.Exp, scale=1.0 / GATE_NORM)
                act.activation(dlast[:, NCHUNK:NCHUNK + NSEQ], gb[:, SEQ + SLEN - 1:NTOK:SLEN], ACT.Exp, scale=1.0 / GATE_NORM).then_inc(s["dlast_ok"], 1)
                act.wait_ge(s["kt_d"], h + 1)
                act.activation(kt[:, 0:NTOK], kt[:, 0:NTOK], ACT.Exp, scale=1.0 / GATE_NORM).then_inc(s["kt_e"], 1)
                act.wait_ge(s["lev_qk"], len(LEVELS) * (h + 1))
                act.activation(dd[:, :], gb[:, :], ACT.Exp, scale=1.0 / GATE_NORM).then_inc(s["qb_e"], 1)
                job_at(4)
                act.activation(p3(vT[:, :]), slot3(bankA), ACT.Tanh, scale=0.5).then_inc(s["zg_tanh"], 1)
                hi(3 * h, N_GLA + 6)
                token_tiles("kT", lambda c, n, nr: kT[0:nr, c:c + n, :])
                for g in range(2):
                    for d in range(VH):
                        full(f"O{g}{d}")
                        act.activation(oo[d][:, g * 512:(g + 1) * 512], ps[:, bank(f"O{g}{d}"), :], ACT.Copy).then_inc(s["c_act"], 1)
                full("Os")
                act.activation(oo[0][:, SEQ:NTOK], ps[:, bank("Os"), 0:STOK], ACT.Copy)
                act.activation(oo[1][:, SEQ:NTOK], ps[:, bank("Os"), STOK:2 * STOK], ACT.Copy).then_inc(s["c_act"], 1)
                act.wait_ge(*emptied(h, "Os"))
                for d in range(VH):
                    act.activation(qk[:, d, :], oo[d][:, :], ACT.Square).then_inc(s["o_sq"], 1)
                job_at(5)
                act.wait_ge(s["zg_silu"], 2 * h + 1)
                act.activation(p3(vT[:, :]), slot3(bankB), ACT.Tanh, scale=0.5).then_inc(s["zg_tanh"], 1)
                hi(3 * h, N_GLA + 7)
                for j in range(PIECES):
                    full(f"nrm{j}")
                    act.activation(kt[:, j * PIECE:(j + 1) * PIECE], ps[:, bank(f"nrm{j}"), 0:PIECE], ACT.Ln,
                                   bias=ssum[:, 31:32]).then_inc(s["c_act"], 1)
                act.wait_ge(*emptied(h, "nrm2"))
                act.activation(kt[:, :], kt[:, :], ACT.Exp, scale=-0.5).then_inc(s["n_rstd"], 1)
                act.wait_ge(*emptied(h, "KV3"))
                act.dma_start(out[4][0, 0][h], st[:, NCHUNK - 1, :]).then_inc(s["st_out"], 16)
                act.wait_ge(*emptied(h, "sKV3"))
                act.dma_start(out[7][0].rearrange("b h p v -> h p b v")[h], st0[:, :, :]).then_inc(s["st0_out"], 16)

            act.wait_ge(s["og_ok"], 2 * HEADS)
            act.wait_ge(s["st_out"], 16 * HEADS)
            act.wait_ge(s["st0_out"], 16 * HEADS)
            with act.Fori(0, KT) as i:
                act.activation(act_s[:, 0, i, :], keep[:, i, :], ACT.Copy).then_inc(s["act_hi"], 1)
            act.wait_ge(s["act_lo"], 2 * KT)
            with act.Fori(0, KT // 2) as i:
                for j, b in ((0, bankA), (1, bankB)):
                    act.wait_ge(s["job_done"], 2 * i + (N_GB + j + 1))
                    act.activation(p3(keep[:, 2 * i + j, :]), slot3(b), ACT.Tanh, scale=0.5,
                                   bias=dvec[:, 2 * i + j, V_BMB:V_BMB + 1]).then_inc(gb_tanh[j], 1)
                    hi(i, N_GB + j + 2)

            def w_out_hi(i, j):
                act.wait_ge(s["wo_in"], 32 * i + 16 * (j + 1))
                act.activation(wos[:, 0, 2 * i + j, :], woraw[:, :], ACT.Copy).then_inc(s["wo_hi"], 1)

            with act.Fori(0, KT // 2 - 1) as i:
                for j in range(2):
                    w_out_hi(i, j)
                    act.wait_ge(s["job_done"], 2 * i + (N_YB + j + 1))
                    hi(i, N_YB + j + 2)
            for j in range(2):
                w_out_hi(KT // 2 - 1, j)

            def merged_hi(n):
                nr = x_rows[n][2]
                if n >= 2:
                    act.wait_ge(s["y_mm"], n - 1)
                act.activation(ms[:, n % 2, 0, :, 0:nr], keep[:, :, n * P:n * P + nr], ACT.Copy).then_inc(s["m_hi"], 1)

            act.wait_ge(merged[0], KT // 2)
            act.wait_ge(merged[1], KT // 2)
            act.wait_ge(s["job_done"], N_YB + KT)
            merged_hi(0)
            for n in range(TTILES):
                nr = x_rows[n][2]
                if n + 1 < TTILES:
                    merged_hi(n + 1)
                act.wait_ge(s["y_res"], n + 1)
                act.activation(junk1[0:nr, :], yy[0:nr, n % 2, :], ACT.Square, accum_out=ssum[0:nr, 16 + n:17 + n]).then_inc(s["y_sq"], 1)
                act.wait_ge(s["y_sq"], n + 1)
                act.activation(rstd[0:nr, 16 + n:17 + n], ssum[0:nr, 16 + n:17 + n], ACT.Sqrt, scale=1.0 / D,
                               bias=ssum[0:nr, 31:32]).then_inc(s["y_rms"], 1)

        @block.vector
        def _(dve):
            dve.memset(rows[:, :], 0.0).then_inc(s["pad_ok"], 1)
            dve.memset(xn[:, :, :, NTOK:TOK].bitcast(F32), 0.0).then_inc(s["pad_ok"], 1)
            dve.memset(ssum[:, 31:32], EPS).then_inc(s["pad_ok"], 1)
            dve.wait_ge(s["ng_in"], 16)

            def x_lo(n):
                nr = x_rows[n][2]
                b = bankA if n % 2 == 0 else bankB
                cols = slice(n * P, n * P + nr)
                dve.wait_ge(s["x_hi"], n + 1)
                dve.tensor_tensor(xn[:, 1, :, cols], ps[:, b:b + 2, :].rearrange("p a (c n) -> p (a c) n", n=P)[:, :, 0:nr],
                                  xn[:, 0, :, cols].bitcast(F32), ALU.subtract).then_inc(s["x_lo"], 1)

            for n in range(TTILES):
                nr = x_rows[n][2]
                dve.wait_ge(s["x_rms"], n + 1)
                dve.reciprocal(rstd[0:nr, n:n + 1], rstd[0:nr, n:n + 1]).then_inc(s["x_rstd"], 1)
                dve.wait_ge(s["x_rstd"], n + 1)
                tile = xt[0:nr, n % 4, :]
                dve.scalar_tensor_tensor(tile, tile, rstd[0:nr, n:n + 1], ngb[0:nr, :], ALU.mult, ALU.mult).then_inc(s["x_scaled"], 1)
                if n >= 1:
                    x_lo(n - 1)
            x_lo(TTILES - 1)
            dve.wait_ge(s["rows_T"], 1)
            dve.tensor_copy(vec[:, :, :], ps[:, 6, 0:KT * NROW].rearrange("p (k r) -> p k r", k=KT)).then_inc(s["vec_ok"], 1)

            n_tiny = [2]

            def tiny_step(ins):
                n_tiny[0] += 1
                ins.then_inc(s["tiny_ok"], 1)
                dve.wait_ge(s["tiny_ok"], n_tiny[0])

            dve.wait_ge(s["tiny_ok"], 2)
            e, r, q, mx, v = (tiny[:, n, :] for n in range(5))
            tiny_step(dve.tensor_scalar(r, e, 2.0, None, ALU.add))
            tiny_step(dve.reciprocal(r, r))
            tiny_step(dve.tensor_tensor(e, e, r, ALU.mult))
            tiny_step(dve.tensor_tensor(r, e, e, ALU.mult))
            tiny_step(dve.tensor_scalar(q, r, 1.0 / 17, None, ALU.mult))
            for c in (15, 13, 11, 9, 7, 5, 3):
                tiny_step(dve.scalar_tensor_tensor(q, q, 1.0 / c, r, ALU.add, ALU.mult))
            tiny_step(dve.scalar_tensor_tensor(q, q, 1.0, e, ALU.add, ALU.mult))
            tiny_step(dve.tensor_scalar(mx, vec[:, :, R_LAM], -1.0, 0.0, ALU.mult, ALU.max))
            tiny_step(dve.scalar_tensor_tensor(v, q, 2.0, mx, ALU.mult, ALU.add))
            dve.tensor_scalar(dvec[:, :, V_C], v, RG_C / 2, None, ALU.mult)
            dve.tensor_scalar(dvec[:, :, V_NC], v, -RG_C / 2, None, ALU.mult)
            dve.tensor_scalar(dvec[:, :, V_BR:V_BI + 1], vec[:, :, R_BR:R_BI + 1], 0.5, None, ALU.mult)
            dve.tensor_scalar(dvec[:, :, V_BMA:V_BMB + 1], vec[:, :, R_BM:R_BM + 2], 0.5, None, ALU.mult).then_inc(s["dvec_ok"], 1)

            dve.wait_ge(s["x_T"], TTILES)
            dve.memset(xbuf[:, 0:HIST], 0.0)
            dve.memset(xc[:, NTOK:TOK], 0.0)
            hist = xbuf[:, XS:XW].rearrange("p (q n) -> p q n", q=NSEQ)
            with dve.Fori(0, KT) as i:
                dve.tensor_copy(hist[:, :, 0:HIST], vec[:, i, R_CS:NROW].rearrange("p (q n) -> p q n", q=NSEQ)).then_inc(s["hist_ok"], 1)
                dve.wait_ge(s["hist_ok"], i + 1)
                dve.wait_ge(s["x_evac"], i + 1)
                xcp = xc[:, 0:SEQ]
                xcq = xc[:, SEQ:NTOK].rearrange("p (q n) -> p q n", q=NSEQ)
                for k in range(CONV):
                    wk = vec[:, i, R_CONVW + k:R_CONVW + k + 1]
                    for which, (dst, src) in enumerate(((xcp, xbuf[:, k:k + SEQ]), (xcq, hist[:, :, k:k + SLEN]))):
                        if k == 0:
                            ins = dve.tensor_scalar(dst, src, wk, vec[:, i, R_CONVB:R_CONVB + 1], ALU.mult, ALU.add)
                        else:
                            dve.wait_ge(s["conv_step"], 8 * i + (2 * k - 1 + which))
                            ins = dve.scalar_tensor_tensor(dst, src, wk, dst, ALU.mult, ALU.add)
                        ins.then_inc(s["conv_step"], 1)
                dve.tensor_copy(tails[:, i, T_C:T_C + HIST], xbuf[:, SEQ:SEQ + HIST])
                dve.tensor_copy(tails[:, i, T_C + HIST:NTAIL].rearrange("p (q n) -> p q n", q=NSEQ),
                                hist[:, :, SLEN:SLEN + HIST]).then_inc(s["x_tail"], 1)
                dve.wait_ge(s["g_hi"], i + 1)
                dve.tensor_tensor(glo[:, :, :], graw[:, :, :], ghi[:, :, :].bitcast(F32), ALU.subtract).then_inc(s["g_lo"], 1)
                dve.wait_ge(s["xc_hi"], i + 1)
                dve.tensor_tensor(xcs[:, 1, :], xc[:, :], xcs[:, 0, :].bitcast(F32), ALU.subtract).then_inc(s["xc_lo"], 1)
                dve.wait_ge(s["z_tanh"], i + 1)
                dve.scalar_tensor_tensor(p3(sz[:, :]), p3(tz[:, :]), 1.0, slot3(bankB), ALU.add, ALU.mult).then_inc(s["z_silu"], 1)
                dve.wait_ge(s["i_tanh"], i + 1)
                dve.scalar_tensor_tensor(ti[:, :], ti[:, :], 1.0, xc[:, :], ALU.add, ALU.mult).then_inc(s["i_x"], 1)
                dve.wait_ge(s["a_ok"], i + 1)
                dve.tensor_tensor(hh[:, :], dec[:, :], dec[:, :], ALU.mult).then_inc(s["a_sq"], 1)
                dve.wait_ge(s["a_sq"], i + 1)
                dve.wait_ge(s["t_ok"], i + 1)
                dve.scalar_tensor_tensor(wt[:, :], hh[:, :], 1.0, wt[:, :], ALU.add, ALU.mult).then_inc(s["w_ok"], 1)
                first_a = dec[:, SEQ:NTOK:SLEN]
                first_u = ti[:, SEQ:NTOK:SLEN]
                dve.tensor_tensor(fix[:, :], first_a, vec[:, i, R_H0:R_H0 + NSEQ], ALU.mult).then_inc(s["fix_step"], 1)
                dve.wait_ge(s["m_ok"], i + 1)
                dve.wait_ge(s["i_x"], i + 1)
                dve.tensor_tensor(ti[:, :], ti[:, :], wt[:, :], ALU.mult).then_inc(s["u_ok"], 1)
                dve.wait_ge(s["u_ok"], i + 1)
                dve.wait_ge(s["fix_step"], 3 * i + 1)
                dve.tensor_tensor(first_u, first_u, fix[:, :], ALU.add).then_inc(s["fix_step"], 1)
                dve.memset(first_a, 0.0).then_inc(s["fix_step"], 1)
                dve.wait_ge(s["fix_step"], 3 * i + 3)
                dve.tensor_tensor_scan(hh[:, :], dec[:, :], ti[:, :], 0.0, ALU.mult, ALU.add).then_inc(s["h_ok"], 1)
                dve.wait_ge(s["h_ok"], i + 1)
                dve.wait_ge(s["z_silu"], i + 1)
                dve.tensor_tensor(keep[:, i, :], hh[:, :], sz[:, :], ALU.mult).then_inc(s["hz_ok"], 1)
                dve.tensor_copy(tails[:, i, T_H:T_H + 1], hh[:, SEQ - 1:SEQ])
                dve.tensor_copy(tails[:, i, T_H + 1:T_H + 1 + NSEQ], hh[:, SEQ + SLEN - 1:NTOK:SLEN]).then_inc(s["h_tail"], 1)

            def split_operand(first):
                with dve.Fori(0, KT) as i:
                    dve.wait_ge(s["act_hi"], i + (first + 1))
                    dve.tensor_tensor(act_s[:, 1, i, :], keep[:, i, :], act_s[:, 0, i, :].bitcast(F32), ALU.subtract).then_inc(s["act_lo"], 1)

            dve.wait_ge(s["h_tail"], KT)
            split_operand(0)
            dve.wait_ge(s["act_lo"], KT)
            dve.memset(aw[:, :, :].bitcast(F32), 0.0).then_inc(s["alo_zero"], 1)
            with dve.Fori(0, KT) as i:
                dve.wait_ge(s["ga_tanh"], i + 1)
                dve.wait_ge(s["job_done"], 2 * i + (N_MIXA + 2))
                dve.wait_ge(s["ma_out"], 16 * i)
                dve.scalar_tensor_tensor(p3(ma[:, :]), p3(ta[:, :]), 1.0, slot3(bankB), ALU.add, ALU.mult).then_inc(s["ma_ok"], 1)
            dve.wait_ge(s["alo_hi"], 1)
            dve.tensor_tensor(aw[:, :, RANK:2 * RANK], araw[:, :, :], aw[:, :, 0:RANK].bitcast(F32), ALU.subtract).then_inc(s["alo_lo"], 1)

            dve.memset(att[:, :, :], 0.0).then_inc(s["att_zero"], 1)
            dve.wait_ge(s["att_zero"], 1)
            dve.wait_ge(s["masks_ok"], 1)
            dve.wait_ge(s["tails_out"], 64)
            dve.wait_ge(s["ma_out"], 16 * KT)
            with dve.Fori(0, HEADS) as h:
                def full(name):
                    dve.wait_ge(s["c_full"], full_at(h, name))

                def distance(l):
                    m = LEVELS[l]
                    n = SEQ if m > SLEVELS[0] else NTOK
                    v = gb[:, 0:n].rearrange("p (n m) -> p n m", m=2 * m)
                    if l >= 2:
                        dve.wait_ge(s["lev_qk"], h * len(LEVELS) + (l - 1))
                    dve.tensor_tensor(ring[l % 2][:, 0:n].rearrange("p (n m) -> p n m", m=2 * m), v,
                                      v[:, :, m - 1:m].to_broadcast([P, n // (2 * m), 2 * m]), ALU.subtract).then_inc(s["lev_d"], 1)

                def level_operands(l):
                    m = LEVELS[l]
                    dve.wait_ge(s["lev_e"], h * len(LEVELS) + (l + 1))
                    if l >= 2:
                        full(f"L{l - 2}")
                    src = ring[l % 2]
                    if m in SLEVELS:
                        dst = qks[:, SLEVELS.index(m), :]
                        dve.tensor_tensor(half(dst, m, 0), half(kb[:, SEQ:NTOK], m, 0), half(src[:, SEQ:NTOK], m, 0), ALU.mult)
                        dve.tensor_tensor(half(dst, m, 1), half(qb[:, SEQ:NTOK], m, 1), half(src[:, SEQ:NTOK], m, 1), ALU.mult)
                    dst = qk[:, l % 2, 0:SEQ]
                    dve.tensor_tensor(half(dst, m, 0), half(kb[:, 0:SEQ], m, 0), half(src[:, 0:SEQ], m, 0), ALU.mult)
                    dve.tensor_tensor(half(dst, m, 1), half(qb[:, 0:SEQ], m, 1), half(src[:, 0:SEQ], m, 1), ALU.mult).then_inc(s["lev_qk"], 1)

                def order(name):
                    n = [x for x, e in STEPS[:INDEX[name]] if e == "dve"]
                    if n:
                        dve.wait_ge(*emptied(h, n[-1]))
                    dve.sem_inc(s["dve_passed"], 1)

                def keep_level(l):
                    m = LEVELS[l]
                    full(f"L{l}")
                    order(f"L{l}")
                    dst = att[:, 0:NCHUNK, :].rearrange("p c (q h m) -> p c q h m", h=2, m=m)[:, :, :, 1, :]
                    mask = lmask[:, l, :].bitcast(U32).rearrange("p (o q m) -> p o q m", o=1, m=m).to_broadcast([P, NCHUNK, 64 // m, m])
                    dve.copy_predicated(dst, mask, ps[:, bank(f"L{l}"), :].rearrange("p (c q m) -> p c q m", c=NCHUNK, m=m)).then_inc(s["c_dve"], 1)

                def keep_diagonal(n):
                    full(f"dg{n}")
                    order(f"dg{n}")
                    mask = ident[:, :].bitcast(U32).rearrange("p (o m) -> p o m", o=1).to_broadcast([P, 4, P])
                    dve.copy_predicated(att[:, 4 * n:4 * n + 4, :], mask,
                                        ps[:, bank(f"dg{n}"), :].rearrange("p (c m) -> p c m", c=4)).then_inc(s["c_dve"], 1)

                dve.wait_ge(s["g_ln"], h + 1)
                dve.scalar_tensor_tensor(gb[:, :], gb[:, :], 0.0, dd[:, :], ALU.min, ALU.subtract).then_inc(s["g_ok"], 1)
                dve.wait_ge(s["g_ok"], h + 1)
                dve.tensor_tensor_scan(gb[:, :], notfirst[:, :], gb[:, :], 0.0, ALU.mult, ALU.add).then_inc(s["b_ok"], 1)
                dve.wait_ge(s["b_ok"], h + 1)
                dve.wait_ge(s["c_full"], h * NSTEP)
                distance(0)
                distance(1)
                dve.wait_ge(s["q_ok"], h + 1)
                dve.wait_ge(s["k_ok"], h + 1)
                level_operands(0)
                distance(2)
                keep_diagonal(0)
                keep_diagonal(1)
                for l in range(1, len(LEVELS)):
                    level_operands(l)
                    if l + 2 < len(LEVELS):
                        distance(l + 2)
                    if l == len(LEVELS) - 2:
                        dve.wait_ge(s["lev_qk"], h * len(LEVELS) + (l + 1))
                        for c0, c1, n in ((0, SEQ, CHUNK), (SEQ, NTOK, SLEN)):
                            v = gb[:, c0:c1].rearrange("p (c n) -> p c n", n=n)
                            ins = dve.tensor_tensor(kt[:, c0:c1].rearrange("p (c n) -> p c n", n=n),
                                                    v[:, :, n - 1:n].to_broadcast([P, (c1 - c0) // n, n]), v, ALU.subtract)
                        ins.then_inc(s["kt_d"], 1)
                    keep_level(l - 1)
                keep_level(len(LEVELS) - 1)
                dve.wait_ge(s["kt_e"], h + 1)
                dve.tensor_tensor(kt[:, 0:NTOK], kt[:, 0:NTOK], kb[:, 0:NTOK], ALU.mult).then_inc(s["kt_ok"], 1)
                full("smp")
                order("smp")
                for l, m in enumerate(SLEVELS):
                    mask = lmask[0:STOK, LEVELS.index(m), 0:32].bitcast(U32).rearrange("p (q m) -> p q m", m=m)
                    dve.copy_predicated(half(att[0:STOK, NCHUNK, 0:STOK], m, 1), mask,
                                        ps[0:STOK, bank("smp"), 32 * l:32 * l + 32].rearrange("p (q m) -> p q m", m=m)).then_inc(s["att_step"], 1)
                    dve.wait_ge(s["att_step"], 3 * h + (l + 1))
                    dve.sem_inc(s["dve_passed"], 1)
                dve.copy_predicated(att[0:STOK, NCHUNK, 0:STOK], ident[0:STOK, 0:STOK].bitcast(U32),
                                    ps[0:STOK, bank("smp"), 128:128 + STOK]).then_inc(s["c_dve"], 1)
                dve.wait_ge(s["qb_e"], h + 1)
                dve.tensor_tensor(qb[:, :], qb[:, :], dd[:, :], ALU.mult).then_inc(s["qb_ok"], 1)
                dve.wait_ge(s["zg_tanh"], 2 * h + 1)
                dve.scalar_tensor_tensor(p3(keep[:, 2 * h, :]), p3(vT[:, :]), 1.0, slot3(bankA), ALU.add, ALU.mult).then_inc(s["zg_silu"], 1)
                dve.wait_ge(*emptied(h, "kTc"))
                dve.tensor_tensor(kt[0:STOK, 0:NSEQ * P].rearrange("p (q n) -> p q n", q=NSEQ),
                                  kT[0:STOK, NCHUNK:NCHUNK + 1, :].to_broadcast([STOK, NSEQ, P]),
                                  smask[:, :].rearrange("p (q o) -> p q o", o=1).to_broadcast([STOK, NSEQ, P]), ALU.mult).then_inc(s["ktm_ok"], 1)
                dve.wait_ge(s["dlast_ok"], h + 1)
                dve.wait_ge(s["st_out"], 16 * h)
                for n in range(NCHUNK // 2):
                    full(f"KV{n}")
                    b = bank(f"KV{n}")
                    if n == 0:
                        ins = dve.tensor_copy(st[:, 0, :], ps[:, b, 0:DV])
                    else:
                        dve.wait_ge(*emptied(h, f"KV{n - 1}"))
                        ins = dve.scalar_tensor_tensor(st[:, 2 * n, :], st[:, 2 * n - 1, :], dlast[:, 2 * n:2 * n + 1], ps[:, b, 0:DV],
                                                       ALU.mult, ALU.add)
                    ins.then_inc(s["st_ok"], 1)
                    dve.wait_ge(s["st_ok"], (NCHUNK // 2) * h + (n + 1))
                    dve.scalar_tensor_tensor(st[:, 2 * n + 1, :], st[:, 2 * n, :], dlast[:, 2 * n + 1:2 * n + 2], ps[:, b, DV:2 * DV],
                                             ALU.mult, ALU.add).then_inc(s["c_dve"], 1)
                for n in range(NSEQ // 2):
                    full(f"sKV{n}")
                    for c in range(2):
                        q = 2 * n + c
                        ins = dve.scalar_tensor_tensor(st0[:, q, :], st0[:, q, :], dlast[:, NCHUNK + q:NCHUNK + q + 1],
                                                       ps[:, bank(f"sKV{n}"), c * DV:(c + 1) * DV], ALU.mult, ALU.add)
                    ins.then_inc(s["c_dve"], 1)
                dve.wait_ge(s["zg_tanh"], 2 * h + 2)
                dve.scalar_tensor_tensor(p3(keep[:, 2 * h + 1, :]), p3(vT[:, :]), 1.0, slot3(bankB), ALU.add, ALU.mult).then_inc(s["zg_silu"], 1)
                dve.wait_ge(s["n_rstd"], h + 1)
                for d in range(VH):
                    dve.scalar_tensor_tensor(oo[d][:, :], oo[d][:, :], vec[:, 2 * h + d, R_GN:R_GN + 1], kt[:, :], ALU.mult, ALU.mult).then_inc(s["o_norm"], 1)
                dve.wait_ge(s["zg_silu"], 2 * h + 2)
                for d in range(VH):
                    dve.wait_ge(s["o_norm"], 2 * h + (d + 1))
                    dve.tensor_tensor(keep[:, 2 * h + d, :], keep[:, 2 * h + d, :], oo[d][:, :], ALU.mult).then_inc(s["og_ok"], 1)

            split_operand(KT)
            dve.wait_ge(gb_tanh[0], KT // 2)
            dve.wait_ge(gb_tanh[1], KT // 2)
            with dve.Fori(0, KT // 2) as i:
                for j, b in ((0, bankA), (1, bankB)):
                    dve.wait_ge(s["wo_hi"], 2 * i + (j + 1))
                    dve.tensor_tensor(wos[:, 1, 2 * i + j, :], woraw[:, :], wos[:, 0, 2 * i + j, :].bitcast(F32), ALU.subtract).then_inc(s["wo_lo"], 1)
                    tile = keep[:, 2 * i + j, :]
                    dve.wait_ge(s["job_done"], 2 * i + (N_YB + j + 1))
                    dve.scalar_tensor_tensor(p3(tile), p3(tile), 1.0, slot3(b), ALU.add, ALU.mult).then_inc(s["yb_part"], 1)
                    dve.wait_ge(s["yb_part"], 2 * i + (j + 1))
                    dve.wait_ge(mal_in[j], 16 * (i + 1))
                    dve.tensor_tensor(tile[:, 0:NTOK], tile[:, 0:NTOK], mal[:, j, :], ALU.add).then_inc(merged[j], 1)

            def merged_lo(n):
                nr = x_rows[n][2]
                dve.wait_ge(s["m_hi"], n + 1)
                dve.tensor_tensor(ms[:, n % 2, 1, :, 0:nr], keep[:, :, n * P:n * P + nr], ms[:, n % 2, 0, :, 0:nr].bitcast(F32),
                                  ALU.subtract).then_inc(s["m_lo"], 1)

            merged_lo(0)
            for n in range(TTILES):
                nr = x_rows[n][2]
                b = (bankA, bankB)[n % 2]
                y = yy[0:nr, n % 2, :]
                if n + 1 < TTILES:
                    merged_lo(n + 1)
                if n == 0:
                    dve.wait_ge(s["fng_in"], 16)
                if n >= 2:
                    dve.wait_ge(y_out[n % 2], 16 * (n // 2))
                dve.wait_ge(s["y_mm"], n + 1)
                dve.wait_ge(s_xr[n % 2], 16 * (n // 2 + 1))
                dve.scalar_tensor_tensor(y.rearrange("p (a b) -> p a b", a=2), ps[0:nr, b:b + 2, :], 0.25,
                                         xr[0:nr, n % 2, :].rearrange("p (a b) -> p a b", a=2), ALU.mult, ALU.add).then_inc(s["y_res"], 1)
                dve.wait_ge(s["y_rms"], n + 1)
                r = rstd[0:nr, 16 + n:17 + n]
                dve.reciprocal(r, r).then_inc(s["y_rstd"], 1)
                dve.wait_ge(s["y_rstd"], n + 1)
                dve.scalar_tensor_tensor(y, y, r, fng[0:nr, :], ALU.mult, ALU.mult).then_inc(s["y_ok"], 1)


INPUTS = ["x_prompt", "x_sample", "state_lru_h", "state_lru_conv", "state_gla", "norm_g", "w_in", "conv_w", "conv_b",
          "w_r", "b_r", "w_i", "b_i", "lam", "w_a2", "b_a", "gla_norm_g", "w_lru_o", "w_gla_o", "b_merge", "w_out",
          "final_norm_g"]
OUTPUTS = [(1, SEQ, D), (NSEQ, SLEN, D), (1, 1, D), (1, 1, HIST, D), (1, 1, HEADS, DK, DV),
           (1, NSEQ, D), (1, NSEQ, HIST, D), (1, NSEQ, HEADS, DK, DV)]


def kernel(**inputs):
    import numpy as np
    import concourse.bacc as bacc
    from concourse.bass_utils import run_bass_kernel_spmd

    nc = bacc.Bacc("TRN2", target_bir_lowering=False, num_devices=1)
    arrays, t = {}, {}
    for name in INPUTS:
        a = np.ascontiguousarray(inputs[name])
        arrays["in_" + name] = a
        t[name] = nc.dram_tensor("in_" + name, a.shape, mybir.dt.from_np(a.dtype), kind="ExternalInput").ap()
    out = [nc.dram_tensor(f"out_{n}", shape, F32, kind="ExternalOutput").ap() for n, shape in enumerate(OUTPUTS)]
    build(nc, t, out)
    r = run_bass_kernel_spmd(nc, [arrays], core_ids=[0])
    return tuple(r.results[0][f"out_{n}"] for n in range(len(OUTPUTS)))
```

```python
import concourse.bass as bass
from concourse import mybir
from contextlib import ExitStack

F32 = mybir.dt.float32
F32R = mybir.dt.float32r
BF16 = mybir.dt.bfloat16
U32 = mybir.dt.uint32
ALU = mybir.AluOpType
ACT = mybir.ActivationFunctionType

P = 128
D = 1024
KT = D // P
SEQ = 1024
NSEQ, SLEN = 8, 8
STOK = NSEQ * SLEN
NTOK = SEQ + STOK
PIECE = 364
PIECES = 3
TOK = PIECE * PIECES
CONV = 4
HIST = CONV - 1
HEADS = 4
DK = 128
DV = 256
VH = DV // P
RANK = 16
CHUNK = 128
NCHUNK = SEQ // CHUNK
TTILES = NCHUNK + 1
LEVELS = (64, 32, 16, 8, 4, 2, 1)
SLEVELS = (4, 2, 1)
GATE_NORM = 16.0
EPS = 1e-6
RG_C = 8.0
COL_X, COL_Z, COL_Q, COL_K, COL_V, COL_ZG = 0, D, 2 * D, 2 * D + 512, 3 * D, 4 * D
COL_A = 5 * D
COL_GA = COL_A + RANK
COL_GB = COL_GA + D
N_IN = COL_GB + D
R_CONVW, R_CONVB, R_BR, R_BI, R_LAM, R_GN, R_BM, R_BA = 0, 4, 5, 6, 7, 8, 9, 11
R_H0, R_CS = 12, 20
NROW = R_CS + NSEQ * HIST
V_BR, V_BI, V_BMA, V_BMB, V_C, V_NC = range(6)
N_LRU, N_MIXA, N_GLA = 0, 2 * KT, 4 * KT
N_GB = N_GLA + 6 * HEADS
N_YB = N_GB + 8
ONE = 1
STARTS_AT_ONE = ("ma_ok", "wo_lo", "r_tanh", "i_tanh", "ga_tanh", "zg_silu", "x_tail", "i_done", "z_silu", "hz_ok", "st0_out", "st_out",
                 "og_ok", "merged0", "merged1", "gb_tanh0", "gb_tanh1", "c_full", "c_act", "c_dve")
NTAIL = 1 + NSEQ + HIST + NSEQ * HIST
T_H, T_C = 0, 1 + NSEQ
XS = HIST + SEQ
XW = XS + NSEQ * (HIST + SLEN)


def head_steps():
    steps = [("g0", "act"), ("g1", "act"), ("g2", "act"), ("dg0", "dve"), ("dg1", "dve")]
    steps += [("L0", "dve"), ("L1", "dve"), ("L2", "dve"), ("vt0a", "act"), ("vt0b", "act"), ("vt0c", "act")]
    steps += [("L3", "dve"), ("L4", "dve"), ("L5", "dve"), ("L6", "dve")]
    steps += [("vt1a", "act"), ("vt1b", "act"), ("vt1c", "act"), ("smp", "dve")]
    steps += [("kTa", "act"), ("kTb", "act"), ("kTc", "act")]
    steps += [(f"KV{n}", "dve") for n in range(NCHUNK // 2)]
    steps += [(f"O{g}{d}", "act") for g in range(2) for d in range(VH)] + [("Os", "act")]
    steps += [(f"sKV{n}", "dve") for n in range(NSEQ // 2)]
    steps += [(f"nrm{j}", "act") for j in range(PIECES)]
    return steps


def build(nc, t, out):
    ctx = ExitStack()
    with ctx:
        base = -(-nc.sbuf_base // 32) * 32

        def at(name, shape, dt, offset):
            return nc.alloc_sbuf_tensor_at(name, shape, dt, offset=base + offset)

        TILE = TOK * 4
        SLOT = -(-TILE // 32) * 32
        o_xn = 0
        o_raw = o_xn + 2 * KT * TILE
        o_hi = o_raw + 2 * KT * P * 4
        o_lo = o_hi + 2 * KT * P * 4
        o_keep = o_lo + 2 * KT * P * 4
        o_const = o_keep + KT * TILE
        xn = at("xn", [P, 2, KT, TOK], F32R, o_xn)
        raw = at("raw", [P, 2, KT, P], F32, o_raw)
        whi = at("whi", [P, 2, KT, P], F32R, o_hi)
        wlo = at("wlo", [P, 2, KT, P], F32R, o_lo)
        keep = at("keep", [P, KT, TOK], F32, o_keep)
        a = [o_const]

        def take(name, shape, dt, size):
            h = at(name, shape, dt, a[0])
            a[0] += -(-size // 32) * 32
            return h

        ident = take("ident", [P, P], F32, P * 4)
        vec = take("vec", [P, KT, NROW], F32, KT * NROW * 4)
        dvec = take("dvec", [P, KT, 6], F32, KT * 6 * 4)
        tiny = take("tiny", [P, 5, KT], F32, 5 * KT * 4)
        ssum = take("ssum", [P, 32], F32, 128)
        rstd = take("rstd", [P, 32], F32, 128)
        o_glaconst = a[0]
        ones = take("ones", [P, P], F32, P * 4)
        notfirst = take("notfirst", [P, TOK], BF16, TOK * 2)
        lmask = take("lmask", [P, len(LEVELS), 64], F32, len(LEVELS) * 64 * 4)
        smask = take("smask", [STOK, NSEQ], F32, NSEQ * 4)
        wa2 = take("wa2", [2 * RANK, P], F32, P * 4)
        o_alo = a[0]
        alo = take("alo", [2 * RANK, TOK], F32, TILE)
        tails = at("tails", [P, KT, NTAIL], F32, o_alo)
        o_work = a[0]

        w = [o_work]

        def work(name, shape, dt, size):
            h = at(name, shape, dt, w[0])
            w[0] += -(-size // 32) * 32
            return h

        xbuf = work("xbuf", [P, XW], F32, XW * 4)
        xc = work("xc", [P, TOK], F32, TILE)
        xcs = work("xcs", [P, 2, TOK], F32R, 2 * TILE)
        tr = work("tr", [P, TOK], F32, TILE)
        ti = work("ti", [P, TOK], F32, TILE)
        dec = work("dec", [P, TOK], F32, TILE)
        wt = work("wt", [P, TOK], F32, TILE)
        tz = work("tz", [P, TOK], F32, TILE)
        sz = work("sz", [P, TOK], F32, TILE)
        hh = work("hh", [P, TOK], F32, TILE)
        fix = work("fix", [P, NSEQ], F32, NSEQ * 4)
        graw = work("graw", [P, 2, P], F32, 2 * P * 4)
        ghi = work("ghi", [P, 2, P], F32R, 2 * P * 4)
        glo = work("glo", [P, 2, P], F32R, 2 * P * 4)
        xt = at("xt", [P, TTILES, D], F32, o_work)
        ngb = at("ngb", [P, D], F32, o_work + TTILES * D * 4)
        junk0 = at("junk0", [P, D], F32, o_work + (TTILES + 1) * D * 4)
        rows = at("rows", [NROW, D], F32, o_work + (TTILES + 2) * D * 4)
        act_s = at("act_s", [P, 2, KT, TOK], F32R, o_work)
        w[0] = o_work + 2 * KT * TILE
        trow = at("trow", [NTAIL, D], F32, o_keep)
        araw = work("araw", [P, KT, RANK], F32, KT * RANK * 4)
        aw = work("aw", [P, KT, 2 * RANK], F32R, KT * 2 * RANK * 4)
        assert w[0] <= nc.sbuf_usable_end - base
        w[0] = o_work
        qb = work("qb", [P, TOK], F32, TILE)
        kb = work("kb", [P, TOK], F32, TILE)
        gb = work("gb", [P, TOK], F32, TILE)
        dd = work("dd", [P, TOK], F32, TILE)
        qk = work("qk", [P, 2, TOK], F32, 2 * TILE)
        qks = work("qks", [P, len(SLEVELS), STOK], F32, len(SLEVELS) * STOK * 4)
        vT = work("vT", [P, TOK], F32, TILE)
        vv = work("vv", [P, TTILES, DV], F32, TTILES * DV * 4)
        att = work("att", [P, TTILES, P], F32, TTILES * P * 4)
        kt = work("kt", [P, TOK], F32, TILE)
        kT = work("kT", [P, TTILES, P], F32, TTILES * P * 4)
        st = work("st", [P, NCHUNK, DV], F32, NCHUNK * DV * 4)
        st0 = work("st0", [P, NSEQ, DV], F32, NSEQ * DV * 4)
        dlast = work("dlast", [P, NCHUNK + NSEQ], F32, 64)
        assert w[0] <= nc.sbuf_usable_end - base and o_work + 2 * KT * TILE <= nc.sbuf_usable_end - base
        assert NTAIL * KT * 4 <= TILE
        oo = [gb, kb]
        ring = [dd, kt]
        wos = at("wos", [P, 2, KT, D], F32R, o_xn)
        woraw = at("woraw", [P, D], F32, o_xn + 2 * KT * D * 4)
        mal = at("mal", [P, 2, NTOK], F32, o_glaconst)
        assert o_glaconst + 2 * NTOK * 4 <= o_work
        w[0] = o_work
        ms = work("ms", [P, 2, 2, KT, P], F32R, 4 * KT * P * 4)
        xr = work("xr", [P, 2, D], F32, 2 * D * 4)
        yy = work("yy", [P, 2, D], F32, 2 * D * 4)
        fng = work("fng", [P, D], F32, D * 4)
        junk1 = work("junk1", [P, D], F32, D * 4)

        ps = ctx.enter_context(nc.psum_tensor("ps", [P, 8, 512], F32))
        bankA, bankB = 0, 3
        bankX, bankR = (3, 6), 5

        def slot3(b):
            return ps[:, b:b + PIECES, 0:PIECE]

        def p3(ap):
            return ap.rearrange("p (a b) -> p a b", a=PIECES)

        scratch = nc.dram_tensor("branch_a", (KT, P, TOK), F32, kind="Internal").ap()

        def sem(name):
            return ctx.enter_context(nc.semaphore(name))

        s = {n: sem(n) for n in (
            "rows_in", "ng_in", "ident_ok", "rows_T", "vec_ok", "dvec_ok", "tiny_ok", "masks_ok", "pool_step",
            "x_sq", "x_rms", "x_rstd", "x_scaled", "x_T", "x_hi", "x_lo", "pad_ok", "eps_ok",
            "hi_ok", "lo_ok", "job_done",
            "g_in", "g_hi", "g_lo", "x_evac", "hist_ok", "conv_step", "x_tail", "xc_hi", "xc_lo", "z_tanh", "z_silu", "z_copy",
            "r_done", "i_done", "r_tanh", "i_tanh", "a_ok", "t_ok", "i_x", "a_sq", "w_ok", "m_ok", "u_ok",
            "fix_step", "h_ok", "hz_ok", "h_tail", "tails_T", "tails_ok", "tails_out",
            "act_hi", "act_lo", "dve_passed", "pe_passed", "sp_passed", "act_passed", "ga_first", "ga_tanh", "ma_ok", "ma_out",
            "alo_in", "alo_hi", "alo_lo", "alo_mm", "alo_ok", "wa2_in", "att_zero", "c_full", "c_act", "c_dve",
            "g_abs", "g_exp", "g_ln", "g_ok", "b_ok", "q_ok", "k_ok", "lev_d", "lev_e", "lev_qk", "vT_ok",
            "kt_d", "kt_e", "kt_ok", "qb_e", "qb_ok", "dlast_ok", "st_ok", "ktm_ok", "att_step", "st0_in", "st_out", "st0_out",
            "o_sq", "n_ln", "n_rstd", "zg_tanh", "zg_silu", "o_norm", "og_ok",
            "gb_tanh0", "gb_tanh1", "wo_in", "wo_hi", "wo_lo", "mal_in0", "mal_in1", "yb_part", "merged0", "merged1",
            "fng_in", "m_hi", "m_lo", "y_mm", "y_res", "y_sq", "y_rms", "y_rstd", "y_ok", "y_out0", "y_out1",
        )}
        s_x = [sem(f"x_in{n}") for n in range(4)]
        s_raw = [sem(f"raw_in{n}") for n in range(2)]
        s_xr = [sem(f"xr_in{n}") for n in range(2)]
        gb_tanh = [s["gb_tanh0"], s["gb_tanh1"]]
        mal_in = [s["mal_in0"], s["mal_in1"]]
        merged = [s["merged0"], s["merged1"]]
        y_out = [s["y_out0"], s["y_out1"]]

        STEPS = head_steps()
        NSTEP = len(STEPS)
        INDEX = {name: n for n, (name, _) in enumerate(STEPS)}
        assert NSTEP % 2 == 0
        PER = {e: sum(x == e for _, x in STEPS) for e in ("act", "dve")}

        def bank(name):
            return 6 + INDEX[name] % 2

        def full_at(h, name):
            return h * NSTEP + (ONE + INDEX[name] + 1)

        def drained_at(h, n):
            if n < 0:
                assert STEPS[-1][1] == STEPS[n][1]
                return s["c_" + STEPS[-1][1]], h * PER[STEPS[-1][1]] + ONE
            engine = STEPS[n][1]
            count = sum(x == engine for _, x in STEPS[:n + 1])
            return s["c_" + engine], h * PER[engine] + (ONE + count)

        def emptied(h, name):
            return drained_at(h, INDEX[name])

        w_in = t["w_in"][0].rearrange("(k p) n -> p k n", p=P)
        w_lo_v = t["w_lru_o"][0].rearrange("(k p) n -> p k n", p=P)
        w_go_v = t["w_gla_o"][0].rearrange("(k p) n -> p k n", p=P)
        x_rows = [(t["x_prompt"][0], n * P, P) for n in range(NCHUNK)] + [(t["x_sample"].rearrange("a b d -> (a b) d"), 0, STOK)]

        def half(ap, m, which):
            return ap.rearrange("p (n h m) -> p n h m", h=2, m=m)[:, :, which, :]

        y_rows = [(out[0][0], n * P, P) for n in range(NCHUNK)] + [(out[1].rearrange("a b d -> (a b) d"), 0, STOK)]

        def store_y(sp, n):
            dst, r0, nr = y_rows[n]
            sp.wait_ge(s["y_ok"], n + 1)
            sp.dma_start(dst[r0:r0 + nr, :], yy[0:nr, n % 2, :]).then_inc(y_out[n % 2], 16)

        block = ctx.enter_context(nc.Block())

        @block.sync
        def _(sp):
            def row(r, ap):
                sp.dma_start(rows[r:r + ap.shape[0], 0:ap.shape[1]], ap).then_inc(s["rows_in"], 16)

            def load_x(n):
                src, r0, nr = x_rows[n]
                sp.dma_start(xt[0:nr, n, :], src[r0:r0 + nr, :]).then_inc(s_x[n % 4], 16)

            load_x(0)
            load_x(1)
            load_x(2)
            sp.dma_start(raw[:, 0], w_in[:, :, COL_X:COL_X + P]).then_inc(s_raw[0], 16)
            load_x(3)
            sp.wait_ge(s["pad_ok"], 1)
            row(R_CONVW, t["conv_w"][0])
            for r, name in ((R_CONVB, "conv_b"), (R_BR, "b_r"), (R_BI, "b_i"), (R_LAM, "lam"), (R_GN, "gla_norm_g"), (R_BA, "b_a")):
                row(r, t[name])
            row(R_BM, t["b_merge"].rearrange("o (r d) -> (o r) d", r=2))
            row(R_H0, t["state_lru_h"][0])
            row(R_CS, t["state_lru_conv"][0].rearrange("b k w -> (b k) w"))
            for n in range(4, TTILES):
                sp.wait_ge(s["x_sq"], n - 3)
                load_x(n)
            sp.dma_start(raw[:, 1], w_in[:, :, COL_Z:COL_Z + P]).then_inc(s_raw[1], 16)

            def load(n, slot, src):
                sp.wait_ge(s["lo_ok"], n - 1)
                sp.sem_inc(s["sp_passed"], 1)
                sp.dma_start(raw[:, slot], src).then_inc(s_raw[slot], 16)

            def load_gates(i):
                sp.dma_start(graw[:, 0], t["w_r"][0][i]).then_inc(s["g_in"], 16)
                sp.dma_start(graw[:, 1], t["w_i"][0][i]).then_inc(s["g_in"], 16)

            sp.wait_ge(s["x_T"], TTILES)
            load_gates(0)
            with sp.Fori(1, KT) as i:
                load(2 * i, 0, w_in[:, :, bass.ds(i * P + COL_X, P)])
                load(2 * i + 1, 1, w_in[:, :, bass.ds(i * P + COL_Z, P)])
                sp.wait_ge(s["g_lo"], i)
                load_gates(i)
            load(N_MIXA, 0, w_in[:, :, COL_GA:COL_GA + P])
            with sp.Fori(0, KT - 1) as i:
                load(2 * i + N_MIXA + 1, 1, w_in[:, :, bass.ds(i * P + (COL_GA + P), P)])
                load(2 * i + N_MIXA + 2, 0, w_lo_v[:, :, bass.ds(i * P, P)])
            load(N_MIXA + 2 * KT - 1, 1, w_lo_v[:, :, (KT - 1) * P:D])
            sp.dma_start(araw[:, :, :], w_in[:, :, COL_A:COL_A + RANK]).then_inc(s["alo_in"], 16)
            with sp.Fori(0, HEADS) as h:
                for j, (col, step) in enumerate(((COL_Q, P), (COL_K, P), (COL_V, DV), (COL_V + P, DV), (COL_ZG, DV), (COL_ZG + P, DV))):
                    load(6 * h + (N_GLA + j), (N_GLA + j) % 2, w_in[:, :, bass.ds(h * step + col, P)])
            with sp.Fori(0, KT // 2) as i:
                for j in range(2):
                    load(2 * i + (N_GB + j), (N_GB + j) % 2, w_in[:, :, bass.ds(i * 2 * P + (COL_GB + j * P), P)])
            sp.wait_ge(s["ma_out"], 16 * KT)
            with sp.Fori(0, KT // 2) as i:
                for j in range(2):
                    load(2 * i + (N_YB + j), (N_YB + j) % 2, w_go_v[:, :, bass.ds(i * 2 * P + j * P, P)])
                    sp.wait_ge(s["job_done"], N_YB)
                    sp.wait_ge(s["wo_lo"], ONE + 2 * i + j)
                    sp.dma_start(woraw[:, :], t["w_out"][0][bass.ds(i * 2 * P + j * P, P), :]).then_inc(s["wo_in"], 16)
                    sp.wait_ge(merged[j], i + ONE)
                    sp.dma_start(mal[:, j, :], scratch[2 * i + j][:, 0:NTOK]).then_inc(mal_in[j], 16)
            sp.wait_ge(s["job_done"], N_YB + KT)
            sp.dma_start(fng[:, :], t["final_norm_g"].rearrange("(o d) -> o d", o=1).to_broadcast([P, D])).then_inc(s["fng_in"], 16)
            for n in range(TTILES):
                if n >= 2:
                    sp.wait_ge(s["y_res"], n - 1)
                src, r0, nr = x_rows[n]
                sp.dma_start(xr[0:nr, n % 2, :], src[r0:r0 + nr, :]).then_inc(s_xr[n % 2], 16)
                if n >= 1:
                    store_y(sp, n - 1)
            store_y(sp, TTILES - 1)
            for sm, v in ((y_out[0], 16 * 5), (y_out[1], 16 * 4), (s["tails_out"], 64), (s["st_out"], ONE + 16 * HEADS),
                          (s["st0_out"], ONE + 16 * HEADS), (s["ma_out"], 16 * KT)):
                sp.wait_ge(sm, v)


        @block.gpsimd
        def _(pool):
            n = [0]

            def step(ins):
                n[0] += 1
                ins.then_inc(s["pool_step"], 1)
                pool.wait_ge(s["pool_step"], n[0])

            for name in STARTS_AT_ONE:
                pool.sem_inc(s[name], 1)
            step(pool.memset(ident[:, :], 0.0))
            pool.affine_select(out=ident[:, :], in_=ident[:, :], compare_op=ALU.not_equal, fill=1.0, base=0,
                               pattern=[[-1, P]], channel_multiplier=1).then_inc(s["ident_ok"], 1)
            for l, m in enumerate(LEVELS):
                mask = lmask[:, l, :]
                step(pool.memset(mask, 1.0))
                step(pool.affine_select(out=mask, in_=mask, compare_op=ALU.is_ge, fill=0.0, base=0,
                                        pattern=[[-2 * m, 64 // m], [0, m]], channel_multiplier=1))
                step(pool.affine_select(out=mask, in_=mask, compare_op=ALU.is_ge, fill=0.0, base=m - 1,
                                        pattern=[[2 * m, 64 // m], [0, m]], channel_multiplier=-1))
            step(pool.memset(smask[:, :], 1.0))
            step(pool.affine_select(out=smask[:, :], in_=smask[:, :], compare_op=ALU.is_ge, fill=0.0, base=0,
                                    pattern=[[-SLEN, NSEQ]], channel_multiplier=1))
            step(pool.affine_select(out=smask[:, :], in_=smask[:, :], compare_op=ALU.is_ge, fill=0.0, base=SLEN - 1,
                                    pattern=[[SLEN, NSEQ]], channel_multiplier=-1))
            step(pool.memset(ones[:, :], 1.0 / DV))
            step(pool.memset(notfirst[:, :], 1.0))
            step(pool.memset(notfirst[:, 0:SEQ].rearrange("p (n c) -> p n c", c=CHUNK)[:, :, 0:1], 0.0))
            step(pool.memset(notfirst[:, SEQ:NTOK].rearrange("p (n c) -> p n c", c=SLEN)[:, :, 0:1], 0.0))
            pool.memset(notfirst[:, NTOK:TOK], 0.0).then_inc(s["masks_ok"], 1)

            def lo(i, c):
                pool.wait_ge(s["hi_ok"], 2 * i + (c + 1))
                pool.tensor_tensor(wlo[:, c % 2], raw[:, c % 2], whi[:, c % 2].bitcast(F32), ALU.subtract).then_inc(s["lo_ok"], 1)

            with pool.Fori(0, (N_YB + KT) // 2) as i:
                lo(i, 0)
                lo(i, 1)

        @block.tensor
        def _(pe):
            def split_product(dst, wh, wl, mh, ml, first, last):
                pe.matmul(dst, wh, mh, start=first, stop=False)
                pe.matmul(dst, wh, ml, start=False, stop=False)
                return pe.matmul(dst, wl, mh, start=False, stop=last)

            def piece(c, b, mov, j):
                for k in range(KT):
                    cols = slice(j * PIECE, (j + 1) * PIECE)
                    ins = split_product(ps[:, b + j, 0:PIECE], whi[:, c % 2, k, :], wlo[:, c % 2, k, :],
                                        mov[:, 0, k, cols], mov[:, 1, k, cols], k == 0, k == KT - 1)
                return ins

            def job(i, c, b, mov):
                pe.wait_ge(s["lo_ok"], 2 * i + (c + 1))
                for j in range(PIECES):
                    ins = piece(c, b, mov, j)
                ins.then_inc(s["job_done"], 1)

            def x_transpose(n):
                nr = x_rows[n][2]
                b = bankX[n % 2]
                pe.wait_ge(s["x_scaled"], n + 1)
                if n >= 2:
                    pe.wait_ge(s["x_lo"], n - 1)
                for k in range(KT):
                    ins = pe.transpose(ps[:, b + k // 4, (k % 4) * P:(k % 4) * P + nr], xt[0:nr, n, k * P:(k + 1) * P],
                                       ident[0:nr, 0:nr])
                ins.then_inc(s["x_T"], 1)

            pe.wait_ge(s["ident_ok"], 1)
            for n in range(4):
                x_transpose(n)
            pe.wait_ge(s["rows_in"], 16 * 10)
            for k in range(KT):
                ins = pe.transpose(ps[:, bankR, k * NROW:(k + 1) * NROW], rows[:, k * P:(k + 1) * P], ident[0:NROW, 0:NROW])
            ins.then_inc(s["rows_T"], 1)
            x_transpose(4)
            pe.wait_ge(s["lo_ok"], 1)
            piece(0, bankA, xn, 0)
            x_transpose(5)
            x_transpose(6)
            pe.wait_ge(s["x_lo"], 6)
            piece(0, bankA, xn, 1)
            x_transpose(7)
            x_transpose(8)
            pe.wait_ge(s["x_lo"], TTILES)
            pe.wait_ge(s["pad_ok"], 2)
            piece(0, bankA, xn, 2).then_inc(s["job_done"], 1)
            pe.wait_ge(s["vec_ok"], 1)

            def z_and_gates(i):
                pe.wait_ge(s["i_tanh"], i + ONE)
                job(i, N_LRU + 1, bankB, xn)
                pe.wait_ge(s["xc_lo"], i + 1)
                pe.wait_ge(s["g_lo"], i + 1)
                for g, b in ((0, bankA), (1, bankB)):
                    if g == 1:
                        pe.wait_ge(s["z_copy"], i + 1)
                    for j in range(PIECES):
                        cols = slice(j * PIECE, (j + 1) * PIECE)
                        ins = split_product(ps[:, b + j, 0:PIECE], ghi[:, g, :], glo[:, g, :], xcs[:, 0, cols], xcs[:, 1, cols],
                                            True, True)
                    ins.then_inc(s["r_done"] if g == 0 else s["i_done"], 1)

            with pe.Fori(0, KT - 1) as i:
                z_and_gates(i)
                pe.wait_ge(s["r_tanh"], i + (ONE + 1))
                job(i, N_LRU + 2, bankA, xn)
            z_and_gates(KT - 1)

            pe.wait_ge(s["r_tanh"], ONE + KT)
            job(0, N_MIXA, bankA, xn)
            pe.wait_ge(s["i_tanh"], ONE + KT)
            with pe.Fori(0, KT - 1) as i:
                pe.wait_ge(s["ga_tanh"], i + ONE)
                job(i, N_MIXA + 1, bankB, xn)
                pe.wait_ge(s["act_lo"], KT)
                pe.wait_ge(s["ga_first"], 1)
                pe.wait_ge(s["ma_ok"], i + ONE)
                job(i, N_MIXA + 2, bankA, act_s)
            pe.wait_ge(s["ga_tanh"], KT - 1 + ONE)
            job(0, N_MIXA + 2 * KT - 1, bankB, act_s)
            pe.wait_ge(s["h_tail"], KT)
            pe.wait_ge(s["vec_ok"], 1)
            for k in range(KT):
                ins = pe.transpose(ps[0:NTAIL, 6 + k // 4, (k % 4) * P:(k % 4 + 1) * P], tails[:, k, :], ident[:, :])
            ins.then_inc(s["tails_T"], 1)

            pe.wait_ge(s["alo_lo"], 1)
            pe.wait_ge(s["ma_ok"], KT - 1 + ONE)
            for j in range(PIECES):
                for k in range(KT):
                    for r in range(2):
                        ins = pe.matmul(ps[0:2 * RANK, bankA + j, 0:PIECE], aw[:, k, :], xn[:, r, k, j * PIECE:(j + 1) * PIECE],
                                        start=(k == 0 and r == 0), stop=(k == KT - 1 and r == 1))
            ins.then_inc(s["alo_mm"], 1)
            pe.wait_ge(s["masks_ok"], 1)
            pe.wait_ge(s["alo_ok"], 1)
            pe.wait_ge(s["tails_ok"], 2)
            pe.wait_ge(s["ma_ok"], KT + ONE)
            with pe.Fori(0, HEADS) as h:
                def c_step(name, emit):
                    pe.wait_ge(*drained_at(h, INDEX[name] - 2))
                    emit(bank(name)).then_inc(s["c_full"], 1)

                def gate(j):
                    def emit(b):
                        return pe.matmul(ps[:, b, 0:PIECE], wa2[:, :], alo[:, j * PIECE:(j + 1) * PIECE], start=True, stop=True)
                    c_step(f"g{j}", emit)

                def diagonal(n):
                    def emit(b):
                        for c in range(4):
                            cols = slice((4 * n + c) * P, (4 * n + c + 1) * P)
                            ins = pe.matmul(ps[:, b, c * P:(c + 1) * P], kb[:, cols], qb[:, cols], start=True, stop=True)
                        return ins
                    c_step(f"dg{n}", emit)

                def level(l):
                    pe.wait_ge(s["lev_qk"], h * len(LEVELS) + (l + 1))

                    def emit(b):
                        for c in range(NCHUNK):
                            tile = qk[:, l % 2, c * P:(c + 1) * P]
                            ins = pe.matmul(ps[:, b, c * 64:(c + 1) * 64], tile, half(tile, LEVELS[l], 1), start=True, stop=True)
                        return ins
                    c_step(f"L{l}", emit)

                def sample_levels(b):
                    for l, m in enumerate(SLEVELS):
                        pe.matmul(ps[0:STOK, b, 32 * l:32 * l + 32], qks[:, l, :], half(qks[:, l, :], m, 1), start=True, stop=True)
                    return pe.matmul(ps[0:STOK, b, 128:128 + STOK], kb[:, SEQ:NTOK], qb[:, SEQ:NTOK], start=True, stop=True)

                def transposes(prefix, src):
                    for g, name in enumerate("abc"):
                        def emit(b):
                            if g == 2:
                                pe.sem_inc(s["pe_passed"], 1)
                            for n in range(4 * g, min(4 * g + 4, TTILES)):
                                nr = P if n < NCHUNK else STOK
                                ins = pe.transpose(ps[0:nr, b, (n % 4) * P:(n % 4 + 1) * P], src[:, n * P:n * P + nr], ident[:, :])
                            return ins
                        c_step(prefix + name, emit)

                def outer(n):
                    def emit(b):
                        for c in range(2):
                            ins = pe.matmul(ps[:, b, c * DV:(c + 1) * DV], kT[:, 2 * n + c, :], vv[:, 2 * n + c, :], start=True, stop=True)
                        return ins
                    c_step(f"KV{n}", emit)

                def output(g, d):
                    def emit(b):
                        for c in range(4 * g, 4 * g + 4):
                            dst = ps[:, b, (c % 4) * P:(c % 4 + 1) * P]
                            ins = pe.matmul(dst, vv[:, c, d * P:(d + 1) * P], att[:, c, :], start=True, stop=(c == 0))
                            if c > 0:
                                ins = pe.matmul(dst, st[:, c - 1, d * P:(d + 1) * P], qb[:, c * P:(c + 1) * P], start=False, stop=True)
                        return ins
                    c_step(f"O{g}{d}", emit)

                def sample_output(b):
                    for d in range(VH):
                        lo = d * STOK
                        pe.matmul(ps[:, b, lo:lo + STOK], vv[0:STOK, NCHUNK, d * P:(d + 1) * P], att[0:STOK, NCHUNK, 0:STOK],
                                  start=True, stop=False, skip_group_check=True)
                        for q in range(NSEQ):
                            ins = pe.matmul(ps[:, b, lo + q * SLEN:lo + (q + 1) * SLEN], st0[:, q, d * P:(d + 1) * P],
                                            qb[:, SEQ + q * SLEN:SEQ + (q + 1) * SLEN], start=False, stop=(q == NSEQ - 1),
                                            skip_group_check=True)
                    return ins

                def sample_outer(n):
                    def emit(b):
                        for c in range(2):
                            ins = pe.matmul(ps[:, b, c * DV:(c + 1) * DV], kt[0:STOK, (2 * n + c) * P:(2 * n + c + 1) * P],
                                            vv[0:STOK, NCHUNK, :], start=True, stop=True)
                        return ins
                    c_step(f"sKV{n}", emit)

                def mean_square(j):
                    def emit(b):
                        for d in range(VH):
                            ins = pe.matmul(ps[:, b, 0:PIECE], ones[:, :], qk[:, d, j * PIECE:(j + 1) * PIECE], start=(d == 0), stop=(d == 1))
                        return ins
                    c_step(f"nrm{j}", emit)

                def start_job(c):
                    pe.wait_ge(s["lo_ok"], 6 * h + (N_GLA + c + 1))

                def part(c, b, j):
                    ins = piece(N_GLA + c, b, xn, j)
                    if j == PIECES - 1:
                        ins.then_inc(s["job_done"], 1)

                start_job(0)
                pe.wait_ge(s["zg_silu"], ONE + 2 * h)
                for j in range(PIECES):
                    part(0, bankA, j)
                pe.wait_ge(s["wa2_in"], 32 * (h + 1))
                gate(0)
                gate(1)
                start_job(1)
                part(1, bankB, 0)
                gate(2)
                part(1, bankB, 1)
                part(1, bankB, 2)
                start_job(2)
                pe.wait_ge(s["q_ok"], h + 1)
                part(2, bankA, 0)
                pe.wait_ge(s["k_ok"], h + 1)
                diagonal(0)
                diagonal(1)
                part(2, bankA, 1)
                level(0)
                part(2, bankA, 2)
                level(1)
                start_job(3)
                part(3, bankB, 0)
                level(2)
                pe.wait_ge(s["vT_ok"], 2 * h + 1)
                transposes("vt0", vT)
                part(3, bankB, 1)
                level(3)
                part(3, bankB, 2)
                level(4)
                start_job(4)
                part(4, bankA, 0)
                level(5)
                part(4, bankA, 1)
                level(6)
                pe.wait_ge(s["vT_ok"], 2 * h + 2)
                transposes("vt1", vT)
                part(4, bankA, 2)
                c_step("smp", sample_levels)
                pe.wait_ge(s["kt_ok"], h + 1)
                transposes("kT", kt)
                start_job(5)
                part(5, bankB, 0)
                pe.wait_ge(*emptied(h, "kTc"))
                for n in range(NCHUNK // 2):
                    outer(n)
                part(5, bankB, 1)
                pe.wait_ge(s["qb_ok"], h + 1)
                pe.wait_ge(*emptied(h, "KV3"))
                for g in range(2):
                    for d in range(VH):
                        output(g, d)
                pe.wait_ge(s["st0_in"], 16 * (h + 1))
                c_step("Os", sample_output)
                part(5, bankB, 2)
                pe.wait_ge(s["ktm_ok"], h + 1)
                for n in range(NSEQ // 2):
                    sample_outer(n)
                pe.wait_ge(s["o_sq"], 2 * (h + 1))
                for j in range(PIECES):
                    mean_square(j)

            pe.wait_ge(s["zg_silu"], ONE + 2 * HEADS)
            with pe.Fori(0, KT // 2) as i:
                for j, b in ((0, bankA), (1, bankB)):
                    pe.wait_ge(gb_tanh[j], i + ONE)
                    job(i, N_GB + j, b, xn)
            pe.wait_ge(s["act_lo"], 2 * KT)
            pe.wait_ge(gb_tanh[0], ONE + KT // 2)
            pe.wait_ge(gb_tanh[1], ONE + KT // 2)
            with pe.Fori(0, KT // 2) as i:
                for j, b in ((0, bankA), (1, bankB)):
                    pe.wait_ge(merged[j], i + ONE)
                    job(i, N_YB + j, b, act_s)
            pe.wait_ge(s["wo_lo"], ONE + KT)
            pe.wait_ge(merged[0], ONE + KT // 2)
            pe.wait_ge(merged[1], ONE + KT // 2)

            def out_tile(n, slot):
                pe.wait_ge(s["m_lo"], n + 1)
                b = (bankA, bankB)[slot]
                for e in range(2):
                    for k in range(KT):
                        ins = split_product(ps[:, b + e, :], ms[:, slot, 0, k, :], ms[:, slot, 1, k, :],
                                            wos[:, 0, k, e * 512:(e + 1) * 512], wos[:, 1, k, e * 512:(e + 1) * 512],
                                            k == 0, k == KT - 1)
                ins.then_inc(s["y_mm"], 1)

            out_tile(0, 0)
            out_tile(1, 1)
            with pe.Fori(1, NCHUNK // 2) as i:
                for slot in range(2):
                    pe.wait_ge(s["y_res"], 2 * i + (slot - 1))
                    out_tile(2 * i + slot, slot)
            pe.wait_ge(s["y_res"], NCHUNK - 1)
            out_tile(NCHUNK, 0)

        @block.scalar
        def _(act):
            def hi(i, c):
                act.wait_ge(s_raw[c % 2], 16 * i + 16 * (c // 2 + 1))
                if not isinstance(i, int) or c >= 2:
                    act.wait_ge(s["job_done"], 2 * i + (c - 1))
                act.activation(whi[:, c % 2], raw[:, c % 2], ACT.Copy).then_inc(s["hi_ok"], 1)

            act.dma_start(ngb[:, :], t["norm_g"][0:1, :].to_broadcast([P, D])).then_inc(s["ng_in"], 16)
            act.wait_ge(s["eps_ok"], 1)
            act.activation(rstd[:, 31:32], ssum[:, 31:32], ACT.Sqrt)

            def x_rms(n):
                nr = x_rows[n][2]
                act.wait_ge(s_x[n % 4], 16 * (n // 4 + 1))
                act.activation(junk0[0:nr, :], xt[0:nr, n, :], ACT.Square, accum_out=ssum[0:nr, n:n + 1]).then_inc(s["x_sq"], 1)
                act.wait_ge(s["x_sq"], n + 1)
                act.wait_ge(s["eps_ok"], 1)
                act.activation(rstd[0:nr, n:n + 1], ssum[0:nr, n:n + 1], ACT.Sqrt, scale=1.0 / D, bias=ssum[0:nr, 31:32]).then_inc(s["x_rms"], 1)

            def x_hi(n):
                nr = x_rows[n][2]
                b = bankX[n % 2]
                act.wait_ge(s["x_T"], n + 1)
                act.activation(xn[:, 0, :, n * P:n * P + nr], ps[:, b:b + 2, :].rearrange("p a (c n) -> p (a c) n", n=P)[:, :, 0:nr],
                               ACT.Copy).then_inc(s["x_hi"], 1)

            x_rms(0)
            x_rms(1)
            for n in range(TTILES):
                x_hi(n)
                if n + 2 < TTILES:
                    x_rms(n + 2)
                if n == 1:
                    hi(0, 0)
            hi(0, 1)
            act.wait_ge(s["vec_ok"], 1)
            act.activation(tiny[:, 0, :], vec[:, :, R_LAM], ACT.Abs).then_inc(s["tiny_ok"], 1)
            act.wait_ge(s["tiny_ok"], 1)
            act.activation(tiny[:, 0, :], tiny[:, 0, :], ACT.Exp, scale=-1.0).then_inc(s["tiny_ok"], 1)
            act.wait_ge(s["x_T"], TTILES)
            act.wait_ge(s["x_lo"], TTILES)

            act.wait_ge(s["dvec_ok"], 1)
            with act.Fori(0, KT) as i:
                act.wait_ge(s["job_done"], 2 * i + 1)
                act.wait_ge(s["x_tail"], i + ONE)
                act.activation(xbuf[:, HIST:HIST + 2 * PIECE].rearrange("p (a b) -> p a b", a=2), ps[:, bankA:bankA + 2, 0:PIECE], ACT.Copy)
                act.activation(xbuf[:, HIST + 2 * PIECE:XS], ps[:, bankA + 2, 0:SEQ - 2 * PIECE], ACT.Copy)
                act.activation(xbuf[:, XS:XW].rearrange("p (q n) -> p q n", q=NSEQ)[:, :, HIST:HIST + SLEN],
                               ps[:, bankA + 2, SEQ - 2 * PIECE:NTOK - 2 * PIECE].rearrange("p (q n) -> p q n", q=NSEQ),
                               ACT.Copy).then_inc(s["x_evac"], 1)
                hi(i, 2)
                act.wait_ge(s["g_in"], 32 * (i + 1))
                act.wait_ge(s["i_done"], i + ONE)
                act.activation(ghi[:, :, :], graw[:, :, :], ACT.Copy).then_inc(s["g_hi"], 1)
                act.wait_ge(s["conv_step"], 8 * (i + 1))
                act.activation(xcs[:, 0, :], xc[:, :], ACT.Copy).then_inc(s["xc_hi"], 1)
                hi(i, 3)
                act.wait_ge(s["r_done"], i + 1)
                act.activation(p3(tr[:, :]), slot3(bankA), ACT.Tanh, scale=0.5, bias=dvec[:, i, V_BR:V_BR + 1]).then_inc(s["r_tanh"], 1)
                act.wait_ge(s["i_done"], ONE + i + 1)
                act.wait_ge(s["hz_ok"], i + ONE)
                act.activation(p3(ti[:, :]), slot3(bankB), ACT.Tanh, scale=0.5, bias=dvec[:, i, V_BI:V_BI + 1]).then_inc(s["i_tanh"], 1)
                act.wait_ge(s["z_copy"], i + 1)
                act.activation(tz[:, :], sz[:, :], ACT.Tanh, scale=0.5).then_inc(s["z_tanh"], 1)
                act.wait_ge(s["r_tanh"], ONE + i + 1)
                act.activation(dec[:, :], tr[:, :], ACT.Exp, scale=dvec[:, i, V_NC:V_NC + 1], bias=dvec[:, i, V_NC:V_NC + 1]).then_inc(s["a_ok"], 1)
                act.activation(wt[:, :], tr[:, :], ACT.Tanh, scale=dvec[:, i, V_C:V_C + 1], bias=dvec[:, i, V_C:V_C + 1]).then_inc(s["t_ok"], 1)
                act.wait_ge(s["w_ok"], i + 1)
                act.activation(wt[:, :], wt[:, :], ACT.Sqrt, scale=0.25).then_inc(s["m_ok"], 1)

            act.wait_ge(s["hz_ok"], ONE + KT)
            act.wait_ge(s["x_tail"], ONE + KT)
            with act.Fori(0, KT) as i:
                act.activation(act_s[:, 0, i, :], keep[:, i, :], ACT.Copy).then_inc(s["act_hi"], 1)
            act.wait_ge(s["job_done"], N_MIXA + 1)
            act.wait_ge(s["act_lo"], 1)
            act.activation(p3(keep[:, 0, :]), slot3(bankA), ACT.Tanh, scale=0.5, bias=dvec[:, 0, V_BMA:V_BMA + 1]).then_inc(s["ga_first"], 1)
            hi(0, N_MIXA + 2)
            act.wait_ge(s["act_lo"], KT)
            with act.Fori(0, KT - 1) as i:
                act.wait_ge(s["job_done"], 2 * i + (N_MIXA + 2))
                act.sem_inc(s["act_passed"], 1)
                act.activation(p3(keep[:, i + 1, :]), slot3(bankB), ACT.Tanh, scale=0.5, bias=dvec[:, i + 1, V_BMA:V_BMA + 1]).then_inc(s["ga_tanh"], 1)
                hi(i, N_MIXA + 3)
                act.wait_ge(s["job_done"], 2 * i + (N_MIXA + 3))
                hi(i, N_MIXA + 4)
                act.wait_ge(s["ma_ok"], i + (ONE + 1))
                act.dma_start(scratch[i], keep[:, i, :]).then_inc(s["ma_out"], 16)
            hi(0, N_MIXA + 2 * KT + 1)
            act.wait_ge(s["ma_ok"], KT + ONE)
            act.dma_start(scratch[KT - 1], keep[:, KT - 1, :]).then_inc(s["ma_out"], 16)
            act.wait_ge(s["alo_in"], 16)
            act.activation(aw[:, :, 0:RANK], araw[:, :, :], ACT.Copy).then_inc(s["alo_hi"], 1)
            act.wait_ge(s["tails_T"], 1)
            act.wait_ge(s["ma_out"], 16 * KT)
            for n in range(2):
                act.activation(trow[:, n * 512:(n + 1) * 512], ps[0:NTAIL, 6 + n, :], ACT.Copy).then_inc(s["tails_ok"], 1)
            act.wait_ge(s["tails_ok"], 2)
            for dst, r0, nr in ((out[2][0], 0, 1), (out[5][0], 1, NSEQ), (out[3][0, 0], T_C, HIST),
                                (out[6][0].rearrange("b k w -> (b k) w"), T_C + HIST, NSEQ * HIST)):
                act.dma_start(dst, trow[r0:r0 + nr, :]).then_inc(s["tails_out"], 16)
            act.wait_ge(s["alo_mm"], 1)
            act.activation(alo[:, :].rearrange("p (a b) -> p a b", a=PIECES), ps[0:2 * RANK, bankA:bankA + PIECES, 0:PIECE],
                           ACT.Copy).then_inc(s["alo_ok"], 1)

            with act.Fori(0, HEADS) as h:
                def job_at(c):
                    act.wait_ge(s["job_done"], 6 * h + (N_GLA + c + 1))

                def full(name):
                    act.wait_ge(s["c_full"], full_at(h, name))

                def token_tiles(prefix, dst):
                    for g, name in enumerate("abc"):
                        full(prefix + name)
                        if g < 2:
                            act.activation(dst(4 * g, 4, P), ps[:, bank(prefix + name), :].rearrange("p (c n) -> p c n", n=P),
                                           ACT.Copy).then_inc(s["c_act"], 1)
                        else:
                            act.activation(dst(8, 1, STOK), ps[0:STOK, bank(prefix + name), 0:P].rearrange("p (c n) -> p c n", n=P),
                                           ACT.Copy).then_inc(s["c_act"], 1)

                def level_exp(l):
                    m = LEVELS[l]
                    n = SEQ if m > SLEVELS[0] else NTOK
                    act.wait_ge(s["lev_d"], h * len(LEVELS) + (l + 1))
                    for which, sign in ((0, -1.0), (1, 1.0)):
                        v = half(ring[l % 2][:, 0:n], m, which)
                        ins = act.activation(v, v, ACT.Exp, scale=sign / GATE_NORM)
                    ins.then_inc(s["lev_e"], 1)

                for r in range(2):
                    act.dma_start(wa2[r * RANK:(r + 1) * RANK, :], t["w_a2"][0][:, bass.ds(h * P, P)]).then_inc(s["wa2_in"], 16)
                job_at(0)
                act.activation(p3(qb[:, :]), slot3(bankA), ACT.Copy, scale=float(DK) ** -0.5).then_inc(s["q_ok"], 1)
                hi(3 * h, N_GLA + 2)
                act.wait_ge(s["st0_out"], ONE + 16 * h)
                act.dma_start(st0[:, :, :], t["state_gla"][0].rearrange("b h p v -> h p b v")[h]).then_inc(s["st0_in"], 16)
                act.wait_ge(s["og_ok"], ONE + 2 * h)
                for j in range(PIECES):
                    full(f"g{j}")
                    act.sem_inc(s["act_passed"], 1)
                    act.activation(gb[:, j * PIECE:(j + 1) * PIECE], ps[:, bank(f"g{j}"), 0:PIECE], ACT.Identity,
                                   bias=vec[:, h, R_BA:R_BA + 1]).then_inc(s["c_act"], 1)
                act.wait_ge(*emptied(h, "g2"))
                act.activation(dd[:, :], gb[:, :], ACT.Abs).then_inc(s["g_abs"], 1)
                act.wait_ge(s["g_abs"], h + 1)
                act.activation(dd[:, :], dd[:, :], ACT.Exp, scale=-1.0).then_inc(s["g_exp"], 1)
                act.wait_ge(s["g_exp"], h + 1)
                act.activation(dd[:, :], dd[:, :], ACT.Ln, bias=1.0).then_inc(s["g_ln"], 1)
                job_at(1)
                act.activation(p3(kb[:, :]), slot3(bankB), ACT.Copy).then_inc(s["k_ok"], 1)
                hi(3 * h, N_GLA + 3)
                level_exp(0)
                level_exp(1)
                level_exp(2)
                job_at(2)
                act.activation(p3(vT[:, :]), slot3(bankA), ACT.Copy).then_inc(s["vT_ok"], 1)
                hi(3 * h, N_GLA + 4)
                level_exp(3)
                token_tiles("vt0", lambda c, n, nr: vv[0:nr, c:c + n, 0:P])
                level_exp(4)
                job_at(3)
                act.activation(p3(vT[:, :]), slot3(bankB), ACT.Copy).then_inc(s["vT_ok"], 1)
                hi(3 * h, N_GLA + 5)
                level_exp(5)
                level_exp(6)
                token_tiles("vt1", lambda c, n, nr: vv[0:nr, c:c + n, P:DV])
                act.activation(dlast[:, 0:NCHUNK], gb[:, CHUNK - 1:SEQ:CHUNK], ACT.Exp, scale=1.0 / GATE_NORM)
                act.activation(dlast[:, NCHUNK:NCHUNK + NSEQ], gb[:, SEQ + SLEN - 1:NTOK:SLEN], ACT.Exp, scale=1.0 / GATE_NORM).then_inc(s["dlast_ok"], 1)
                act.wait_ge(s["kt_d"], h + 1)
                act.activation(kt[:, 0:NTOK], kt[:, 0:NTOK], ACT.Exp, scale=1.0 / GATE_NORM).then_inc(s["kt_e"], 1)
                act.wait_ge(s["lev_qk"], len(LEVELS) * (h + 1))
                act.activation(dd[:, :], gb[:, :], ACT.Exp, scale=1.0 / GATE_NORM).then_inc(s["qb_e"], 1)
                job_at(4)
                act.activation(p3(vT[:, :]), slot3(bankA), ACT.Tanh, scale=0.5).then_inc(s["zg_tanh"], 1)
                hi(3 * h, N_GLA + 6)
                token_tiles("kT", lambda c, n, nr: kT[0:nr, c:c + n, :])
                for g in range(2):
                    for d in range(VH):
                        full(f"O{g}{d}")
                        act.activation(oo[d][:, g * 512:(g + 1) * 512], ps[:, bank(f"O{g}{d}"), :], ACT.Copy).then_inc(s["c_act"], 1)
                full("Os")
                act.activation(oo[0][:, SEQ:NTOK], ps[:, bank("Os"), 0:STOK], ACT.Copy)
                act.activation(oo[1][:, SEQ:NTOK], ps[:, bank("Os"), STOK:2 * STOK], ACT.Copy).then_inc(s["c_act"], 1)
                act.wait_ge(*emptied(h, "Os"))
                for d in range(VH):
                    act.activation(qk[:, d, :], oo[d][:, :], ACT.Square).then_inc(s["o_sq"], 1)
                job_at(5)
                act.wait_ge(s["zg_silu"], ONE + 2 * h + 1)
                act.activation(p3(vT[:, :]), slot3(bankB), ACT.Tanh, scale=0.5).then_inc(s["zg_tanh"], 1)
                hi(3 * h, N_GLA + 7)
                for j in range(PIECES):
                    full(f"nrm{j}")
                    act.activation(kt[:, j * PIECE:(j + 1) * PIECE], ps[:, bank(f"nrm{j}"), 0:PIECE], ACT.Ln,
                                   bias=ssum[:, 31:32]).then_inc(s["c_act"], 1)
                act.wait_ge(*emptied(h, "nrm2"))
                act.activation(kt[:, :], kt[:, :], ACT.Exp, scale=-0.5).then_inc(s["n_rstd"], 1)
                act.wait_ge(*emptied(h, "KV3"))
                act.dma_start(out[4][0, 0][h], st[:, NCHUNK - 1, :]).then_inc(s["st_out"], 16)
                act.wait_ge(*emptied(h, "sKV3"))
                act.dma_start(out[7][0].rearrange("b h p v -> h p b v")[h], st0[:, :, :]).then_inc(s["st0_out"], 16)

            act.wait_ge(s["og_ok"], ONE + 2 * HEADS)
            act.wait_ge(s["st_out"], ONE + 16 * HEADS)
            act.wait_ge(s["st0_out"], ONE + 16 * HEADS)
            with act.Fori(0, KT) as i:
                act.activation(act_s[:, 0, i, :], keep[:, i, :], ACT.Copy).then_inc(s["act_hi"], 1)
            act.wait_ge(s["act_lo"], 2 * KT)
            with act.Fori(0, KT // 2) as i:
                for j, b in ((0, bankA), (1, bankB)):
                    act.wait_ge(s["job_done"], 2 * i + (N_GB + j + 1))
                    act.activation(p3(keep[:, 2 * i + j, :]), slot3(b), ACT.Tanh, scale=0.5,
                                   bias=dvec[:, 2 * i + j, V_BMB:V_BMB + 1]).then_inc(gb_tanh[j], 1)
                    hi(i, N_GB + j + 2)

            def w_out_hi(i, j):
                act.wait_ge(s["wo_in"], 32 * i + 16 * (j + 1))
                act.activation(wos[:, 0, 2 * i + j, :], woraw[:, :], ACT.Copy).then_inc(s["wo_hi"], 1)

            with act.Fori(0, KT // 2 - 1) as i:
                for j in range(2):
                    w_out_hi(i, j)
                    act.wait_ge(s["job_done"], 2 * i + (N_YB + j + 1))
                    hi(i, N_YB + j + 2)
            for j in range(2):
                w_out_hi(KT // 2 - 1, j)

            def merged_hi(n):
                nr = x_rows[n][2]
                if n >= 2:
                    act.wait_ge(s["y_mm"], n - 1)
                act.activation(ms[:, n % 2, 0, :, 0:nr], keep[:, :, n * P:n * P + nr], ACT.Copy).then_inc(s["m_hi"], 1)

            act.wait_ge(merged[0], ONE + KT // 2)
            act.wait_ge(merged[1], ONE + KT // 2)
            act.wait_ge(s["job_done"], N_YB + KT)
            merged_hi(0)
            for n in range(TTILES):
                nr = x_rows[n][2]
                if n + 1 < TTILES:
                    merged_hi(n + 1)
                act.wait_ge(s["y_res"], n + 1)
                act.activation(junk1[0:nr, :], yy[0:nr, n % 2, :], ACT.Square, accum_out=ssum[0:nr, 16 + n:17 + n]).then_inc(s["y_sq"], 1)
                act.wait_ge(s["y_sq"], n + 1)
                act.activation(rstd[0:nr, 16 + n:17 + n], ssum[0:nr, 16 + n:17 + n], ACT.Sqrt, scale=1.0 / D,
                               bias=ssum[0:nr, 31:32]).then_inc(s["y_rms"], 1)

        @block.vector
        def _(dve):
            dve.memset(ssum[:, 31:32], EPS).then_inc(s["eps_ok"], 1)
            dve.memset(rows[:, :], 0.0).then_inc(s["pad_ok"], 1)
            dve.memset(xn[:, :, :, NTOK:TOK].bitcast(F32), 0.0).then_inc(s["pad_ok"], 1)
            dve.wait_ge(s["ng_in"], 16)

            def x_lo(n):
                nr = x_rows[n][2]
                b = bankX[n % 2]
                cols = slice(n * P, n * P + nr)
                dve.wait_ge(s["x_hi"], n + 1)
                dve.tensor_tensor(xn[:, 1, :, cols], ps[:, b:b + 2, :].rearrange("p a (c n) -> p (a c) n", n=P)[:, :, 0:nr],
                                  xn[:, 0, :, cols].bitcast(F32), ALU.subtract).then_inc(s["x_lo"], 1)

            def x_scale(n):
                nr = x_rows[n][2]
                dve.wait_ge(s["x_rms"], n + 1)
                dve.reciprocal(rstd[0:nr, n:n + 1], rstd[0:nr, n:n + 1]).then_inc(s["x_rstd"], 1)
                dve.wait_ge(s["x_rstd"], n + 1)
                tile = xt[0:nr, n, :]
                dve.scalar_tensor_tensor(tile, tile, rstd[0:nr, n:n + 1], ngb[0:nr, :], ALU.mult, ALU.mult).then_inc(s["x_scaled"], 1)

            x_scale(0)
            x_scale(1)
            for n in range(TTILES):
                x_lo(n)
                if n + 2 < TTILES:
                    x_scale(n + 2)
                if n == 4:
                    dve.wait_ge(s["rows_T"], 1)
                    dve.tensor_copy(vec[:, :, :], ps[:, bankR, 0:KT * NROW].rearrange("p (k r) -> p k r", k=KT)).then_inc(s["vec_ok"], 1)

            n_tiny = [2]

            def tiny_step(ins):
                n_tiny[0] += 1
                ins.then_inc(s["tiny_ok"], 1)
                dve.wait_ge(s["tiny_ok"], n_tiny[0])

            dve.wait_ge(s["tiny_ok"], 2)
            e, r, q, mx, v = (tiny[:, n, :] for n in range(5))
            tiny_step(dve.tensor_scalar(r, e, 2.0, None, ALU.add))
            tiny_step(dve.reciprocal(r, r))
            tiny_step(dve.tensor_tensor(e, e, r, ALU.mult))
            tiny_step(dve.tensor_tensor(r, e, e, ALU.mult))
            tiny_step(dve.tensor_scalar(q, r, 1.0 / 17, None, ALU.mult))
            for c in (15, 13, 11, 9, 7, 5, 3):
                tiny_step(dve.scalar_tensor_tensor(q, q, 1.0 / c, r, ALU.add, ALU.mult))
            tiny_step(dve.scalar_tensor_tensor(q, q, 1.0, e, ALU.add, ALU.mult))
            tiny_step(dve.tensor_scalar(mx, vec[:, :, R_LAM], -1.0, 0.0, ALU.mult, ALU.max))
            tiny_step(dve.scalar_tensor_tensor(v, q, 2.0, mx, ALU.mult, ALU.add))
            dve.tensor_scalar(dvec[:, :, V_C], v, RG_C / 2, None, ALU.mult)
            dve.tensor_scalar(dvec[:, :, V_NC], v, -RG_C / 2, None, ALU.mult)
            dve.tensor_scalar(dvec[:, :, V_BR:V_BI + 1], vec[:, :, R_BR:R_BI + 1], 0.5, None, ALU.mult)
            dve.tensor_scalar(dvec[:, :, V_BMA:V_BMB + 1], vec[:, :, R_BM:R_BM + 2], 0.5, None, ALU.mult).then_inc(s["dvec_ok"], 1)

            dve.wait_ge(s["x_T"], TTILES)
            dve.memset(xbuf[:, 0:HIST], 0.0)
            dve.memset(xc[:, NTOK:TOK], 0.0)
            hist = xbuf[:, XS:XW].rearrange("p (q n) -> p q n", q=NSEQ)
            with dve.Fori(0, KT) as i:
                dve.tensor_copy(hist[:, :, 0:HIST], vec[:, i, R_CS:NROW].rearrange("p (q n) -> p q n", q=NSEQ)).then_inc(s["hist_ok"], 1)
                dve.wait_ge(s["hist_ok"], i + 1)
                dve.wait_ge(s["x_evac"], i + 1)
                xcp = xc[:, 0:SEQ]
                xcq = xc[:, SEQ:NTOK].rearrange("p (q n) -> p q n", q=NSEQ)
                for k in range(CONV):
                    wk = vec[:, i, R_CONVW + k:R_CONVW + k + 1]
                    for which, (dst, src) in enumerate(((xcp, xbuf[:, k:k + SEQ]), (xcq, hist[:, :, k:k + SLEN]))):
                        if k == 0:
                            ins = dve.tensor_scalar(dst, src, wk, vec[:, i, R_CONVB:R_CONVB + 1], ALU.mult, ALU.add)
                        else:
                            dve.wait_ge(s["conv_step"], 8 * i + (2 * k - 1 + which))
                            ins = dve.scalar_tensor_tensor(dst, src, wk, dst, ALU.mult, ALU.add)
                        ins.then_inc(s["conv_step"], 1)
                dve.tensor_copy(tails[:, i, T_C:T_C + HIST], xbuf[:, SEQ:SEQ + HIST])
                dve.tensor_copy(tails[:, i, T_C + HIST:NTAIL].rearrange("p (q n) -> p q n", q=NSEQ),
                                hist[:, :, SLEN:SLEN + HIST]).then_inc(s["x_tail"], 1)
                dve.wait_ge(s["g_hi"], i + 1)
                dve.tensor_tensor(glo[:, :, :], graw[:, :, :], ghi[:, :, :].bitcast(F32), ALU.subtract).then_inc(s["g_lo"], 1)
                dve.wait_ge(s["xc_hi"], i + 1)
                dve.tensor_tensor(xcs[:, 1, :], xc[:, :], xcs[:, 0, :].bitcast(F32), ALU.subtract).then_inc(s["xc_lo"], 1)
                dve.wait_ge(s["job_done"], 2 * i + 2)
                dve.tensor_copy(p3(sz[:, :]), slot3(bankB)).then_inc(s["z_copy"], 1)
                dve.wait_ge(s["i_tanh"], ONE + i + 1)
                dve.scalar_tensor_tensor(ti[:, :], ti[:, :], 1.0, xc[:, :], ALU.add, ALU.mult).then_inc(s["i_x"], 1)
                dve.wait_ge(s["a_ok"], i + 1)
                dve.tensor_tensor(hh[:, :], dec[:, :], dec[:, :], ALU.mult).then_inc(s["a_sq"], 1)
                dve.wait_ge(s["a_sq"], i + 1)
                dve.wait_ge(s["t_ok"], i + 1)
                dve.scalar_tensor_tensor(wt[:, :], hh[:, :], 1.0, wt[:, :], ALU.add, ALU.mult).then_inc(s["w_ok"], 1)
                dve.wait_ge(s["z_tanh"], i + 1)
                dve.wait_ge(s["z_copy"], i + 1)
                dve.scalar_tensor_tensor(sz[:, :], tz[:, :], 1.0, sz[:, :], ALU.add, ALU.mult).then_inc(s["z_silu"], 1)
                first_a = dec[:, SEQ:NTOK:SLEN]
                first_u = ti[:, SEQ:NTOK:SLEN]
                dve.tensor_tensor(fix[:, :], first_a, vec[:, i, R_H0:R_H0 + NSEQ], ALU.mult).then_inc(s["fix_step"], 1)
                dve.wait_ge(s["m_ok"], i + 1)
                dve.wait_ge(s["i_x"], i + 1)
                dve.tensor_tensor(ti[:, :], ti[:, :], wt[:, :], ALU.mult).then_inc(s["u_ok"], 1)
                dve.wait_ge(s["u_ok"], i + 1)
                dve.wait_ge(s["fix_step"], 3 * i + 1)
                dve.tensor_tensor(first_u, first_u, fix[:, :], ALU.add).then_inc(s["fix_step"], 1)
                dve.memset(first_a, 0.0).then_inc(s["fix_step"], 1)
                dve.wait_ge(s["fix_step"], 3 * i + 3)
                dve.tensor_tensor_scan(hh[:, :], dec[:, :], ti[:, :], 0.0, ALU.mult, ALU.add).then_inc(s["h_ok"], 1)
                dve.wait_ge(s["h_ok"], i + 1)
                dve.wait_ge(s["z_silu"], ONE + i + 1)
                dve.tensor_tensor(keep[:, i, :], hh[:, :], sz[:, :], ALU.mult).then_inc(s["hz_ok"], 1)
                dve.tensor_copy(tails[:, i, T_H:T_H + 1], hh[:, SEQ - 1:SEQ])
                dve.tensor_copy(tails[:, i, T_H + 1:T_H + 1 + NSEQ], hh[:, SEQ + SLEN - 1:NTOK:SLEN]).then_inc(s["h_tail"], 1)

            def split_operand(first):
                with dve.Fori(0, KT) as i:
                    dve.wait_ge(s["act_hi"], i + (first + 1))
                    dve.tensor_tensor(act_s[:, 1, i, :], keep[:, i, :], act_s[:, 0, i, :].bitcast(F32), ALU.subtract).then_inc(s["act_lo"], 1)

            dve.wait_ge(s["h_tail"], KT)
            split_operand(0)
            dve.wait_ge(s["ga_first"], 1)
            with dve.Fori(0, KT - 1) as i:
                dve.wait_ge(s["ga_tanh"], i + ONE)
                dve.wait_ge(s["job_done"], 2 * i + (N_MIXA + 3))
                dve.scalar_tensor_tensor(p3(keep[:, i, :]), p3(keep[:, i, :]), 1.0, slot3(bankA), ALU.add, ALU.mult).then_inc(s["ma_ok"], 1)
            dve.wait_ge(s["ga_tanh"], KT - 1 + ONE)
            dve.wait_ge(s["job_done"], N_MIXA + 2 * KT)
            dve.scalar_tensor_tensor(p3(keep[:, KT - 1, :]), p3(keep[:, KT - 1, :]), 1.0, slot3(bankB), ALU.add, ALU.mult).then_inc(s["ma_ok"], 1)
            dve.wait_ge(s["alo_hi"], 1)
            dve.tensor_tensor(aw[:, :, RANK:2 * RANK], araw[:, :, :], aw[:, :, 0:RANK].bitcast(F32), ALU.subtract).then_inc(s["alo_lo"], 1)

            dve.wait_ge(s["alo_mm"], 1)
            dve.memset(att[:, :, :], 0.0).then_inc(s["att_zero"], 1)
            dve.wait_ge(s["att_zero"], 1)
            dve.wait_ge(s["masks_ok"], 1)
            dve.wait_ge(s["tails_out"], 64)
            dve.wait_ge(s["ma_out"], 16 * KT)
            with dve.Fori(0, HEADS) as h:
                def full(name):
                    dve.wait_ge(s["c_full"], full_at(h, name))

                def distance(l):
                    m = LEVELS[l]
                    n = SEQ if m > SLEVELS[0] else NTOK
                    v = gb[:, 0:n].rearrange("p (n m) -> p n m", m=2 * m)
                    if l >= 2:
                        dve.wait_ge(s["lev_qk"], h * len(LEVELS) + (l - 1))
                    dve.tensor_tensor(ring[l % 2][:, 0:n].rearrange("p (n m) -> p n m", m=2 * m), v,
                                      v[:, :, m - 1:m].to_broadcast([P, n // (2 * m), 2 * m]), ALU.subtract).then_inc(s["lev_d"], 1)

                def level_operands(l):
                    m = LEVELS[l]
                    dve.wait_ge(s["lev_e"], h * len(LEVELS) + (l + 1))
                    if l >= 2:
                        full(f"L{l - 2}")
                    src = ring[l % 2]
                    if m in SLEVELS:
                        dst = qks[:, SLEVELS.index(m), :]
                        dve.tensor_tensor(half(dst, m, 0), half(kb[:, SEQ:NTOK], m, 0), half(src[:, SEQ:NTOK], m, 0), ALU.mult)
                        dve.tensor_tensor(half(dst, m, 1), half(qb[:, SEQ:NTOK], m, 1), half(src[:, SEQ:NTOK], m, 1), ALU.mult)
                    dst = qk[:, l % 2, 0:SEQ]
                    dve.tensor_tensor(half(dst, m, 0), half(kb[:, 0:SEQ], m, 0), half(src[:, 0:SEQ], m, 0), ALU.mult)
                    dve.tensor_tensor(half(dst, m, 1), half(qb[:, 0:SEQ], m, 1), half(src[:, 0:SEQ], m, 1), ALU.mult).then_inc(s["lev_qk"], 1)

                def order(name):
                    n = [x for x, e in STEPS[:INDEX[name]] if e == "dve"]
                    if n:
                        dve.wait_ge(*emptied(h, n[-1]))
                    dve.sem_inc(s["dve_passed"], 1)

                def keep_level(l):
                    m = LEVELS[l]
                    full(f"L{l}")
                    order(f"L{l}")
                    dst = att[:, 0:NCHUNK, :].rearrange("p c (q h m) -> p c q h m", h=2, m=m)[:, :, :, 1, :]
                    mask = lmask[:, l, :].bitcast(U32).rearrange("p (o q m) -> p o q m", o=1, m=m).to_broadcast([P, NCHUNK, 64 // m, m])
                    dve.copy_predicated(dst, mask, ps[:, bank(f"L{l}"), :].rearrange("p (c q m) -> p c q m", c=NCHUNK, m=m)).then_inc(s["c_dve"], 1)

                def keep_diagonal(n):
                    full(f"dg{n}")
                    order(f"dg{n}")
                    mask = ident[:, :].bitcast(U32).rearrange("p (o m) -> p o m", o=1).to_broadcast([P, 4, P])
                    dve.copy_predicated(att[:, 4 * n:4 * n + 4, :], mask,
                                        ps[:, bank(f"dg{n}"), :].rearrange("p (c m) -> p c m", c=4)).then_inc(s["c_dve"], 1)

                dve.wait_ge(s["g_ln"], h + 1)
                dve.scalar_tensor_tensor(gb[:, :], gb[:, :], 0.0, dd[:, :], ALU.min, ALU.subtract).then_inc(s["g_ok"], 1)
                dve.wait_ge(s["g_ok"], h + 1)
                dve.tensor_tensor_scan(gb[:, :], notfirst[:, :], gb[:, :], 0.0, ALU.mult, ALU.add).then_inc(s["b_ok"], 1)
                dve.wait_ge(s["b_ok"], h + 1)
                dve.wait_ge(s["c_full"], ONE + h * NSTEP)
                distance(0)
                distance(1)
                dve.wait_ge(s["q_ok"], h + 1)
                dve.wait_ge(s["k_ok"], h + 1)
                level_operands(0)
                distance(2)
                keep_diagonal(0)
                keep_diagonal(1)
                for l in range(1, len(LEVELS)):
                    level_operands(l)
                    if l + 2 < len(LEVELS):
                        distance(l + 2)
                    if l == len(LEVELS) - 2:
                        dve.wait_ge(s["lev_qk"], h * len(LEVELS) + (l + 1))
                        for c0, c1, n in ((0, SEQ, CHUNK), (SEQ, NTOK, SLEN)):
                            v = gb[:, c0:c1].rearrange("p (c n) -> p c n", n=n)
                            ins = dve.tensor_tensor(kt[:, c0:c1].rearrange("p (c n) -> p c n", n=n),
                                                    v[:, :, n - 1:n].to_broadcast([P, (c1 - c0) // n, n]), v, ALU.subtract)
                        ins.then_inc(s["kt_d"], 1)
                    keep_level(l - 1)
                keep_level(len(LEVELS) - 1)
                dve.wait_ge(s["kt_e"], h + 1)
                dve.tensor_tensor(kt[:, 0:NTOK], kt[:, 0:NTOK], kb[:, 0:NTOK], ALU.mult).then_inc(s["kt_ok"], 1)
                full("smp")
                order("smp")
                for l, m in enumerate(SLEVELS):
                    mask = lmask[0:STOK, LEVELS.index(m), 0:32].bitcast(U32).rearrange("p (q m) -> p q m", m=m)
                    dve.copy_predicated(half(att[0:STOK, NCHUNK, 0:STOK], m, 1), mask,
                                        ps[0:STOK, bank("smp"), 32 * l:32 * l + 32].rearrange("p (q m) -> p q m", m=m)).then_inc(s["att_step"], 1)
                    dve.wait_ge(s["att_step"], 3 * h + (l + 1))
                    dve.sem_inc(s["dve_passed"], 1)
                dve.copy_predicated(att[0:STOK, NCHUNK, 0:STOK], ident[0:STOK, 0:STOK].bitcast(U32),
                                    ps[0:STOK, bank("smp"), 128:128 + STOK]).then_inc(s["c_dve"], 1)
                dve.wait_ge(s["qb_e"], h + 1)
                dve.tensor_tensor(qb[:, :], qb[:, :], dd[:, :], ALU.mult).then_inc(s["qb_ok"], 1)
                dve.wait_ge(s["zg_tanh"], 2 * h + 1)
                dve.scalar_tensor_tensor(p3(keep[:, 2 * h, :]), p3(vT[:, :]), 1.0, slot3(bankA), ALU.add, ALU.mult).then_inc(s["zg_silu"], 1)
                dve.wait_ge(*emptied(h, "kTc"))
                dve.tensor_tensor(kt[0:STOK, 0:NSEQ * P].rearrange("p (q n) -> p q n", q=NSEQ),
                                  kT[0:STOK, NCHUNK:NCHUNK + 1, :].to_broadcast([STOK, NSEQ, P]),
                                  smask[:, :].rearrange("p (q o) -> p q o", o=1).to_broadcast([STOK, NSEQ, P]), ALU.mult).then_inc(s["ktm_ok"], 1)
                dve.wait_ge(s["dlast_ok"], h + 1)
                dve.wait_ge(s["st_out"], ONE + 16 * h)
                for n in range(NCHUNK // 2):
                    full(f"KV{n}")
                    b = bank(f"KV{n}")
                    if n == 0:
                        ins = dve.tensor_copy(st[:, 0, :], ps[:, b, 0:DV])
                    else:
                        dve.wait_ge(*emptied(h, f"KV{n - 1}"))
                        ins = dve.scalar_tensor_tensor(st[:, 2 * n, :], st[:, 2 * n - 1, :], dlast[:, 2 * n:2 * n + 1], ps[:, b, 0:DV],
                                                       ALU.mult, ALU.add)
                    ins.then_inc(s["st_ok"], 1)
                    dve.wait_ge(s["st_ok"], (NCHUNK // 2) * h + (n + 1))
                    dve.scalar_tensor_tensor(st[:, 2 * n + 1, :], st[:, 2 * n, :], dlast[:, 2 * n + 1:2 * n + 2], ps[:, b, DV:2 * DV],
                                             ALU.mult, ALU.add).then_inc(s["c_dve"], 1)
                for n in range(NSEQ // 2):
                    full(f"sKV{n}")
                    for c in range(2):
                        q = 2 * n + c
                        ins = dve.scalar_tensor_tensor(st0[:, q, :], st0[:, q, :], dlast[:, NCHUNK + q:NCHUNK + q + 1],
                                                       ps[:, bank(f"sKV{n}"), c * DV:(c + 1) * DV], ALU.mult, ALU.add)
                    ins.then_inc(s["c_dve"], 1)
                dve.wait_ge(s["zg_tanh"], 2 * h + 2)
                dve.scalar_tensor_tensor(p3(keep[:, 2 * h + 1, :]), p3(vT[:, :]), 1.0, slot3(bankB), ALU.add, ALU.mult).then_inc(s["zg_silu"], 1)
                dve.wait_ge(s["n_rstd"], h + 1)
                for d in range(VH):
                    dve.scalar_tensor_tensor(oo[d][:, :], oo[d][:, :], vec[:, 2 * h + d, R_GN:R_GN + 1], kt[:, :], ALU.mult, ALU.mult).then_inc(s["o_norm"], 1)
                dve.wait_ge(s["zg_silu"], ONE + 2 * h + 2)
                for d in range(VH):
                    dve.wait_ge(s["o_norm"], 2 * h + (d + 1))
                    dve.tensor_tensor(keep[:, 2 * h + d, :], keep[:, 2 * h + d, :], oo[d][:, :], ALU.mult).then_inc(s["og_ok"], 1)

            split_operand(KT)
            dve.wait_ge(gb_tanh[0], ONE + KT // 2)
            dve.wait_ge(gb_tanh[1], ONE + KT // 2)
            with dve.Fori(0, KT // 2) as i:
                for j, b in ((0, bankA), (1, bankB)):
                    dve.wait_ge(s["wo_hi"], 2 * i + (j + 1))
                    dve.tensor_tensor(wos[:, 1, 2 * i + j, :], woraw[:, :], wos[:, 0, 2 * i + j, :].bitcast(F32), ALU.subtract).then_inc(s["wo_lo"], 1)
                    tile = keep[:, 2 * i + j, :]
                    dve.wait_ge(s["job_done"], 2 * i + (N_YB + j + 1))
                    dve.scalar_tensor_tensor(p3(tile), p3(tile), 1.0, slot3(b), ALU.add, ALU.mult).then_inc(s["yb_part"], 1)
                    dve.wait_ge(s["yb_part"], 2 * i + (j + 1))
                    dve.wait_ge(mal_in[j], 16 * (i + 1))
                    dve.tensor_tensor(tile[:, 0:NTOK], tile[:, 0:NTOK], mal[:, j, :], ALU.add).then_inc(merged[j], 1)

            def merged_lo(n):
                nr = x_rows[n][2]
                dve.wait_ge(s["m_hi"], n + 1)
                dve.tensor_tensor(ms[:, n % 2, 1, :, 0:nr], keep[:, :, n * P:n * P + nr], ms[:, n % 2, 0, :, 0:nr].bitcast(F32),
                                  ALU.subtract).then_inc(s["m_lo"], 1)

            merged_lo(0)
            for n in range(TTILES):
                nr = x_rows[n][2]
                b = (bankA, bankB)[n % 2]
                y = yy[0:nr, n % 2, :]
                if n + 1 < TTILES:
                    merged_lo(n + 1)
                if n == 0:
                    dve.wait_ge(s["fng_in"], 16)
                if n >= 2:
                    dve.wait_ge(y_out[n % 2], 16 * (n // 2))
                dve.wait_ge(s["y_mm"], n + 1)
                dve.wait_ge(s_xr[n % 2], 16 * (n // 2 + 1))
                dve.scalar_tensor_tensor(y.rearrange("p (a b) -> p a b", a=2), ps[0:nr, b:b + 2, :], 0.25,
                                         xr[0:nr, n % 2, :].rearrange("p (a b) -> p a b", a=2), ALU.mult, ALU.add).then_inc(s["y_res"], 1)
                dve.wait_ge(s["y_rms"], n + 1)
                r = rstd[0:nr, 16 + n:17 + n]
                dve.reciprocal(r, r).then_inc(s["y_rstd"], 1)
                dve.wait_ge(s["y_rstd"], n + 1)
                dve.scalar_tensor_tensor(y, y, r, fng[0:nr, :], ALU.mult, ALU.mult).then_inc(s["y_ok"], 1)


INPUTS = ["x_prompt", "x_sample", "state_lru_h", "state_lru_conv", "state_gla", "norm_g", "w_in", "conv_w", "conv_b",
          "w_r", "b_r", "w_i", "b_i", "lam", "w_a2", "b_a", "gla_norm_g", "w_lru_o", "w_gla_o", "b_merge", "w_out",
          "final_norm_g"]
OUTPUTS = [(1, SEQ, D), (NSEQ, SLEN, D), (1, 1, D), (1, 1, HIST, D), (1, 1, HEADS, DK, DV),
           (1, NSEQ, D), (1, NSEQ, HIST, D), (1, NSEQ, HEADS, DK, DV)]


def kernel(**inputs):
    import numpy as np
    import concourse.bacc as bacc
    from concourse.bass_utils import run_bass_kernel_spmd

    nc = bacc.Bacc("TRN2", target_bir_lowering=False, num_devices=1)
    arrays, t = {}, {}
    for name in INPUTS:
        a = np.ascontiguousarray(inputs[name])
        arrays["in_" + name] = a
        t[name] = nc.dram_tensor("in_" + name, a.shape, mybir.dt.from_np(a.dtype), kind="ExternalInput").ap()
    out = [nc.dram_tensor(f"out_{n}", shape, F32, kind="ExternalOutput").ap() for n, shape in enumerate(OUTPUTS)]
    build(nc, t, out)
    r = run_bass_kernel_spmd(nc, [arrays], core_ids=[0])
    return tuple(r.results[0][f"out_{n}"] for n in range(len(OUTPUTS)))
```

```python
import concourse.bass as bass
from concourse import mybir
from contextlib import ExitStack

F32 = mybir.dt.float32
F32R = mybir.dt.float32r
BF16 = mybir.dt.bfloat16
U32 = mybir.dt.uint32
ALU = mybir.AluOpType
ACT = mybir.ActivationFunctionType

P = 128
D = 1024
KT = D // P
SEQ = 1024
NSEQ, SLEN = 8, 8
STOK = NSEQ * SLEN
NTOK = SEQ + STOK
PIECE = 364
PIECES = 3
TOK = PIECE * PIECES
CONV = 4
HIST = CONV - 1
HEADS = 4
DK = 128
DV = 256
VH = DV // P
RANK = 16
CHUNK = 128
NCHUNK = SEQ // CHUNK
TTILES = NCHUNK + 1
LEVELS = (64, 32, 16, 8, 4, 2, 1)
PACKED = 2
SLEVELS = (4, 2, 1)
GATE_NORM = 16.0
EPS = 1e-6
RG_C = 8.0
COL_X, COL_Z, COL_Q, COL_K, COL_V, COL_ZG = 0, D, 2 * D, 2 * D + 512, 3 * D, 4 * D
COL_A = 5 * D
COL_GA = COL_A + RANK
COL_GB = COL_GA + D
N_IN = COL_GB + D
R_CONVW, R_CONVB, R_BR, R_BI, R_LAM, R_GN, R_BM, R_BA = 0, 4, 5, 6, 7, 8, 9, 11
R_H0, R_CS = 12, 20
NROW = R_CS + NSEQ * HIST
V_BR, V_BI, V_BMA, V_BMB, V_C, V_NC = range(6)
N_LRU, N_MIXA, N_GLA = 0, 2 * KT, 4 * KT
N_GB = N_GLA + 6 * HEADS
N_YB = N_GB + 8
ONE = 1
STARTS_AT_ONE = ("wa2_lo", "ma_ok", "wo_lo", "r_tanh", "i_tanh", "ga_tanh", "zg_silu", "x_tail", "i_done", "z_silu", "hz_ok",
                 "st0_out", "st_out", "og_ok", "merged0", "merged1", "gb_tanh0", "gb_tanh1", "c_full", "c_act", "c_dve")
NTAIL = 1 + NSEQ + HIST + NSEQ * HIST
T_H, T_C = 0, 1 + NSEQ
XS = HIST + SEQ
XW = XS + NSEQ * (HIST + SLEN)


def head_steps():
    steps = [("g0", "act"), ("g1", "act"), ("g2", "act"), ("dg0", "dve"), ("dg1", "dve")]
    steps += [("L0", "dve"), ("L1", "dve"), ("L2", "dve"), ("vt0a", "act"), ("vt0b", "act"), ("vt0c", "act")]
    steps += [("L3", "dve"), ("L4", "dve"), ("L5", "dve"), ("L6", "dve")]
    steps += [("vt1a", "act"), ("vt1b", "act"), ("vt1c", "act"), ("smp", "dve")]
    steps += [("kTa", "act"), ("kTb", "act"), ("kTc", "act")]
    steps += [(f"KV{n}", "dve") for n in range(NCHUNK // 2)]
    steps += [(f"O{g}{d}", "act") for g in range(2) for d in range(VH)] + [("Os", "act")]
    steps += [(f"sKV{n}", "dve") for n in range(NSEQ // 2)]
    steps += [(f"nrm{j}", "act") for j in range(PIECES)]
    return steps


def build(nc, t, out):
    ctx = ExitStack()
    with ctx:
        base = -(-nc.sbuf_base // 32) * 32

        def at(name, shape, dt, offset):
            return nc.alloc_sbuf_tensor_at(name, shape, dt, offset=base + offset)

        TILE = TOK * 4
        SLOT = -(-TILE // 32) * 32
        o_xn = 0
        o_raw = o_xn + 2 * KT * TILE
        o_hi = o_raw + 2 * KT * P * 4
        o_lo = o_hi + 2 * KT * P * 4
        o_keep = o_lo + 2 * KT * P * 4
        o_const = o_keep + KT * TILE
        xn = at("xn", [P, 2, KT, TOK], F32R, o_xn)
        raw = at("raw", [P, 2, KT, P], F32, o_raw)
        whi = at("whi", [P, 2, KT, P], F32R, o_hi)
        wlo = at("wlo", [P, 2, KT, P], F32R, o_lo)
        keep = at("keep", [P, KT, TOK], F32, o_keep)
        a = [o_const]

        def take(name, shape, dt, size):
            h = at(name, shape, dt, a[0])
            a[0] += -(-size // 32) * 32
            return h

        ident = take("ident", [P, P], F32, P * 4)
        vec = take("vec", [P, KT, NROW], F32, KT * NROW * 4)
        dvec = take("dvec", [P, KT, 6], F32, KT * 6 * 4)
        tiny = take("tiny", [P, 5, KT], F32, 5 * KT * 4)
        ssum = take("ssum", [P, 32], F32, 128)
        rstd = take("rstd", [P, 32], F32, 128)
        o_glaconst = a[0]
        ones = take("ones", [P, P], F32, P * 4)
        notfirst = take("notfirst", [P, TOK], BF16, TOK * 2)
        lmask = take("lmask", [P, len(LEVELS) - PACKED, 64], F32, (len(LEVELS) - PACKED) * 64 * 4)
        smask = take("smask", [P, NSEQ], F32, NSEQ * 4)
        A2 = 2 * RANK
        wa2_raw = take("wa2_raw", [3 * A2, P], F32, P * 4)
        wa2 = take("wa2", [3 * A2, P], F32R, P * 4)
        o_alo = a[0]
        alo = take("alo", [3 * A2, TOK], F32R, TILE)
        tails = at("tails", [P, KT, NTAIL], F32, o_alo)
        o_last = o_alo + -(-(PIECES - 1) * PIECE * 4 // 32) * 32
        aw = at("aw", [P, KT, A2], F32R, o_last)
        araw = at("araw", [P, KT, RANK], F32, o_alo + KT * NTAIL * 4)
        assert KT * NTAIL * 4 + KT * RANK * 4 <= o_last - o_alo and o_last + KT * A2 * 4 <= o_alo + TILE
        o_work = a[0]

        w = [o_work]

        def work(name, shape, dt, size):
            h = at(name, shape, dt, w[0])
            w[0] += -(-size // 32) * 32
            return h

        xbuf = work("xbuf", [P, XW], F32, XW * 4)
        xc = work("xc", [P, TOK], F32, TILE)
        xcs = work("xcs", [P, 2, TOK], F32R, 2 * TILE)
        tr = work("tr", [P, TOK], F32, TILE)
        ti = work("ti", [P, TOK], F32, TILE)
        dec = work("dec", [P, TOK], F32, TILE)
        wt = work("wt", [P, TOK], F32, TILE)
        tz = work("tz", [P, TOK], F32, TILE)
        sz = work("sz", [P, TOK], F32, TILE)
        hh = work("hh", [P, TOK], F32, TILE)
        fix = work("fix", [P, NSEQ], F32, NSEQ * 4)
        graw = work("graw", [P, 2, P], F32, 2 * P * 4)
        ghi = work("ghi", [P, 2, P], F32R, 2 * P * 4)
        glo = work("glo", [P, 2, P], F32R, 2 * P * 4)
        xt = at("xt", [P, TTILES, D], F32, o_work)
        ngb = at("ngb", [P, D], F32, o_work + TTILES * D * 4)
        junk0 = at("junk0", [P, D], F32, o_work + (TTILES + 1) * D * 4)
        rows = at("rows", [NROW, D], F32, o_work + (TTILES + 2) * D * 4)
        act_s = at("act_s", [P, 2, KT, TOK], F32R, o_work)
        trow = at("trow", [NTAIL, D], F32, o_keep)
        w[0] = o_work
        qb = work("qb", [P, TOK], F32, TILE)
        kb = work("kb", [P, TOK], F32, TILE)
        gb = work("gb", [P, TOK], F32, TILE)
        skey = at("skey", [P, P], F32R, w[0])
        svhi = at("svhi", [P, DV], F32R, w[0] + P * 4)
        svlo = at("svlo", [STOK, DV], F32R, w[0] + (P + DV) * 4)
        dd = work("dd", [P, TOK], F32, TILE)
        qk = work("qk", [P, 2, TOK], F32, 2 * TILE)
        qks = work("qks", [P, len(SLEVELS), STOK], F32, len(SLEVELS) * STOK * 4)
        vT = work("vT", [P, TOK], F32, TILE)
        vv = work("vv", [P, TTILES, DV], F32, TTILES * DV * 4)
        att = work("att", [P, TTILES, P], F32, TTILES * P * 4)
        skeys = at("skeys", [P, NSEQ, P], F32R, w[0])
        kt = work("kt", [P, TOK], F32, TILE)
        kT = work("kT", [P, TTILES, P], F32, TTILES * P * 4)
        st = work("st", [P, NCHUNK, DV], F32, NCHUNK * DV * 4)
        st0 = work("st0", [P, NSEQ, DV], F32, NSEQ * DV * 4)
        dlast = work("dlast", [P, NCHUNK + NSEQ], F32, 64)
        assert w[0] <= nc.sbuf_usable_end - base and o_work + 2 * KT * TILE <= nc.sbuf_usable_end - base
        assert NTAIL * KT * 4 <= TILE
        oo = [gb, kb]
        ring = [dd, kt]
        wos = at("wos", [P, 2, KT, D], F32R, o_xn)
        woraw = at("woraw", [P, D], F32, o_xn + 2 * KT * D * 4)
        mal = at("mal", [P, 2, NTOK], F32, o_glaconst)
        assert o_glaconst + 2 * NTOK * 4 <= o_work
        w[0] = o_work
        ms = (whi, wlo)
        xr = work("xr", [P, 2, D], F32, 2 * D * 4)
        yy = work("yy", [P, 2, D], F32, 2 * D * 4)
        fng = work("fng", [P, D], F32, D * 4)
        junk1 = work("junk1", [P, D], F32, D * 4)

        ps = ctx.enter_context(nc.psum_tensor("ps", [P, 8, 512], F32))
        bankA, bankB = 0, 3
        bankX, bankR = (3, 6), 5

        def slot3(b):
            return ps[:, b:b + PIECES, 0:PIECE]

        def p3(ap):
            return ap.rearrange("p (a b) -> p a b", a=PIECES)

        scratch = nc.dram_tensor("branch_a", (KT, P, TOK), F32, kind="Internal").ap()

        def sem(name):
            return ctx.enter_context(nc.semaphore(name))

        s = {n: sem(n) for n in (
            "rows_in", "ng_in", "ident_ok", "rows_T", "vec_ok", "dvec_ok", "tiny_ok", "masks_ok", "pool_step",
            "x_sq", "x_rms", "x_rstd", "x_scaled", "x_T", "x_hi", "x_lo", "pad_ok", "eps_ok",
            "hi_ok", "lo_ok", "job_done",
            "g_in", "g_hi", "g_lo", "x_evac", "hist_ok", "conv_step", "x_tail", "xc_hi", "xc_lo", "z_tanh", "z_silu", "z_copy",
            "r_done", "i_done", "r_tanh", "i_tanh", "a_ok", "t_ok", "i_x", "a_sq", "w_ok", "m_ok", "u_ok",
            "fix_step", "h_ok", "hz_ok", "h_tail", "tails_T", "tails_ok", "tails_out",
            "act_hi", "act_lo", "ga_first", "ga_tanh", "ma_ok", "ma_out",
            "dve_passed", "pe_passed", "sp_passed", "act_passed",
            "alo_in", "alo_hi", "alo_lo", "alo_mm", "alo_first", "alo_ok", "wa2_in", "wa2_hi", "wa2_lo", "att_zero", "c_full", "c_act", "c_dve",
            "g_abs", "g_exp", "g_ln", "g_ok", "b_ok", "q_ok", "k_ok", "lev_d", "lev_e", "lev_qk", "vT_ok",
            "kt_d", "kt_e", "kt_ok", "qb_e", "qb_ok", "dlast_ok", "st_ok", "ktm_ok", "att_step", "st0_in", "st_out", "st0_out",
            "smp_hi", "smp_lo", "smask_ok", "o_sq", "sq_sum", "n_rstd", "zg_tanh", "zg_silu", "o_norm", "og_ok",
            "gb_tanh0", "gb_tanh1", "wo_in", "wo_hi", "wo_lo", "mal_in0", "mal_in1", "yb_part", "merged0", "merged1",
            "fng_in", "m_hi", "m_lo", "y_mm", "y_res", "y_sq", "y_rms", "y_rstd", "y_ok", "y_out0", "y_out1",
        )}
        s_x = [sem(f"x_in{n}") for n in range(4)]
        s_raw = [sem(f"raw_in{n}") for n in range(2)]
        s_xr = [sem(f"xr_in{n}") for n in range(2)]
        gb_tanh = [s["gb_tanh0"], s["gb_tanh1"]]
        mal_in = [s["mal_in0"], s["mal_in1"]]
        merged = [s["merged0"], s["merged1"]]
        y_out = [s["y_out0"], s["y_out1"]]

        STEPS = head_steps()
        NSTEP = len(STEPS)
        INDEX = {name: n for n, (name, _) in enumerate(STEPS)}
        assert NSTEP % 2 == 0
        PER = {e: sum(x == e for _, x in STEPS) for e in ("act", "dve")}

        def bank(name):
            return 6 + INDEX[name] % 2

        def full_at(h, name):
            return h * NSTEP + (ONE + INDEX[name] + 1)

        def drained_at(h, n):
            if n < 0:
                assert STEPS[-1][1] == STEPS[n][1]
                return s["c_" + STEPS[-1][1]], h * PER[STEPS[-1][1]] + ONE
            engine = STEPS[n][1]
            count = sum(x == engine for _, x in STEPS[:n + 1])
            return s["c_" + engine], h * PER[engine] + (ONE + count)

        def emptied(h, name):
            return drained_at(h, INDEX[name])

        w_in = t["w_in"][0].rearrange("(k p) n -> p k n", p=P)
        w_lo_v = t["w_lru_o"][0].rearrange("(k p) n -> p k n", p=P)
        w_go_v = t["w_gla_o"][0].rearrange("(k p) n -> p k n", p=P)
        x_rows = [(t["x_prompt"][0], n * P, P) for n in range(NCHUNK)] + [(t["x_sample"].rearrange("a b d -> (a b) d"), 0, STOK)]

        def half(ap, m, which):
            return ap.rearrange("p (n h m) -> p n h m", h=2, m=m)[:, :, which, :]

        y_rows = [(out[0][0], n * P, P) for n in range(NCHUNK)] + [(out[1].rearrange("a b d -> (a b) d"), 0, STOK)]

        def store_y(sp, n):
            dst, r0, nr = y_rows[n]
            sp.wait_ge(s["y_ok"], n + 1)
            sp.dma_start(dst[r0:r0 + nr, :], yy[0:nr, n % 2, :]).then_inc(y_out[n % 2], 16)

        block = ctx.enter_context(nc.Block())

        @block.sync
        def _(sp):
            def row(r, ap):
                sp.dma_start(rows[r:r + ap.shape[0], 0:ap.shape[1]], ap).then_inc(s["rows_in"], 16)

            def load_x(n):
                src, r0, nr = x_rows[n]
                sp.dma_start(xt[0:nr, n, :], src[r0:r0 + nr, :]).then_inc(s_x[n % 4], 16)

            load_x(0)
            load_x(1)
            load_x(2)
            sp.dma_start(raw[:, 0], w_in[:, :, COL_X:COL_X + P]).then_inc(s_raw[0], 16)
            load_x(3)
            sp.wait_ge(s["pad_ok"], 1)
            row(R_CONVW, t["conv_w"][0])
            for r, name in ((R_CONVB, "conv_b"), (R_BR, "b_r"), (R_BI, "b_i"), (R_LAM, "lam"), (R_GN, "gla_norm_g"), (R_BA, "b_a")):
                row(r, t[name])
            row(R_BM, t["b_merge"].rearrange("o (r d) -> (o r) d", r=2))
            row(R_H0, t["state_lru_h"][0])
            row(R_CS, t["state_lru_conv"][0].rearrange("b k w -> (b k) w"))
            for n in range(4, TTILES):
                sp.wait_ge(s["x_sq"], n - 3)
                load_x(n)
            sp.dma_start(raw[:, 1], w_in[:, :, COL_Z:COL_Z + P]).then_inc(s_raw[1], 16)

            def load(n, slot, src):
                sp.wait_ge(s["lo_ok"], n - 1)
                sp.sem_inc(s["sp_passed"], 1)
                sp.dma_start(raw[:, slot], src).then_inc(s_raw[slot], 16)

            def load_gates(i):
                sp.dma_start(graw[:, 0], t["w_r"][0][i]).then_inc(s["g_in"], 16)
                sp.dma_start(graw[:, 1], t["w_i"][0][i]).then_inc(s["g_in"], 16)

            sp.wait_ge(s["x_T"], TTILES)
            load_gates(0)
            sp.dma_start(araw[:, :, :], w_in[:, :, COL_A:COL_A + RANK]).then_inc(s["alo_in"], 16)
            with sp.Fori(1, KT) as i:
                load(2 * i, 0, w_in[:, :, bass.ds(i * P + COL_X, P)])
                load(2 * i + 1, 1, w_in[:, :, bass.ds(i * P + COL_Z, P)])
                sp.wait_ge(s["g_lo"], i)
                load_gates(i)
            load(N_MIXA, 0, w_in[:, :, COL_GA:COL_GA + P])
            with sp.Fori(0, KT - 1) as i:
                load(2 * i + N_MIXA + 1, 1, w_in[:, :, bass.ds(i * P + (COL_GA + P), P)])
                load(2 * i + N_MIXA + 2, 0, w_lo_v[:, :, bass.ds(i * P, P)])
            load(N_MIXA + 2 * KT - 1, 1, w_lo_v[:, :, (KT - 1) * P:D])
            with sp.Fori(0, HEADS) as h:
                for j, (col, step) in enumerate(((COL_Q, P), (COL_K, P), (COL_V, DV), (COL_V + P, DV), (COL_ZG, DV), (COL_ZG + P, DV))):
                    load(6 * h + (N_GLA + j), (N_GLA + j) % 2, w_in[:, :, bass.ds(h * step + col, P)])
            with sp.Fori(0, KT // 2) as i:
                for j in range(2):
                    load(2 * i + (N_GB + j), (N_GB + j) % 2, w_in[:, :, bass.ds(i * 2 * P + (COL_GB + j * P), P)])
            sp.wait_ge(s["ma_out"], 16 * KT)
            with sp.Fori(0, KT // 2) as i:
                for j in range(2):
                    load(2 * i + (N_YB + j), (N_YB + j) % 2, w_go_v[:, :, bass.ds(i * 2 * P + j * P, P)])
                    sp.wait_ge(s["job_done"], N_YB)
                    sp.wait_ge(s["wo_lo"], 2 * i + j + ONE)
                    sp.dma_start(woraw[:, :], t["w_out"][0][bass.ds(i * 2 * P + j * P, P), :]).then_inc(s["wo_in"], 16)
                    sp.wait_ge(merged[j], i + ONE)
                    sp.dma_start(mal[:, j, :], scratch[2 * i + j][:, 0:NTOK]).then_inc(mal_in[j], 16)
            sp.wait_ge(s["job_done"], N_YB + KT)
            sp.dma_start(fng[:, :], t["final_norm_g"].rearrange("(o d) -> o d", o=1).to_broadcast([P, D])).then_inc(s["fng_in"], 16)
            for n in range(TTILES):
                if n >= 2:
                    sp.wait_ge(s["y_res"], n - 1)
                src, r0, nr = x_rows[n]
                sp.dma_start(xr[0:nr, n % 2, :], src[r0:r0 + nr, :]).then_inc(s_xr[n % 2], 16)
                if n >= 1:
                    store_y(sp, n - 1)
            store_y(sp, TTILES - 1)
            for sm, v in ((y_out[0], 16 * 5), (y_out[1], 16 * 4), (s["tails_out"], 64), (s["st_out"], 16 * HEADS + ONE),
                          (s["st0_out"], 16 * HEADS + ONE), (s["ma_out"], 16 * KT)):
                sp.wait_ge(sm, v)

        @block.gpsimd
        def _(pool):
            n = [0]

            def step(ins):
                n[0] += 1
                ins.then_inc(s["pool_step"], 1)
                pool.wait_ge(s["pool_step"], n[0])

            for name in STARTS_AT_ONE:
                pool.sem_inc(s[name], 1)
            step(pool.memset(ident[:, :], 0.0))
            pool.affine_select(out=ident[:, :], in_=ident[:, :], compare_op=ALU.not_equal, fill=1.0, base=0,
                               pattern=[[-1, P]], channel_multiplier=1).then_inc(s["ident_ok"], 1)
            for l, m in enumerate(LEVELS[PACKED:]):
                mask = lmask[:, l, :]
                step(pool.memset(mask, 1.0))
                step(pool.affine_select(out=mask, in_=mask, compare_op=ALU.is_ge, fill=0.0, base=0,
                                        pattern=[[-2 * m, 64 // m], [0, m]], channel_multiplier=1))
                step(pool.affine_select(out=mask, in_=mask, compare_op=ALU.is_ge, fill=0.0, base=m - 1,
                                        pattern=[[2 * m, 64 // m], [0, m]], channel_multiplier=-1))
            step(pool.memset(smask[0:STOK, :], 1.0))
            step(pool.affine_select(out=smask[0:STOK, :], in_=smask[0:STOK, :], compare_op=ALU.is_ge, fill=0.0, base=0,
                                    pattern=[[-SLEN, NSEQ]], channel_multiplier=1))
            step(pool.affine_select(out=smask[0:STOK, :], in_=smask[0:STOK, :], compare_op=ALU.is_ge, fill=0.0, base=SLEN - 1,
                                    pattern=[[SLEN, NSEQ]], channel_multiplier=-1))
            step(pool.memset(ones[:, :], 1.0 / DV))
            step(pool.memset(notfirst[:, :], 1.0))
            step(pool.memset(notfirst[:, 0:SEQ].rearrange("p (n c) -> p n c", c=CHUNK)[:, :, 0:1], 0.0))
            step(pool.memset(notfirst[:, SEQ:NTOK].rearrange("p (n c) -> p n c", c=SLEN)[:, :, 0:1], 0.0))
            pool.memset(notfirst[:, NTOK:TOK], 0.0).then_inc(s["masks_ok"], 1)

            def lo(i, c):
                pool.wait_ge(s["hi_ok"], 2 * i + (c + 1))
                pool.tensor_tensor(wlo[:, c % 2], raw[:, c % 2], whi[:, c % 2].bitcast(F32), ALU.subtract).then_inc(s["lo_ok"], 1)

            with pool.Fori(0, (N_YB + KT) // 2) as i:
                lo(i, 0)
                lo(i, 1)

        @block.tensor
        def _(pe):
            def split_product(dst, wh, wl, mh, ml, first, last):
                pe.matmul(dst, wh, mh, start=first, stop=False)
                pe.matmul(dst, wh, ml, start=False, stop=False)
                return pe.matmul(dst, wl, mh, start=False, stop=last)

            def piece(c, b, mov, j, ks=range(KT)):
                for k in ks:
                    cols = slice(j * PIECE, (j + 1) * PIECE)
                    ins = split_product(ps[:, b + j, 0:PIECE], whi[:, c % 2, k, :], wlo[:, c % 2, k, :],
                                        mov[:, 0, k, cols], mov[:, 1, k, cols], k == 0, k == KT - 1)
                return ins

            def job(i, c, b, mov):
                pe.wait_ge(s["lo_ok"], 2 * i + (c + 1))
                for j in range(PIECES):
                    ins = piece(c, b, mov, j)
                ins.then_inc(s["job_done"], 1)

            def x_transpose(n):
                nr = x_rows[n][2]
                b = bankX[n % 2]
                pe.wait_ge(s["x_scaled"], n + 1)
                if n >= 2:
                    pe.wait_ge(s["x_lo"], n - 1)
                for k in range(KT):
                    ins = pe.transpose(ps[:, b + k // 4, (k % 4) * P:(k % 4) * P + nr], xt[0:nr, n, k * P:(k + 1) * P],
                                       ident[0:nr, 0:nr])
                ins.then_inc(s["x_T"], 1)

            pe.wait_ge(s["ident_ok"], 1)
            for n in range(4):
                x_transpose(n)
            pe.wait_ge(s["rows_in"], 16 * 10)
            for k in range(KT):
                ins = pe.transpose(ps[:, bankR, k * NROW:(k + 1) * NROW], rows[:, k * P:(k + 1) * P], ident[0:NROW, 0:NROW])
            ins.then_inc(s["rows_T"], 1)
            x_transpose(4)
            pe.wait_ge(s["lo_ok"], 1)
            piece(0, bankA, xn, 0)
            x_transpose(5)
            x_transpose(6)
            pe.wait_ge(s["x_lo"], 6)
            piece(0, bankA, xn, 1, range(KT // 2))
            x_transpose(7)
            x_transpose(8)
            piece(0, bankA, xn, 1, range(KT // 2, KT))
            pe.wait_ge(s["x_lo"], TTILES)
            pe.wait_ge(s["pad_ok"], 2)
            piece(0, bankA, xn, 2).then_inc(s["job_done"], 1)
            pe.wait_ge(s["vec_ok"], 1)

            def z_and_gates(i):
                pe.wait_ge(s["i_tanh"], i + ONE)
                job(i, N_LRU + 1, bankB, xn)
                pe.wait_ge(s["xc_lo"], i + 1)
                pe.wait_ge(s["g_lo"], i + 1)
                for g, b in ((0, bankA), (1, bankB)):
                    if g == 1:
                        pe.wait_ge(s["z_copy"], i + 1)
                    for j in range(PIECES):
                        cols = slice(j * PIECE, (j + 1) * PIECE)
                        ins = split_product(ps[:, b + j, 0:PIECE], ghi[:, g, :], glo[:, g, :], xcs[:, 0, cols], xcs[:, 1, cols],
                                            True, True)
                    ins.then_inc(s["r_done"] if g == 0 else s["i_done"], 1)

            with pe.Fori(0, KT - 1) as i:
                z_and_gates(i)
                pe.wait_ge(s["r_tanh"], i + (ONE + 1))
                job(i, N_LRU + 2, bankA, xn)
            z_and_gates(KT - 1)

            pe.wait_ge(s["r_tanh"], KT + ONE)
            job(0, N_MIXA, bankA, xn)
            pe.wait_ge(s["i_tanh"], KT + ONE)
            with pe.Fori(0, KT - 1) as i:
                pe.wait_ge(s["ga_tanh"], i + ONE)
                job(i, N_MIXA + 1, bankB, xn)
                pe.wait_ge(s["ga_first"], 1)
                pe.wait_ge(s["ma_ok"], i + ONE)
                pe.wait_ge(s["lo_ok"], 2 * i + (N_MIXA + 3))
                for k in range(KT):
                    pe.wait_ge(s["act_lo"], k + 1)
                    piece(N_MIXA + 2, bankA, act_s, 0, range(k, k + 1))
                piece(N_MIXA + 2, bankA, act_s, 1)
                piece(N_MIXA + 2, bankA, act_s, 2).then_inc(s["job_done"], 1)
            pe.wait_ge(s["ga_tanh"], KT - 1 + ONE)
            job(0, N_MIXA + 2 * KT - 1, bankB, act_s)
            pe.wait_ge(s["h_tail"], KT)
            for k in range(KT):
                ins = pe.transpose(ps[0:NTAIL, 6 + k // 4, (k % 4) * P:(k % 4 + 1) * P], tails[:, k, :], ident[:, :])
            ins.then_inc(s["tails_T"], 1)

            pe.wait_ge(s["alo_lo"], 1)
            pe.wait_ge(s["ma_ok"], KT - 1 + ONE)
            for j in range(PIECES):
                for k in range(KT):
                    for r in range(2):
                        ins = pe.matmul(ps[0:2 * RANK, bankA + j, 0:PIECE], aw[:, k, :], xn[:, r, k, j * PIECE:(j + 1) * PIECE],
                                        start=(k == 0 and r == 0), stop=(k == KT - 1 and r == 1))
                ins.then_inc(s["alo_mm"], 1)
            pe.wait_ge(s["masks_ok"], 1)
            pe.wait_ge(s["alo_ok"], 2)
            with pe.Fori(0, HEADS) as h:
                def c_step(name, emit):
                    pe.wait_ge(*drained_at(h, INDEX[name] - 2))
                    emit(bank(name)).then_inc(s["c_full"], 1)

                def gate(j):
                    def emit(b):
                        return pe.matmul(ps[:, b, 0:PIECE], wa2[:, :], alo[:, j * PIECE:(j + 1) * PIECE], start=True, stop=True)
                    c_step(f"g{j}", emit)

                def diagonal(n):
                    def emit(b):
                        for c in range(4):
                            cols = slice((4 * n + c) * P, (4 * n + c + 1) * P)
                            ins = pe.matmul(ps[:, b, c * P:(c + 1) * P], kb[:, cols], qb[:, cols], start=True, stop=True)
                        return ins
                    c_step(f"dg{n}", emit)

                def level(l):
                    pe.wait_ge(s["lev_qk"], h * len(LEVELS) + (l + 1))

                    def emit(b):
                        if l < PACKED:
                            for c in range(0, SEQ // 2, P):
                                ins = pe.matmul(ps[:, b, c:c + P], qk[:, l % 2, c:c + P], qk[:, l % 2, SEQ // 2 + c:SEQ // 2 + c + P],
                                                start=True, stop=True)
                            return ins
                        for c in range(NCHUNK):
                            tile = qk[:, l % 2, c * P:(c + 1) * P]
                            ins = pe.matmul(ps[:, b, c * 64:(c + 1) * 64], tile, half(tile, LEVELS[l], 1), start=True, stop=True)
                        return ins
                    c_step(f"L{l}", emit)

                def sample_levels(b):
                    for l, m in enumerate(SLEVELS):
                        pe.matmul(ps[0:STOK, b, 32 * l:32 * l + 32], qks[:, l, :], half(qks[:, l, :], m, 1), start=True, stop=True)
                    return pe.matmul(ps[0:STOK, b, 128:128 + STOK], kb[:, SEQ:NTOK], qb[:, SEQ:NTOK], start=True, stop=True)

                def transposes(prefix, src, groups):
                    for name in groups:
                        g = "abc".index(name)

                        def emit(b):
                            if g == 2:
                                pe.sem_inc(s["pe_passed"], 1)
                            for n in range(4 * g, min(4 * g + 4, TTILES)):
                                nr = P if n < NCHUNK else STOK
                                ins = pe.transpose(ps[0:nr, b, (n % 4) * P:(n % 4 + 1) * P], src[:, n * P:n * P + nr], ident[:, :])
                            return ins
                        c_step(prefix + name, emit)

                def outer(n):
                    def emit(b):
                        for c in range(2):
                            ins = pe.matmul(ps[:, b, c * DV:(c + 1) * DV], kT[:, 2 * n + c, :], vv[:, 2 * n + c, :], start=True, stop=True)
                        return ins
                    c_step(f"KV{n}", emit)

                def output(g, d):
                    def emit(b):
                        for c in range(4 * g, 4 * g + 4):
                            dst = ps[:, b, (c % 4) * P:(c % 4 + 1) * P]
                            ins = pe.matmul(dst, vv[:, c, d * P:(d + 1) * P], att[:, c, :], start=True, stop=(c == 0))
                            if c > 0:
                                ins = pe.matmul(dst, st[:, c - 1, d * P:(d + 1) * P], qb[:, c * P:(c + 1) * P], start=False, stop=True)
                        return ins
                    c_step(f"O{g}{d}", emit)

                EARLY, LATE = range(KT // 2), range(KT // 2, KT)

                def part(c, b, j, ks=range(KT)):
                    ins = piece(N_GLA + c, b, xn, j, ks)
                    if j == PIECES - 1 and ks[-1] == KT - 1:
                        ins.then_inc(s["job_done"], 1)

                def sample_output(b):
                    between = iter(range(2, KT - 1))
                    for d in range(VH):
                        lo = d * STOK
                        pe.matmul(ps[:, b, lo:lo + STOK], vv[0:STOK, NCHUNK, d * P:(d + 1) * P], att[0:STOK, NCHUNK, 0:STOK],
                                  start=True, stop=False, skip_group_check=True)
                        for q in range(NSEQ):
                            ins = pe.matmul(ps[:, b, lo + q * SLEN:lo + (q + 1) * SLEN], st0[:, q, d * P:(d + 1) * P],
                                            qb[:, SEQ + q * SLEN:SEQ + (q + 1) * SLEN], start=False, stop=(q == NSEQ - 1),
                                            skip_group_check=True)
                            if q in (2, 5) or (q == NSEQ - 1 and d == 0):
                                k = next(between)
                                part(5, bankB, 2, range(k, k + 1))
                    return ins

                def sample_outer(n):
                    def emit(b):
                        for c in range(2):
                            dst = ps[:, b, c * DV:(c + 1) * DV]
                            pe.matmul(dst, skeys[:, 2 * n + c, :], svhi[:, :], start=True, stop=False)
                            ins = pe.matmul(dst, skeys[0:STOK, 2 * n + c, :], svlo[:, :], start=False, stop=True)
                        return ins
                    c_step(f"sKV{n}", emit)

                def mean_square(j):
                    def emit(b):
                        return pe.matmul(ps[:, b, 0:PIECE], ones[:, :], qk[:, 0, j * PIECE:(j + 1) * PIECE], start=True, stop=True)
                    c_step(f"nrm{j}", emit)

                def start_job(c):
                    pe.wait_ge(s["lo_ok"], 6 * h + (N_GLA + c + 1))

                start_job(0)
                pe.wait_ge(s["zg_silu"], 2 * h + ONE)
                part(0, bankA, 0)
                part(0, bankA, 1)
                pe.wait_ge(s["alo_ok"], PIECES)
                part(0, bankA, 2)
                pe.wait_ge(s["tails_ok"], 2)
                pe.wait_ge(s["wa2_lo"], h + (ONE + 1))
                gate(0)
                gate(1)
                start_job(1)
                pe.wait_ge(s["ma_ok"], KT + ONE)
                part(1, bankB, 0)
                gate(2)
                part(1, bankB, 1)
                part(1, bankB, 2)
                start_job(2)
                pe.wait_ge(s["q_ok"], h + 1)
                part(2, bankA, 0)
                pe.wait_ge(s["k_ok"], h + 1)
                diagonal(0)
                diagonal(1)
                part(2, bankA, 1)
                level(0)
                part(2, bankA, 2)
                level(1)
                start_job(3)
                part(3, bankB, 0)
                level(2)
                pe.wait_ge(s["vT_ok"], 2 * h + 1)
                transposes("vt0", vT, "a")
                part(3, bankB, 1, EARLY)
                transposes("vt0", vT, "bc")
                part(3, bankB, 1, LATE)
                level(3)
                part(3, bankB, 2)
                level(4)
                start_job(4)
                part(4, bankA, 0)
                level(5)
                part(4, bankA, 1)
                level(6)
                pe.wait_ge(s["vT_ok"], 2 * h + 2)
                transposes("vt1", vT, "a")
                part(4, bankA, 2, EARLY)
                transposes("vt1", vT, "bc")
                part(4, bankA, 2, LATE)
                c_step("smp", sample_levels)
                pe.wait_ge(s["kt_ok"], h + 1)
                transposes("kT", kt, "a")
                start_job(5)
                part(5, bankB, 0)
                transposes("kT", kt, "bc")
                part(5, bankB, 1, EARLY)
                pe.wait_ge(*emptied(h, "kTc"))
                outer(0)
                outer(1)
                part(5, bankB, 1, LATE)
                outer(2)
                outer(3)
                part(5, bankB, 2, range(2))
                pe.wait_ge(s["qb_ok"], h + 1)
                for g in range(2):
                    pe.wait_ge(*emptied(h, f"KV{2 * g + 1}"))
                    for d in range(VH):
                        output(g, d)
                pe.wait_ge(s["st0_in"], 16 * (h + 1))
                c_step("Os", sample_output)
                pe.wait_ge(s["ktm_ok"], h + 1)
                sample_outer(0)
                sample_outer(1)
                part(5, bankB, 2, range(KT - 1, KT))
                sample_outer(2)
                sample_outer(3)
                pe.wait_ge(s["sq_sum"], 2 * (h + 1))
                for j in range(PIECES):
                    mean_square(j)

            pe.wait_ge(s["zg_silu"], 2 * HEADS + ONE)
            with pe.Fori(0, KT // 2) as i:
                for j, b in ((0, bankA), (1, bankB)):
                    pe.wait_ge(gb_tanh[j], i + ONE)
                    job(i, N_GB + j, b, xn)
            pe.wait_ge(s["act_lo"], 2 * KT)
            with pe.Fori(0, KT // 2) as i:
                for j, b in ((0, bankA), (1, bankB)):
                    pe.wait_ge(gb_tanh[j], KT // 2 + ONE)
                    pe.wait_ge(merged[j], i + ONE)
                    job(i, N_YB + j, b, act_s)
            pe.wait_ge(s["wo_lo"], KT + ONE)
            pe.wait_ge(merged[0], KT // 2 + ONE)

            def out_part(slot, e, ks):
                b = (bankA, bankB)[slot]
                for k in ks:
                    ins = split_product(ps[:, b + e, :], ms[0][:, slot, k, :], ms[1][:, slot, k, :],
                                        wos[:, 0, k, e * 512:(e + 1) * 512], wos[:, 1, k, e * 512:(e + 1) * 512],
                                        k == 0, k == KT - 1)
                return ins

            def out_tile(n, slot):
                pe.wait_ge(s["m_lo"], n + 2)
                out_part(slot, 0, range(KT))
                out_part(slot, 1, range(KT)).then_inc(s["y_mm"], 1)

            pe.wait_ge(s["m_lo"], 1)
            out_part(0, 0, range(KT - 1))
            out_part(0, 1, range(KT - 1))
            pe.wait_ge(s["m_lo"], 2)
            out_part(0, 0, (KT - 1,))
            out_part(0, 1, (KT - 1,)).then_inc(s["y_mm"], 1)
            pe.wait_ge(merged[1], KT // 2 + ONE)
            out_tile(1, 1)
            with pe.Fori(1, NCHUNK // 2) as i:
                for slot in range(2):
                    pe.wait_ge(s["y_res"], 2 * i + (slot - 1))
                    out_tile(2 * i + slot, slot)
            pe.wait_ge(s["y_res"], NCHUNK - 1)
            out_tile(NCHUNK, 0)

        @block.scalar
        def _(act):
            def hi(i, c):
                act.wait_ge(s_raw[c % 2], 16 * i + 16 * (c // 2 + 1))
                if not isinstance(i, int) or c >= 2:
                    act.wait_ge(s["job_done"], 2 * i + (c - 1))
                act.activation(whi[:, c % 2], raw[:, c % 2], ACT.Copy).then_inc(s["hi_ok"], 1)

            act.dma_start(ngb[:, :], t["norm_g"][0:1, :].to_broadcast([P, D])).then_inc(s["ng_in"], 16)
            act.wait_ge(s["eps_ok"], 1)
            act.activation(rstd[:, 31:32], ssum[:, 31:32], ACT.Sqrt)

            def x_rms(n):
                nr = x_rows[n][2]
                act.wait_ge(s_x[n % 4], 16 * (n // 4 + 1))
                act.activation(junk0[0:nr, :], xt[0:nr, n, :], ACT.Square, accum_out=ssum[0:nr, n:n + 1]).then_inc(s["x_sq"], 1)
                act.wait_ge(s["x_sq"], n + 1)
                act.wait_ge(s["eps_ok"], 1)
                act.activation(rstd[0:nr, n:n + 1], ssum[0:nr, n:n + 1], ACT.Sqrt, scale=1.0 / D, bias=ssum[0:nr, 31:32]).then_inc(s["x_rms"], 1)

            def x_hi(n):
                nr = x_rows[n][2]
                b = bankX[n % 2]
                act.wait_ge(s["x_T"], n + 1)
                act.activation(xn[:, 0, :, n * P:n * P + nr], ps[:, b:b + 2, :].rearrange("p a (c n) -> p (a c) n", n=P)[:, :, 0:nr],
                               ACT.Copy).then_inc(s["x_hi"], 1)

            x_rms(0)
            x_rms(1)
            for n in range(TTILES):
                x_hi(n)
                if n + 2 < TTILES:
                    x_rms(n + 2)
                if n == 1:
                    hi(0, 0)
            hi(0, 1)
            act.wait_ge(s["vec_ok"], 1)
            act.activation(tiny[:, 0, :], vec[:, :, R_LAM], ACT.Abs).then_inc(s["tiny_ok"], 1)
            act.wait_ge(s["tiny_ok"], 1)
            act.activation(tiny[:, 0, :], tiny[:, 0, :], ACT.Exp, scale=-1.0).then_inc(s["tiny_ok"], 1)
            act.wait_ge(s["x_T"], TTILES)
            act.wait_ge(s["x_lo"], TTILES)

            with act.Fori(0, KT) as i:
                act.wait_ge(s["job_done"], 2 * i + 1)
                act.wait_ge(s["x_tail"], i + ONE)
                act.activation(xbuf[:, HIST:HIST + 2 * PIECE].rearrange("p (a b) -> p a b", a=2), ps[:, bankA:bankA + 2, 0:PIECE], ACT.Copy)
                act.activation(xbuf[:, HIST + 2 * PIECE:XS], ps[:, bankA + 2, 0:SEQ - 2 * PIECE], ACT.Copy)
                act.activation(xbuf[:, XS:XW].rearrange("p (q n) -> p q n", q=NSEQ)[:, :, HIST:HIST + SLEN],
                               ps[:, bankA + 2, SEQ - 2 * PIECE:NTOK - 2 * PIECE].rearrange("p (q n) -> p q n", q=NSEQ),
                               ACT.Copy).then_inc(s["x_evac"], 1)
                hi(i, 2)
                act.wait_ge(s["g_in"], 32 * (i + 1))
                act.wait_ge(s["i_done"], i + ONE)
                act.activation(ghi[:, :, :], graw[:, :, :], ACT.Copy).then_inc(s["g_hi"], 1)
                act.wait_ge(s["conv_step"], 8 * (i + 1))
                act.activation(xcs[:, 0, :], xc[:, :], ACT.Copy).then_inc(s["xc_hi"], 1)
                hi(i, 3)
                act.wait_ge(s["dvec_ok"], 1)
                act.wait_ge(s["r_done"], i + 1)
                act.activation(p3(tr[:, :]), slot3(bankA), ACT.Tanh, scale=0.5, bias=dvec[:, i, V_BR:V_BR + 1]).then_inc(s["r_tanh"], 1)
                act.wait_ge(s["i_done"], i + (ONE + 1))
                act.wait_ge(s["hz_ok"], i + ONE)
                act.activation(p3(ti[:, :]), slot3(bankB), ACT.Tanh, scale=0.5, bias=dvec[:, i, V_BI:V_BI + 1]).then_inc(s["i_tanh"], 1)
                act.wait_ge(s["z_copy"], i + 1)
                act.activation(tz[:, :], sz[:, :], ACT.Tanh, scale=0.5).then_inc(s["z_tanh"], 1)
                act.wait_ge(s["r_tanh"], i + (ONE + 1))
                act.activation(dec[:, :], tr[:, :], ACT.Exp, scale=dvec[:, i, V_NC:V_NC + 1], bias=dvec[:, i, V_NC:V_NC + 1]).then_inc(s["a_ok"], 1)
                act.activation(wt[:, :], tr[:, :], ACT.Tanh, scale=dvec[:, i, V_C:V_C + 1], bias=dvec[:, i, V_C:V_C + 1]).then_inc(s["t_ok"], 1)
                act.wait_ge(s["w_ok"], i + 1)
                act.activation(wt[:, :], wt[:, :], ACT.Sqrt, scale=0.25).then_inc(s["m_ok"], 1)

            act.wait_ge(s["alo_in"], 16)
            act.activation(aw[:, :, 0:RANK], araw[:, :, :], ACT.Copy).then_inc(s["alo_hi"], 1)
            hi(0, N_MIXA + 2)
            act.wait_ge(s["hz_ok"], KT + ONE)
            act.wait_ge(s["x_tail"], KT + ONE)
            with act.Fori(0, KT - 2) as i:
                act.activation(act_s[:, 0, i, :], keep[:, i, :], ACT.Copy).then_inc(s["act_hi"], 1)
            act.wait_ge(s["job_done"], N_MIXA + 1)
            act.wait_ge(s["act_lo"], 1)
            act.activation(p3(keep[:, 0, :]), slot3(bankA), ACT.Tanh, scale=0.5, bias=dvec[:, 0, V_BMA:V_BMA + 1]).then_inc(s["ga_first"], 1)
            for k in (KT - 2, KT - 1):
                act.activation(act_s[:, 0, k, :], keep[:, k, :], ACT.Copy).then_inc(s["act_hi"], 1)
            act.wait_ge(s["act_lo"], KT)
            with act.Fori(0, KT - 1) as i:
                act.wait_ge(s["job_done"], 2 * i + (N_MIXA + 2))
                act.sem_inc(s["act_passed"], 1)
                act.activation(p3(keep[:, i + 1, :]), slot3(bankB), ACT.Tanh, scale=0.5, bias=dvec[:, i + 1, V_BMA:V_BMA + 1]).then_inc(s["ga_tanh"], 1)
                hi(i, N_MIXA + 3)
                act.wait_ge(s["job_done"], 2 * i + (N_MIXA + 3))
                hi(i, N_MIXA + 4)
                act.wait_ge(s["ma_ok"], i + (ONE + 1))
                act.dma_start(scratch[i], keep[:, i, :]).then_inc(s["ma_out"], 16)
            hi(0, N_MIXA + 2 * KT + 1)
            act.wait_ge(s["ma_ok"], KT + ONE)
            act.dma_start(scratch[KT - 1], keep[:, KT - 1, :]).then_inc(s["ma_out"], 16)
            act.wait_ge(s["tails_T"], 1)
            for j in range(PIECES):
                act.wait_ge(s["alo_mm"], j + 1)
                for r in (0, 2):
                    ins = act.activation(alo[r * A2:(r + 1) * A2, j * PIECE:(j + 1) * PIECE], ps[0:A2, bankA + j, 0:PIECE], ACT.Copy)
                ins.then_inc(s["alo_first"], 1)

            act.wait_ge(s["ma_out"], 16 * KT)
            for n in range(2):
                act.activation(trow[:, n * 512:(n + 1) * 512], ps[0:NTAIL, 6 + n, :], ACT.Copy).then_inc(s["tails_ok"], 1)
            act.wait_ge(s["tails_ok"], 2)
            for dst, r0, nr in ((out[2][0], 0, 1), (out[5][0], 1, NSEQ), (out[3][0, 0], T_C, HIST),
                                (out[6][0].rearrange("b k w -> (b k) w"), T_C + HIST, NSEQ * HIST)):
                act.dma_start(dst, trow[r0:r0 + nr, :]).then_inc(s["tails_out"], 16)

            with act.Fori(0, HEADS) as h:
                def job_at(c):
                    act.wait_ge(s["job_done"], 6 * h + (N_GLA + c + 1))

                def full(name):
                    act.wait_ge(s["c_full"], full_at(h, name))

                def token_tiles(prefix, dst, groups):
                    for name in groups:
                        g = "abc".index(name)
                        full(prefix + name)
                        if g < 2:
                            act.activation(dst(4 * g, 4, P), ps[:, bank(prefix + name), :].rearrange("p (c n) -> p c n", n=P),
                                           ACT.Copy).then_inc(s["c_act"], 1)
                        else:
                            act.activation(dst(8, 1, STOK), ps[0:STOK, bank(prefix + name), 0:P].rearrange("p (c n) -> p c n", n=P),
                                           ACT.Copy).then_inc(s["c_act"], 1)

                def level_exp(l):
                    m = LEVELS[l]
                    n = SEQ if m > SLEVELS[0] else NTOK
                    act.wait_ge(s["lev_d"], h * len(LEVELS) + (l + 1))
                    for which, sign in ((0, -1.0), (1, 1.0)):
                        v = half(ring[l % 2][:, 0:n], m, which)
                        ins = act.activation(v, v, ACT.Exp, scale=sign / GATE_NORM)
                    ins.then_inc(s["lev_e"], 1)

                act.wait_ge(s["wa2_lo"], h + ONE)
                for r in range(6):
                    act.dma_start(wa2_raw[r * RANK:(r + 1) * RANK, :], t["w_a2"][0][:, bass.ds(h * P, P)]).then_inc(s["wa2_in"], 16)
                act.wait_ge(s["wa2_in"], 96 * (h + 1))
                act.activation(wa2[:, :], wa2_raw[:, :], ACT.Copy).then_inc(s["wa2_hi"], 1)
                job_at(0)
                act.activation(p3(qb[:, :]), slot3(bankA), ACT.Copy, scale=float(DK) ** -0.5).then_inc(s["q_ok"], 1)
                hi(3 * h, N_GLA + 2)
                act.wait_ge(s["st0_out"], 16 * h + ONE)
                act.dma_start(st0[:, :, :], t["state_gla"][0].rearrange("b h p v -> h p b v")[h]).then_inc(s["st0_in"], 16)
                act.wait_ge(s["og_ok"], 2 * h + ONE)
                for j in range(PIECES):
                    full(f"g{j}")
                    act.sem_inc(s["act_passed"], 1)
                    act.activation(gb[:, j * PIECE:(j + 1) * PIECE], ps[:, bank(f"g{j}"), 0:PIECE], ACT.Identity,
                                   bias=vec[:, h, R_BA:R_BA + 1]).then_inc(s["c_act"], 1)
                act.wait_ge(*emptied(h, "g2"))
                act.activation(dd[:, :], gb[:, :], ACT.Abs).then_inc(s["g_abs"], 1)
                act.wait_ge(s["g_abs"], h + 1)
                act.activation(dd[:, :], dd[:, :], ACT.Exp, scale=-1.0).then_inc(s["g_exp"], 1)
                act.wait_ge(s["g_exp"], h + 1)
                act.activation(dd[:, :], dd[:, :], ACT.Ln, bias=1.0).then_inc(s["g_ln"], 1)
                job_at(1)
                act.activation(p3(kb[:, :]), slot3(bankB), ACT.Copy).then_inc(s["k_ok"], 1)
                hi(3 * h, N_GLA + 3)
                level_exp(0)
                level_exp(1)
                level_exp(2)
                job_at(2)
                act.activation(p3(vT[:, :]), slot3(bankA), ACT.Copy).then_inc(s["vT_ok"], 1)
                hi(3 * h, N_GLA + 4)
                level_exp(3)
                value0 = lambda c, n, nr: vv[0:nr, c:c + n, 0:P]
                value1 = lambda c, n, nr: vv[0:nr, c:c + n, P:DV]
                key = lambda c, n, nr: kT[0:nr, c:c + n, :]
                token_tiles("vt0", value0, "a")
                level_exp(4)
                token_tiles("vt0", value0, "bc")
                job_at(3)
                act.activation(p3(vT[:, :]), slot3(bankB), ACT.Copy).then_inc(s["vT_ok"], 1)
                hi(3 * h, N_GLA + 5)
                level_exp(5)
                level_exp(6)
                token_tiles("vt1", value1, "a")
                act.activation(dlast[:, 0:NCHUNK], gb[:, CHUNK - 1:SEQ:CHUNK], ACT.Exp, scale=1.0 / GATE_NORM)
                act.activation(dlast[:, NCHUNK:NCHUNK + NSEQ], gb[:, SEQ + SLEN - 1:NTOK:SLEN], ACT.Exp, scale=1.0 / GATE_NORM).then_inc(s["dlast_ok"], 1)
                act.wait_ge(s["kt_d"], h + 1)
                act.activation(kt[:, 0:NTOK], kt[:, 0:NTOK], ACT.Exp, scale=1.0 / GATE_NORM).then_inc(s["kt_e"], 1)
                act.wait_ge(s["lev_qk"], len(LEVELS) * (h + 1))
                act.activation(dd[:, :], gb[:, :], ACT.Exp, scale=1.0 / GATE_NORM).then_inc(s["qb_e"], 1)
                token_tiles("vt1", value1, "bc")
                job_at(4)
                act.activation(p3(vT[:, :]), slot3(bankA), ACT.Tanh, scale=0.5).then_inc(s["zg_tanh"], 1)
                hi(3 * h, N_GLA + 6)
                token_tiles("kT", key, "abc")
                act.wait_ge(s["qb_ok"], h + 1)
                act.wait_ge(*emptied(h, "kTc"))
                act.activation(skey[0:STOK, :], kT[0:STOK, NCHUNK, :], ACT.Copy)
                for r in range(2):
                    ins = act.activation(svhi[r * STOK:(r + 1) * STOK, :], vv[0:STOK, NCHUNK, :], ACT.Copy)
                ins.then_inc(s["smp_hi"], 1)
                for g in range(2):
                    for d in range(VH):
                        full(f"O{g}{d}")
                        act.activation(oo[d][:, g * 512:(g + 1) * 512], ps[:, bank(f"O{g}{d}"), :], ACT.Copy).then_inc(s["c_act"], 1)

                def squares(cols):
                    for d in range(VH):
                        act.activation(qk[:, d, cols], oo[d][:, cols], ACT.Square).then_inc(s["o_sq"], 1)

                act.wait_ge(*emptied(h, "O11"))
                squares(slice(0, SEQ))
                full("Os")
                act.activation(oo[0][:, SEQ:NTOK], ps[:, bank("Os"), 0:STOK], ACT.Copy)
                act.activation(oo[1][:, SEQ:NTOK], ps[:, bank("Os"), STOK:2 * STOK], ACT.Copy).then_inc(s["c_act"], 1)
                act.wait_ge(*emptied(h, "Os"))
                squares(slice(SEQ, TOK))
                job_at(5)
                act.wait_ge(s["zg_silu"], 2 * h + (ONE + 1))
                act.activation(p3(vT[:, :]), slot3(bankB), ACT.Tanh, scale=0.5).then_inc(s["zg_tanh"], 1)
                for j in range(PIECES):
                    full(f"nrm{j}")
                    act.activation(kt[:, j * PIECE:(j + 1) * PIECE], ps[:, bank(f"nrm{j}"), 0:PIECE], ACT.Ln,
                                   bias=ssum[:, 31:32]).then_inc(s["c_act"], 1)
                hi(3 * h, N_GLA + 7)
                act.wait_ge(*emptied(h, "nrm2"))
                act.activation(kt[:, :], kt[:, :], ACT.Exp, scale=-0.5).then_inc(s["n_rstd"], 1)
                act.wait_ge(*emptied(h, "KV3"))
                act.dma_start(out[4][0, 0][h], st[:, NCHUNK - 1, :]).then_inc(s["st_out"], 16)
                act.wait_ge(*emptied(h, "sKV3"))
                act.dma_start(out[7][0].rearrange("b h p v -> h p b v")[h], st0[:, :, :]).then_inc(s["st0_out"], 16)

            act.wait_ge(s["og_ok"], 2 * HEADS + ONE)
            act.wait_ge(s["st_out"], 16 * HEADS + ONE)
            act.wait_ge(s["st0_out"], 16 * HEADS + ONE)
            with act.Fori(0, KT) as i:
                act.activation(act_s[:, 0, i, :], keep[:, i, :], ACT.Copy).then_inc(s["act_hi"], 1)
            with act.Fori(0, KT // 2) as i:
                for j, b in ((0, bankA), (1, bankB)):
                    act.wait_ge(s["act_lo"], 2 * i + (KT + j + 1))
                    act.wait_ge(s["job_done"], 2 * i + (N_GB + j + 1))
                    act.activation(p3(keep[:, 2 * i + j, :]), slot3(b), ACT.Tanh, scale=0.5,
                                   bias=dvec[:, 2 * i + j, V_BMB:V_BMB + 1]).then_inc(gb_tanh[j], 1)
                    hi(i, N_GB + j + 2)

            def w_out_hi(i, j):
                act.wait_ge(s["wo_in"], 32 * i + 16 * (j + 1))
                act.activation(wos[:, 0, 2 * i + j, :], woraw[:, :], ACT.Copy).then_inc(s["wo_hi"], 1)

            with act.Fori(0, KT // 2 - 1) as i:
                for j in range(2):
                    w_out_hi(i, j)
                    act.wait_ge(s["job_done"], 2 * i + (N_YB + j + 1))
                    hi(i, N_YB + j + 2)
            for j in range(2):
                w_out_hi(KT // 2 - 1, j)

            def merged_hi(n):
                nr = x_rows[n][2]
                if n >= 2:
                    act.wait_ge(s["y_mm"], n - 1)
                act.activation(ms[0][:, n % 2, :, 0:nr], keep[:, :, n * P:n * P + nr], ACT.Copy).then_inc(s["m_hi"], 1)

            act.wait_ge(s["job_done"], N_YB + KT - 1)
            act.wait_ge(merged[1], KT // 2 - 1 + ONE)
            act.wait_ge(merged[0], KT // 2 + ONE)
            act.activation(ms[0][:, 0, 0:KT - 1, :], keep[:, 0:KT - 1, 0:P], ACT.Copy).then_inc(s["m_hi"], 1)
            act.wait_ge(s["job_done"], N_YB + KT)
            act.wait_ge(merged[1], KT // 2 + ONE)
            act.activation(ms[0][:, 0, KT - 1, :], keep[:, KT - 1, 0:P], ACT.Copy).then_inc(s["m_hi"], 1)
            for n in range(TTILES):
                nr = x_rows[n][2]
                if n + 1 < TTILES:
                    merged_hi(n + 1)
                act.wait_ge(s["y_res"], n + 1)
                act.activation(junk1[0:nr, :], yy[0:nr, n % 2, :], ACT.Square, accum_out=ssum[0:nr, 16 + n:17 + n]).then_inc(s["y_sq"], 1)
                act.wait_ge(s["y_sq"], n + 1)
                act.activation(rstd[0:nr, 16 + n:17 + n], ssum[0:nr, 16 + n:17 + n], ACT.Sqrt, scale=1.0 / D,
                               bias=ssum[0:nr, 31:32]).then_inc(s["y_rms"], 1)

        @block.vector
        def _(dve):
            dve.memset(ssum[:, 31:32], EPS).then_inc(s["eps_ok"], 1)
            dve.memset(rows[:, :], 0.0).then_inc(s["pad_ok"], 1)
            dve.memset(xn[:, :, :, NTOK:TOK].bitcast(F32), 0.0).then_inc(s["pad_ok"], 1)
            dve.wait_ge(s["ng_in"], 16)

            def x_lo(n):
                nr = x_rows[n][2]
                b = bankX[n % 2]
                cols = slice(n * P, n * P + nr)
                dve.wait_ge(s["x_hi"], n + 1)
                dve.tensor_tensor(xn[:, 1, :, cols], ps[:, b:b + 2, :].rearrange("p a (c n) -> p (a c) n", n=P)[:, :, 0:nr],
                                  xn[:, 0, :, cols].bitcast(F32), ALU.subtract).then_inc(s["x_lo"], 1)

            def x_scale(n):
                nr = x_rows[n][2]
                dve.wait_ge(s["x_rms"], n + 1)
                dve.reciprocal(rstd[0:nr, n:n + 1], rstd[0:nr, n:n + 1]).then_inc(s["x_rstd"], 1)
                dve.wait_ge(s["x_rstd"], n + 1)
                tile = xt[0:nr, n, :]
                dve.scalar_tensor_tensor(tile, tile, rstd[0:nr, n:n + 1], ngb[0:nr, :], ALU.mult, ALU.mult).then_inc(s["x_scaled"], 1)

            x_scale(0)
            x_scale(1)
            for n in range(TTILES):
                x_lo(n)
                if n + 2 < TTILES:
                    x_scale(n + 2)
                if n == 4:
                    dve.wait_ge(s["rows_T"], 1)
                    dve.tensor_copy(vec[:, :, :], ps[:, bankR, 0:KT * NROW].rearrange("p (k r) -> p k r", k=KT)).then_inc(s["vec_ok"], 1)

            n_tiny = [2]

            def tiny_step(ins):
                n_tiny[0] += 1
                ins.then_inc(s["tiny_ok"], 1)
                dve.wait_ge(s["tiny_ok"], n_tiny[0])

            dve.wait_ge(s["tiny_ok"], 2)
            e, r, q, mx, v = (tiny[:, n, :] for n in range(5))
            tiny_step(dve.tensor_scalar(r, e, 2.0, None, ALU.add))
            tiny_step(dve.reciprocal(r, r))
            tiny_step(dve.tensor_tensor(e, e, r, ALU.mult))
            tiny_step(dve.tensor_tensor(r, e, e, ALU.mult))
            tiny_step(dve.tensor_scalar(q, r, 1.0 / 17, None, ALU.mult))
            for c in (15, 13, 11, 9, 7, 5, 3):
                tiny_step(dve.scalar_tensor_tensor(q, q, 1.0 / c, r, ALU.add, ALU.mult))
            tiny_step(dve.scalar_tensor_tensor(q, q, 1.0, e, ALU.add, ALU.mult))
            tiny_step(dve.tensor_scalar(mx, vec[:, :, R_LAM], -1.0, 0.0, ALU.mult, ALU.max))
            tiny_step(dve.scalar_tensor_tensor(v, q, 2.0, mx, ALU.mult, ALU.add))
            dve.tensor_scalar(dvec[:, :, V_C], v, RG_C / 2, None, ALU.mult)
            dve.tensor_scalar(dvec[:, :, V_NC], v, -RG_C / 2, None, ALU.mult)
            dve.tensor_scalar(dvec[:, :, V_BR:V_BI + 1], vec[:, :, R_BR:R_BI + 1], 0.5, None, ALU.mult)
            dve.tensor_scalar(dvec[:, :, V_BMA:V_BMB + 1], vec[:, :, R_BM:R_BM + 2], 0.5, None, ALU.mult).then_inc(s["dvec_ok"], 1)

            dve.wait_ge(s["x_T"], TTILES)
            dve.memset(xbuf[:, 0:HIST], 0.0)
            dve.memset(xc[:, NTOK:TOK], 0.0)
            hist = xbuf[:, XS:XW].rearrange("p (q n) -> p q n", q=NSEQ)
            with dve.Fori(0, KT) as i:
                dve.tensor_copy(hist[:, :, 0:HIST], vec[:, i, R_CS:NROW].rearrange("p (q n) -> p q n", q=NSEQ)).then_inc(s["hist_ok"], 1)
                dve.wait_ge(s["hist_ok"], i + 1)
                dve.wait_ge(s["x_evac"], i + 1)
                xcp = xc[:, 0:SEQ]
                xcq = xc[:, SEQ:NTOK].rearrange("p (q n) -> p q n", q=NSEQ)
                for k in range(CONV):
                    wk = vec[:, i, R_CONVW + k:R_CONVW + k + 1]
                    for which, (dst, src) in enumerate(((xcp, xbuf[:, k:k + SEQ]), (xcq, hist[:, :, k:k + SLEN]))):
                        if k == 0:
                            ins = dve.tensor_scalar(dst, src, wk, vec[:, i, R_CONVB:R_CONVB + 1], ALU.mult, ALU.add)
                        else:
                            dve.wait_ge(s["conv_step"], 8 * i + (2 * k - 1 + which))
                            ins = dve.scalar_tensor_tensor(dst, src, wk, dst, ALU.mult, ALU.add)
                        ins.then_inc(s["conv_step"], 1)
                dve.tensor_copy(tails[:, i, T_C:T_C + HIST], xbuf[:, SEQ:SEQ + HIST])
                dve.tensor_copy(tails[:, i, T_C + HIST:NTAIL].rearrange("p (q n) -> p q n", q=NSEQ),
                                hist[:, :, SLEN:SLEN + HIST]).then_inc(s["x_tail"], 1)
                dve.wait_ge(s["g_hi"], i + 1)
                dve.tensor_tensor(glo[:, :, :], graw[:, :, :], ghi[:, :, :].bitcast(F32), ALU.subtract).then_inc(s["g_lo"], 1)
                dve.wait_ge(s["xc_hi"], i + 1)
                dve.tensor_tensor(xcs[:, 1, :], xc[:, :], xcs[:, 0, :].bitcast(F32), ALU.subtract).then_inc(s["xc_lo"], 1)
                dve.wait_ge(s["job_done"], 2 * i + 2)
                dve.tensor_copy(p3(sz[:, :]), slot3(bankB)).then_inc(s["z_copy"], 1)
                dve.wait_ge(s["i_tanh"], i + (ONE + 1))
                dve.scalar_tensor_tensor(ti[:, :], ti[:, :], 1.0, xc[:, :], ALU.add, ALU.mult).then_inc(s["i_x"], 1)
                dve.wait_ge(s["a_ok"], i + 1)
                dve.tensor_tensor(hh[:, :], dec[:, :], dec[:, :], ALU.mult).then_inc(s["a_sq"], 1)
                dve.wait_ge(s["a_sq"], i + 1)
                dve.wait_ge(s["t_ok"], i + 1)
                dve.scalar_tensor_tensor(wt[:, :], hh[:, :], 1.0, wt[:, :], ALU.add, ALU.mult).then_inc(s["w_ok"], 1)
                dve.wait_ge(s["z_tanh"], i + 1)
                dve.wait_ge(s["z_copy"], i + 1)
                dve.scalar_tensor_tensor(sz[:, :], tz[:, :], 1.0, sz[:, :], ALU.add, ALU.mult).then_inc(s["z_silu"], 1)
                first_a = dec[:, SEQ:NTOK:SLEN]
                first_u = ti[:, SEQ:NTOK:SLEN]
                dve.tensor_tensor(fix[:, :], first_a, vec[:, i, R_H0:R_H0 + NSEQ], ALU.mult).then_inc(s["fix_step"], 1)
                dve.wait_ge(s["m_ok"], i + 1)
                dve.wait_ge(s["i_x"], i + 1)
                dve.tensor_tensor(ti[:, :], ti[:, :], wt[:, :], ALU.mult).then_inc(s["u_ok"], 1)
                dve.wait_ge(s["u_ok"], i + 1)
                dve.wait_ge(s["fix_step"], 3 * i + 1)
                dve.tensor_tensor(first_u, first_u, fix[:, :], ALU.add).then_inc(s["fix_step"], 1)
                dve.memset(first_a, 0.0).then_inc(s["fix_step"], 1)
                dve.wait_ge(s["fix_step"], 3 * i + 3)
                dve.tensor_tensor_scan(hh[:, :], dec[:, :], ti[:, :], 0.0, ALU.mult, ALU.add).then_inc(s["h_ok"], 1)
                dve.wait_ge(s["h_ok"], i + 1)
                dve.wait_ge(s["z_silu"], i + (ONE + 1))
                dve.tensor_tensor(keep[:, i, :], hh[:, :], sz[:, :], ALU.mult).then_inc(s["hz_ok"], 1)
                dve.tensor_copy(tails[:, i, T_H:T_H + 1], hh[:, SEQ - 1:SEQ])
                dve.tensor_copy(tails[:, i, T_H + 1:T_H + 1 + NSEQ], hh[:, SEQ + SLEN - 1:NTOK:SLEN]).then_inc(s["h_tail"], 1)

            def split_operand(first):
                with dve.Fori(0, KT) as i:
                    dve.wait_ge(s["act_hi"], i + (first + 1))
                    dve.tensor_tensor(act_s[:, 1, i, :], keep[:, i, :], act_s[:, 0, i, :].bitcast(F32), ALU.subtract).then_inc(s["act_lo"], 1)

            dve.wait_ge(s["h_tail"], KT)
            split_operand(0)
            dve.wait_ge(s["alo_hi"], 1)
            dve.tensor_tensor(aw[:, :, RANK:2 * RANK], araw[:, :, :], aw[:, :, 0:RANK].bitcast(F32), ALU.subtract).then_inc(s["alo_lo"], 1)
            dve.wait_ge(s["ga_first"], 1)
            with dve.Fori(0, KT - 1) as i:
                dve.wait_ge(s["ga_tanh"], i + ONE)
                dve.wait_ge(s["job_done"], 2 * i + (N_MIXA + 3))
                dve.scalar_tensor_tensor(p3(keep[:, i, :]), p3(keep[:, i, :]), 1.0, slot3(bankA), ALU.add, ALU.mult).then_inc(s["ma_ok"], 1)
            dve.wait_ge(s["ga_tanh"], KT - 1 + ONE)
            dve.wait_ge(s["job_done"], N_MIXA + 2 * KT)
            dve.scalar_tensor_tensor(p3(keep[:, KT - 1, :]), p3(keep[:, KT - 1, :]), 1.0, slot3(bankB), ALU.add, ALU.mult).then_inc(s["ma_ok"], 1)

            for j in range(PIECES):
                cols = slice(j * PIECE, (j + 1) * PIECE)
                dve.wait_ge(s["alo_first"], j + 1)
                dve.tensor_tensor(alo[A2:2 * A2, cols], ps[0:A2, bankA + j, 0:PIECE], alo[0:A2, cols].bitcast(F32),
                                  ALU.subtract).then_inc(s["alo_ok"], 1)
            dve.memset(att[:, :, :], 0.0).then_inc(s["att_zero"], 1)
            dve.wait_ge(s["att_zero"], 1)
            dve.wait_ge(s["masks_ok"], 1)
            dve.tensor_copy(smask[STOK:P, :], smask[0:STOK, :]).then_inc(s["smask_ok"], 1)
            dve.wait_ge(s["smask_ok"], 1)
            dve.wait_ge(s["tails_out"], 64)
            dve.wait_ge(s["ma_out"], 16 * KT)
            with dve.Fori(0, HEADS) as h:
                def full(name):
                    dve.wait_ge(s["c_full"], full_at(h, name))

                def distance(l):
                    m = LEVELS[l]
                    n = SEQ if m > SLEVELS[0] else NTOK
                    v = gb[:, 0:n].rearrange("p (n m) -> p n m", m=2 * m)
                    if l >= 2:
                        dve.wait_ge(s["lev_qk"], h * len(LEVELS) + (l - 1))
                    dve.tensor_tensor(ring[l % 2][:, 0:n].rearrange("p (n m) -> p n m", m=2 * m), v,
                                      v[:, :, m - 1:m].to_broadcast([P, n // (2 * m), 2 * m]), ALU.subtract).then_inc(s["lev_d"], 1)

                def level_operands(l):
                    m = LEVELS[l]
                    dve.wait_ge(s["lev_e"], h * len(LEVELS) + (l + 1))
                    if l >= 2:
                        full(f"L{l - 2}")
                    src = ring[l % 2]
                    if m in SLEVELS:
                        dst = qks[:, SLEVELS.index(m), :]
                        dve.tensor_tensor(half(dst, m, 0), half(kb[:, SEQ:NTOK], m, 0), half(src[:, SEQ:NTOK], m, 0), ALU.mult)
                        dve.tensor_tensor(half(dst, m, 1), half(qb[:, SEQ:NTOK], m, 1), half(src[:, SEQ:NTOK], m, 1), ALU.mult)
                    if l < PACKED:
                        dsts = [qk[:, l % 2, r * (SEQ // 2):(r + 1) * (SEQ // 2)].rearrange("p (n m) -> p n m", m=m) for r in range(2)]
                    else:
                        dsts = [half(qk[:, l % 2, 0:SEQ], m, r) for r in range(2)]
                    dve.tensor_tensor(dsts[0], half(kb[:, 0:SEQ], m, 0), half(src[:, 0:SEQ], m, 0), ALU.mult)
                    dve.tensor_tensor(dsts[1], half(qb[:, 0:SEQ], m, 1), half(src[:, 0:SEQ], m, 1), ALU.mult).then_inc(s["lev_qk"], 1)

                def order(name):
                    n = [x for x, e in STEPS[:INDEX[name]] if e == "dve"]
                    if n:
                        dve.wait_ge(*emptied(h, n[-1]))
                    dve.sem_inc(s["dve_passed"], 1)

                def keep_level(l):
                    m = LEVELS[l]
                    full(f"L{l}")
                    order(f"L{l}")
                    if l < PACKED:
                        blocks = P // m
                        for n in range(blocks):
                            c, q = n * 2 // blocks, n % (blocks // 2)
                            ins = dve.tensor_copy(att[2 * m * q:2 * m * q + m, c:NCHUNK:2, 2 * m * q + m:2 * m * (q + 1)],
                                                  ps[n * m:(n + 1) * m, bank(f"L{l}"), :].rearrange("p (c t) -> p c t", t=P)[:, :, n * m:(n + 1) * m])
                        ins.then_inc(s["c_dve"], 1)
                        return
                    dst = att[:, 0:NCHUNK, :].rearrange("p c (q h m) -> p c q h m", h=2, m=m)[:, :, :, 1, :]
                    mask = lmask[:, l - PACKED, :].bitcast(U32).rearrange("p (o q m) -> p o q m", o=1, m=m).to_broadcast([P, NCHUNK, 64 // m, m])
                    dve.copy_predicated(dst, mask, ps[:, bank(f"L{l}"), :].rearrange("p (c q m) -> p c q m", c=NCHUNK, m=m)).then_inc(s["c_dve"], 1)

                def keep_diagonal(n):
                    full(f"dg{n}")
                    order(f"dg{n}")
                    mask = ident[:, :].bitcast(U32).rearrange("p (o m) -> p o m", o=1).to_broadcast([P, 4, P])
                    dve.copy_predicated(att[:, 4 * n:4 * n + 4, :], mask,
                                        ps[:, bank(f"dg{n}"), :].rearrange("p (c m) -> p c m", c=4)).then_inc(s["c_dve"], 1)

                dve.wait_ge(s["wa2_hi"], h + 1)
                dve.tensor_tensor(wa2[2 * A2:3 * A2, :], wa2_raw[2 * A2:3 * A2, :], wa2[2 * A2:3 * A2, :].bitcast(F32),
                                  ALU.subtract).then_inc(s["wa2_lo"], 1)
                dve.wait_ge(s["g_ln"], h + 1)
                dve.scalar_tensor_tensor(gb[:, :], gb[:, :], 0.0, dd[:, :], ALU.min, ALU.subtract).then_inc(s["g_ok"], 1)
                dve.wait_ge(s["g_ok"], h + 1)
                dve.tensor_tensor_scan(gb[:, :], notfirst[:, :], gb[:, :], 0.0, ALU.mult, ALU.add).then_inc(s["b_ok"], 1)
                dve.wait_ge(s["b_ok"], h + 1)
                dve.wait_ge(s["c_full"], h * NSTEP + ONE)
                distance(0)
                distance(1)
                dve.wait_ge(s["q_ok"], h + 1)
                dve.wait_ge(s["k_ok"], h + 1)
                level_operands(0)
                distance(2)
                keep_diagonal(0)
                keep_diagonal(1)
                for l in range(1, len(LEVELS)):
                    level_operands(l)
                    if l + 2 < len(LEVELS):
                        distance(l + 2)
                    if l == len(LEVELS) - 2:
                        dve.wait_ge(s["lev_qk"], h * len(LEVELS) + (l + 1))
                        for c0, c1, n in ((0, SEQ, CHUNK), (SEQ, NTOK, SLEN)):
                            v = gb[:, c0:c1].rearrange("p (c n) -> p c n", n=n)
                            ins = dve.tensor_tensor(kt[:, c0:c1].rearrange("p (c n) -> p c n", n=n),
                                                    v[:, :, n - 1:n].to_broadcast([P, (c1 - c0) // n, n]), v, ALU.subtract)
                        ins.then_inc(s["kt_d"], 1)
                    keep_level(l - 1)
                keep_level(len(LEVELS) - 1)
                dve.wait_ge(s["kt_e"], h + 1)
                dve.tensor_tensor(kt[:, 0:NTOK], kt[:, 0:NTOK], kb[:, 0:NTOK], ALU.mult).then_inc(s["kt_ok"], 1)
                full("smp")
                order("smp")
                for l, m in enumerate(SLEVELS):
                    mask = lmask[0:STOK, LEVELS.index(m) - PACKED, 0:32].bitcast(U32).rearrange("p (q m) -> p q m", m=m)
                    dve.copy_predicated(half(att[0:STOK, NCHUNK, 0:STOK], m, 1), mask,
                                        ps[0:STOK, bank("smp"), 32 * l:32 * l + 32].rearrange("p (q m) -> p q m", m=m)).then_inc(s["att_step"], 1)
                    dve.wait_ge(s["att_step"], 3 * h + (l + 1))
                    dve.sem_inc(s["dve_passed"], 1)
                dve.copy_predicated(att[0:STOK, NCHUNK, 0:STOK], ident[0:STOK, 0:STOK].bitcast(U32),
                                    ps[0:STOK, bank("smp"), 128:128 + STOK]).then_inc(s["c_dve"], 1)
                dve.wait_ge(s["qb_e"], h + 1)
                dve.tensor_tensor(qb[:, :], qb[:, :], dd[:, :], ALU.mult).then_inc(s["qb_ok"], 1)
                dve.wait_ge(s["zg_tanh"], 2 * h + 1)
                dve.scalar_tensor_tensor(p3(keep[:, 2 * h, :]), p3(vT[:, :]), 1.0, slot3(bankA), ALU.add, ALU.mult).then_inc(s["zg_silu"], 1)
                dve.wait_ge(s["dlast_ok"], h + 1)
                dve.wait_ge(s["st_out"], 16 * h + ONE)
                for n in range(NCHUNK // 2):
                    full(f"KV{n}")
                    b = bank(f"KV{n}")
                    if n == 0:
                        ins = dve.tensor_copy(st[:, 0, :], ps[:, b, 0:DV])
                    else:
                        dve.wait_ge(*emptied(h, f"KV{n - 1}"))
                        ins = dve.scalar_tensor_tensor(st[:, 2 * n, :], st[:, 2 * n - 1, :], dlast[:, 2 * n:2 * n + 1], ps[:, b, 0:DV],
                                                       ALU.mult, ALU.add)
                    ins.then_inc(s["st_ok"], 1)
                    dve.wait_ge(s["st_ok"], (NCHUNK // 2) * h + (n + 1))
                    dve.scalar_tensor_tensor(st[:, 2 * n + 1, :], st[:, 2 * n, :], dlast[:, 2 * n + 1:2 * n + 2], ps[:, b, DV:2 * DV],
                                             ALU.mult, ALU.add).then_inc(s["c_dve"], 1)
                dve.wait_ge(s["smp_hi"], h + 1)
                dve.tensor_tensor(skey[STOK:P, :], kT[0:STOK, NCHUNK, :], skey[0:STOK, :].bitcast(F32), ALU.subtract)
                dve.tensor_tensor(svlo[:, :], vv[0:STOK, NCHUNK, :], svhi[0:STOK, :].bitcast(F32), ALU.subtract).then_inc(s["smp_lo"], 1)
                dve.wait_ge(s["smp_lo"], h + 1)
                dve.tensor_tensor(skeys[:, :, :], skey[:, :].bitcast(F32).rearrange("p (o n) -> p o n", o=1).to_broadcast([P, NSEQ, P]),
                                  smask[:, :].rearrange("p (q o) -> p q o", o=1).to_broadcast([P, NSEQ, P]), ALU.mult).then_inc(s["ktm_ok"], 1)

                def add_squares(m):
                    cols = (slice(0, SEQ), slice(SEQ, TOK))[m]
                    dve.wait_ge(s["o_sq"], 4 * h + (2 * m + 2))
                    dve.tensor_tensor(qk[:, 0, cols], qk[:, 0, cols], qk[:, 1, cols], ALU.add).then_inc(s["sq_sum"], 1)

                add_squares(0)
                for n in range(NSEQ // 2):
                    if n == 2:
                        add_squares(1)
                    full(f"sKV{n}")
                    for c in range(2):
                        q = 2 * n + c
                        ins = dve.scalar_tensor_tensor(st0[:, q, :], st0[:, q, :], dlast[:, NCHUNK + q:NCHUNK + q + 1],
                                                       ps[:, bank(f"sKV{n}"), c * DV:(c + 1) * DV], ALU.mult, ALU.add)
                    ins.then_inc(s["c_dve"], 1)
                dve.wait_ge(s["zg_tanh"], 2 * h + 2)
                dve.scalar_tensor_tensor(p3(keep[:, 2 * h + 1, :]), p3(vT[:, :]), 1.0, slot3(bankB), ALU.add, ALU.mult).then_inc(s["zg_silu"], 1)
                dve.wait_ge(s["n_rstd"], h + 1)
                for d in range(VH):
                    dve.scalar_tensor_tensor(oo[d][:, :], oo[d][:, :], vec[:, 2 * h + d, R_GN:R_GN + 1], kt[:, :], ALU.mult, ALU.mult).then_inc(s["o_norm"], 1)
                dve.wait_ge(s["zg_silu"], 2 * h + (ONE + 2))
                for d in range(VH):
                    dve.wait_ge(s["o_norm"], 2 * h + (d + 1))
                    dve.tensor_tensor(keep[:, 2 * h + d, :], keep[:, 2 * h + d, :], oo[d][:, :], ALU.mult).then_inc(s["og_ok"], 1)

            split_operand(KT)
            dve.wait_ge(gb_tanh[0], KT // 2 + ONE)
            dve.wait_ge(gb_tanh[1], KT // 2 + ONE)

            def merge(i, j):
                b = (bankA, bankB)[j]
                dve.wait_ge(s["wo_hi"], 2 * i + (j + 1))
                dve.tensor_tensor(wos[:, 1, 2 * i + j, :], woraw[:, :], wos[:, 0, 2 * i + j, :].bitcast(F32), ALU.subtract).then_inc(s["wo_lo"], 1)
                tile = keep[:, 2 * i + j, :]
                dve.wait_ge(s["job_done"], 2 * i + (N_YB + j + 1))
                dve.scalar_tensor_tensor(p3(tile), p3(tile), 1.0, slot3(b), ALU.add, ALU.mult).then_inc(s["yb_part"], 1)
                dve.wait_ge(s["yb_part"], 2 * i + (j + 1))
                dve.wait_ge(mal_in[j], 16 * (i + 1))
                dve.tensor_tensor(tile[:, 0:NTOK], tile[:, 0:NTOK], mal[:, j, :], ALU.add).then_inc(merged[j], 1)

            def first_lo(m):
                ks = (slice(0, KT - 1), slice(KT - 1, KT))[m]
                dve.wait_ge(s["m_hi"], m + 1)
                dve.tensor_tensor(ms[1][:, 0, ks, :], keep[:, ks, 0:P], ms[0][:, 0, ks, :].bitcast(F32), ALU.subtract).then_inc(s["m_lo"], 1)

            with dve.Fori(0, KT // 2 - 1) as i:
                merge(i, 0)
                merge(i, 1)
            merge(KT // 2 - 1, 0)
            first_lo(0)
            merge(KT // 2 - 1, 1)
            first_lo(1)

            def merged_lo(n):
                nr = x_rows[n][2]
                dve.wait_ge(s["m_hi"], n + 2)
                dve.tensor_tensor(ms[1][:, n % 2, :, 0:nr], keep[:, :, n * P:n * P + nr], ms[0][:, n % 2, :, 0:nr].bitcast(F32),
                                  ALU.subtract).then_inc(s["m_lo"], 1)

            for n in range(TTILES):
                nr = x_rows[n][2]
                b = (bankA, bankB)[n % 2]
                y = yy[0:nr, n % 2, :]
                if n + 1 < TTILES:
                    merged_lo(n + 1)
                if n == 0:
                    dve.wait_ge(s["fng_in"], 16)
                if n >= 2:
                    dve.wait_ge(y_out[n % 2], 16 * (n // 2))
                dve.wait_ge(s["y_mm"], n + 1)
                dve.wait_ge(s_xr[n % 2], 16 * (n // 2 + 1))
                dve.scalar_tensor_tensor(y.rearrange("p (a b) -> p a b", a=2), ps[0:nr, b:b + 2, :], 0.25,
                                         xr[0:nr, n % 2, :].rearrange("p (a b) -> p a b", a=2), ALU.mult, ALU.add).then_inc(s["y_res"], 1)
                dve.wait_ge(s["y_rms"], n + 1)
                r = rstd[0:nr, 16 + n:17 + n]
                dve.reciprocal(r, r).then_inc(s["y_rstd"], 1)
                dve.wait_ge(s["y_rstd"], n + 1)
                dve.scalar_tensor_tensor(y, y, r, fng[0:nr, :], ALU.mult, ALU.mult).then_inc(s["y_ok"], 1)


INPUTS = ["x_prompt", "x_sample", "state_lru_h", "state_lru_conv", "state_gla", "norm_g", "w_in", "conv_w", "conv_b",
          "w_r", "b_r", "w_i", "b_i", "lam", "w_a2", "b_a", "gla_norm_g", "w_lru_o", "w_gla_o", "b_merge", "w_out",
          "final_norm_g"]
OUTPUTS = [(1, SEQ, D), (NSEQ, SLEN, D), (1, 1, D), (1, 1, HIST, D), (1, 1, HEADS, DK, DV),
           (1, NSEQ, D), (1, NSEQ, HIST, D), (1, NSEQ, HEADS, DK, DV)]


def kernel(**inputs):
    import numpy as np
    import concourse.bacc as bacc
    from concourse.bass_utils import run_bass_kernel_spmd

    nc = bacc.Bacc("TRN2", target_bir_lowering=False, num_devices=1)
    arrays, t = {}, {}
    for name in INPUTS:
        a = np.ascontiguousarray(inputs[name])
        arrays["in_" + name] = a
        t[name] = nc.dram_tensor("in_" + name, a.shape, mybir.dt.from_np(a.dtype), kind="ExternalInput").ap()
    out = [nc.dram_tensor(f"out_{n}", shape, F32, kind="ExternalOutput").ap() for n, shape in enumerate(OUTPUTS)]
    build(nc, t, out)
    r = run_bass_kernel_spmd(nc, [arrays], core_ids=[0])
    return tuple(r.results[0][f"out_{n}"] for n in range(len(OUTPUTS)))
```
